# Optimizing a Trainium2 kernel written in Bass

```python
import jax, jax.numpy as jnp
from jax import lax
import numpy as np

D_MODEL = 1024
BATCH = 1
SEQ = 1024
DEPTH = 1
DEC_BATCH = 1
DEC_SEQ = 32
PAST_LEN = 256

CHUNK = 64
N_HEADS_ATT = 16
HEAD_DIM = 64
ATT_WIDTH = N_HEADS_ATT * HEAD_DIM
ATT_SCALE = HEAD_DIM ** -0.5
Q_BLOCK = 128
SSM_EXPAND = 2
D_INNER = SSM_EXPAND * D_MODEL
SSM_HEAD_DIM = 64
N_HEADS_SSM = D_INNER // SSM_HEAD_DIM
N_GROUPS = 8
D_STATE = 128
CONV_W = 4
CONV_DIM = D_INNER + 2 * N_GROUPS * D_STATE
D_FF = 4 * D_MODEL
D_PROJ = 3 * ATT_WIDTH + N_HEADS_ATT + D_INNER + CONV_DIM + N_HEADS_SSM + 2 * D_MODEL
EPS = 1e-6

kernel_name = 'fox_ssd_hybrid_stream_step'

def _rmsnorm(x, w):
    xf = x.astype(jnp.float32)
    y = xf * lax.rsqrt(jnp.mean(xf * xf, axis=-1, keepdims=True) + EPS)
    return (y * w.astype(jnp.float32)).astype(x.dtype)

def _split_proj(proj):
    sizes = (ATT_WIDTH, ATT_WIDTH, ATT_WIDTH, N_HEADS_ATT, D_INNER, CONV_DIM, N_HEADS_SSM, D_MODEL, D_MODEL)
    parts = []
    start = 0
    for s in sizes:
        parts.append(proj[..., start:start + s])
        start += s
    return parts

def _fox_attend(q, cq, qpos, k, v, ck, kpos):
    s = jnp.einsum('bqhd,bkhd->bhqk', q, k, preferred_element_type=jnp.float32) * ATT_SCALE
    bias = jnp.swapaxes(cq, 1, 2)[:, :, :, None] - jnp.swapaxes(ck, 1, 2)[:, :, None, :]
    mask = kpos[None, :] <= qpos[:, None]
    s = jnp.where(mask, s + bias, -jnp.inf)
    p = jax.nn.softmax(s, axis=-1)
    return jnp.einsum('bhqk,bkhd->bqhd', p.astype(v.dtype), v)

def _fox_prompt(q, k, v, logf):
    b, T, H, d = q.shape
    c = jnp.cumsum(logf, axis=1)
    pos = jnp.arange(T)
    nb = T // Q_BLOCK
    qs = q.reshape(b, nb, Q_BLOCK, H, d).swapaxes(0, 1)
    cs = c.reshape(b, nb, Q_BLOCK, H).swapaxes(0, 1)
    ps = pos.reshape(nb, Q_BLOCK)

    def blk(args):
        qb, cb, pb = args
        return _fox_attend(qb, cb, pb, k, v, c, pos)

    o = lax.map(blk, (qs, cs, ps))
    return o.swapaxes(0, 1).reshape(b, T, H, d)

def _causal_conv(xbc, conv_past, conv_w, conv_b):
    T = xbc.shape[1]
    xin = jnp.concatenate([conv_past.astype(xbc.dtype), xbc], axis=1)
    out = conv_b
    for i in range(CONV_W):
        out = out + xin[:, i:i + T] * conv_w[i]
    return jax.nn.silu(out), xin[:, T:]

def _ssd(x, dt, A, Bm, Cm, h0):
    b, T, H, P = x.shape
    G, N = Bm.shape[2], Bm.shape[3]
    R = H // G
    L = min(CHUNK, T)
    nc = T // L
    f32 = jnp.float32
    xc = x.astype(f32).reshape(b, nc, L, G, R, P)
    dtc = dt.astype(f32).reshape(b, nc, L, G, R)
    Bc = Bm.astype(f32).reshape(b, nc, L, G, N)
    Cc = Cm.astype(f32).reshape(b, nc, L, G, N)
    acum = jnp.cumsum(dtc * A.astype(f32).reshape(G, R), axis=2)
    tri = jnp.tril(jnp.ones((L, L), dtype=bool))[:, :, None, None]
    seg = acum[:, :, :, None] - acum[:, :, None, :]
    decay = jnp.exp(jnp.where(tri, seg, -jnp.inf))
    cb = jnp.einsum('bclgn,bcsgn->bclsg', Cc, Bc)
    m = cb[..., None] * decay * dtc[:, :, None]
    y_diag = jnp.einsum('bclsgr,bcsgrp->bclgrp', m, xc)
    w_state = jnp.exp(acum[:, :, -1:] - acum) * dtc
    states = jnp.einsum('bclgn,bclgrp->bcgrpn', Bc, xc * w_state[..., None])
    chunk_decay = jnp.exp(acum[:, :, -1])

    def step(h, inp):
        dec, st = inp
        return h * dec[..., None, None] + st, h

    h_last, h_prev = lax.scan(step, h0.astype(f32).reshape(b, G, R, P, N),
                              (jnp.moveaxis(chunk_decay, 1, 0), jnp.moveaxis(states, 1, 0)))
    h_prev = jnp.moveaxis(h_prev, 0, 1)
    y_off = jnp.einsum('bclgn,bcgrpn->bclgrp', Cc, h_prev) * jnp.exp(acum)[..., None]
    y = (y_diag + y_off).reshape(b, T, H, P)
    return y, h_last.reshape(b, H, P, N)

def _layer(x, past, params):
    (norm1_w, w_in, b_f, q_norm_w, k_norm_w, conv_w, conv_b, dt_bias, A_log, D_skip,
     ssm_norm_w, w_pa, w_pb, w_out, norm2_w, w_up, w_down) = params
    f32 = jnp.float32
    b, T, _ = x.shape
    xn = _rmsnorm(x, norm1_w)
    proj = xn @ w_in
    q, k, v, f_raw, z, xbc, dt_raw, g_att, g_ssm = _split_proj(proj)
    q = _rmsnorm(q.reshape(b, T, N_HEADS_ATT, HEAD_DIM), q_norm_w)
    k = _rmsnorm(k.reshape(b, T, N_HEADS_ATT, HEAD_DIM), k_norm_w)
    v = v.reshape(b, T, N_HEADS_ATT, HEAD_DIM)
    logf = jax.nn.log_sigmoid(f_raw.astype(f32) + b_f.astype(f32))
    if past is None:
        att = _fox_prompt(q, k, v, logf)
        conv_past = jnp.zeros((b, CONV_W - 1, CONV_DIM), x.dtype)
        h0 = jnp.zeros((b, N_HEADS_SSM, SSM_HEAD_DIM, D_STATE), f32)
    else:
        k_past, v_past, logf_past, conv_past, h0 = past
        n_past = k_past.shape[1]
        k_all = jnp.concatenate([k_past.astype(k.dtype), k], axis=1)
        v_all = jnp.concatenate([v_past.astype(v.dtype), v], axis=1)
        c_all = jnp.cumsum(jnp.concatenate([logf_past.astype(f32), logf], axis=1), axis=1)
        att = _fox_attend(q, c_all[:, n_past:], n_past + jnp.arange(T), k_all, v_all, c_all,
                          jnp.arange(n_past + T))
    xbc_c, conv_new = _causal_conv(xbc, conv_past, conv_w, conv_b)
    xs = xbc_c[..., :D_INNER]
    Bm = xbc_c[..., D_INNER:D_INNER + N_GROUPS * D_STATE].reshape(b, T, N_GROUPS, D_STATE)
    Cm = xbc_c[..., D_INNER + N_GROUPS * D_STATE:].reshape(b, T, N_GROUPS, D_STATE)
    dt = jax.nn.softplus(dt_raw.astype(f32) + dt_bias.astype(f32))
    A = -jnp.exp(A_log.astype(f32))
    xh = xs.reshape(b, T, N_HEADS_SSM, SSM_HEAD_DIM)
    y, h_new = _ssd(xh, dt, A, Bm, Cm, h0)
    y = y + xh.astype(f32) * D_skip.astype(f32)[:, None]
    y = y.reshape(b, T, D_INNER) * jax.nn.silu(z.astype(f32))
    yg = y.reshape(b, T, N_GROUPS, D_INNER // N_GROUPS)
    yg = yg * lax.rsqrt(jnp.mean(yg * yg, axis=-1, keepdims=True) + EPS)
    y_ssm = (yg.reshape(b, T, D_INNER) * ssm_norm_w.astype(f32)).astype(x.dtype)
    merged = (jax.nn.sigmoid(g_att) * (att.reshape(b, T, ATT_WIDTH) @ w_pa)
              + jax.nn.sigmoid(g_ssm) * (y_ssm @ w_pb))
    x = x + merged @ w_out
    h = _rmsnorm(x, norm2_w)
    x = x + jnp.square(jax.nn.relu(h @ w_up)) @ w_down
    new_state = (k, v, logf.astype(x.dtype), conv_new, h_new.astype(x.dtype))
    return x, new_state

def _stack(states, i):
    return jnp.stack([s[i] for s in states], axis=0)

def setup_inputs(seed: int = 0) -> dict:
    key = jax.random.key(seed)
    ks = jax.random.split(key, 32)
    f32 = jnp.float32

    def nrm(k, shape, scale):
        return jax.random.normal(k, shape, f32) * scale

    dt0 = jnp.exp(jax.random.uniform(ks[16], (DEPTH, N_HEADS_SSM), f32, np.log(1e-3), np.log(1e-1)))
    return {
        'x_prompt': nrm(ks[0], (BATCH, SEQ, D_MODEL), 1.0),
        'x_sample': nrm(ks[1], (DEC_BATCH, DEC_SEQ, D_MODEL), 1.0),
        'cache_k': nrm(ks[2], (DEPTH, DEC_BATCH, PAST_LEN, N_HEADS_ATT, HEAD_DIM), 1.0),
        'cache_v': nrm(ks[3], (DEPTH, DEC_BATCH, PAST_LEN, N_HEADS_ATT, HEAD_DIM), 1.0),
        'cache_logf': jax.nn.log_sigmoid(3.0 + nrm(ks[4], (DEPTH, DEC_BATCH, PAST_LEN, N_HEADS_ATT), 0.5)),
        'state_conv': nrm(ks[5], (DEPTH, DEC_BATCH, CONV_W - 1, CONV_DIM), 1.0),
        'state_ssm': nrm(ks[6], (DEPTH, DEC_BATCH, N_HEADS_SSM, SSM_HEAD_DIM, D_STATE), 0.1),
        'norm1_w': 1.0 + nrm(ks[7], (DEPTH, D_MODEL), 0.02),
        'w_in': nrm(ks[8], (DEPTH, D_MODEL, D_PROJ), D_MODEL ** -0.5),
        'b_f': 3.0 + nrm(ks[9], (DEPTH, N_HEADS_ATT), 0.3),
        'q_norm_w': 1.0 + nrm(ks[10], (DEPTH, HEAD_DIM), 0.02),
        'k_norm_w': 1.0 + nrm(ks[11], (DEPTH, HEAD_DIM), 0.02),
        'conv_w': nrm(ks[12], (DEPTH, CONV_W, CONV_DIM), 0.5),
        'conv_b': nrm(ks[13], (DEPTH, CONV_DIM), 0.02),
        'dt_bias': dt0 + jnp.log(-jnp.expm1(-dt0)),
        'A_log': jnp.log(jax.random.uniform(ks[14], (DEPTH, N_HEADS_SSM), f32, 1.0, 16.0)),
        'D_skip': 1.0 + nrm(ks[15], (DEPTH, N_HEADS_SSM), 0.1),
        'ssm_norm_w': 1.0 + nrm(ks[17], (DEPTH, D_INNER), 0.02),
        'w_pa': nrm(ks[18], (DEPTH, ATT_WIDTH, D_MODEL), ATT_WIDTH ** -0.5),
        'w_pb': nrm(ks[19], (DEPTH, D_INNER, D_MODEL), D_INNER ** -0.5),
        'w_out': nrm(ks[20], (DEPTH, D_MODEL, D_MODEL), D_MODEL ** -0.5),
        'norm2_w': 1.0 + nrm(ks[21], (DEPTH, D_MODEL), 0.02),
        'w_up': nrm(ks[22], (DEPTH, D_MODEL, D_FF), D_MODEL ** -0.5),
        'w_down': nrm(ks[23], (DEPTH, D_FF, D_MODEL), D_FF ** -0.5),
    }

def reference(x_prompt, x_sample, cache_k, cache_v, cache_logf, state_conv, state_ssm,
              norm1_w, w_in, b_f, q_norm_w, k_norm_w, conv_w, conv_b, dt_bias, A_log, D_skip,
              ssm_norm_w, w_pa, w_pb, w_out, norm2_w, w_up, w_down):
    yp = x_prompt
    ys = x_sample
    states_p = []
    states_s = []
    for l in range(DEPTH):
        params = (norm1_w[l], w_in[l], b_f[l], q_norm_w[l], k_norm_w[l], conv_w[l], conv_b[l],
                  dt_bias[l], A_log[l], D_skip[l], ssm_norm_w[l], w_pa[l], w_pb[l], w_out[l],
                  norm2_w[l], w_up[l], w_down[l])
        yp, st_p = _layer(yp, None, params)
        ys, st_s = _layer(ys, (cache_k[l], cache_v[l], cache_logf[l], state_conv[l], state_ssm[l]), params)
        states_p.append(st_p)
        states_s.append(st_s)
    k_prompt = _stack(states_p, 0)
    v_prompt = _stack(states_p, 1)
    logf_prompt = _stack(states_p, 2)
    conv_prompt = _stack(states_p, 3)
    ssm_prompt = _stack(states_p, 4)
    k_sample = _stack(states_s, 0)
    v_sample = _stack(states_s, 1)
    logf_sample = _stack(states_s, 2)
    conv_sample = _stack(states_s, 3)
    ssm_sample = _stack(states_s, 4)
    return (yp, ys, k_prompt, v_prompt, logf_prompt, conv_prompt, ssm_prompt,
            k_sample, v_sample, logf_sample, conv_sample, ssm_sample)


_drawn_inputs = setup_inputs


def setup_inputs(seed=0):
    import zlib

    import numpy as np

    out = dict(_drawn_inputs(seed))
    spreads = {}
    factors = {'cache_logf': 64.0,
     'q_norm_w': 25.447,
     'k_norm_w': 7.646,
     'ssm_norm_w': 5.325,
     'norm2_w': 3.241}
    for name, (base, spread) in spreads.items():
        noise = np.random.default_rng([zlib.crc32(name.encode()), seed]).standard_normal(out[name].shape)
        drawn = base * np.exp(spread * noise) if base else spread * noise
        out[name] = __import__('jax').numpy.asarray(drawn.astype(out[name].dtype))
    for name, factor in factors.items():
        out[name] = (out[name] * factor).astype(out[name].dtype)
    return out
```

```python
from contextlib import ExitStack

import numpy as np
import concourse.bass as bass
from concourse import mybir

F32 = mybir.dt.float32
F32R = mybir.dt.float32r
BF16 = mybir.dt.bfloat16
ALU = mybir.AluOpType
ACT = mybir.ActivationFunctionType
AX = mybir.AxisListType

P = 128
D = 1024
KB = D // P
TP = 1024
TS = 32
PAST = 256
T = TP + TS
NT = TP // P
TW = (NT + 1) * P
TT = T // 3
H = 16
HD = 64
DI = 2048
HS = 32
G = 8
N = 128
GH = HS // G
GW = DI // G
CW = 4
CD = DI + 2 * G * N
FF = 4 * D
FS = 512
EPS = 1e-6
NEG = -1e30
C_Q, C_K, C_V, C_F = 0, D, 2 * D, 3 * D
C_Z = C_F + H
C_X = C_Z + DI
C_B = C_X + DI
C_C = C_B + G * N
C_DT = C_X + CD
C_GA = C_DT + HS
DPROJ = C_GA + 2 * D
PW = 256


class Chain:

    def __init__(self, eng, sem):
        self.eng, self.sem, self.base, self.n = eng, sem, 0, 0

    def __call__(self, ins):
        ins.then_inc(self.sem, 1)
        self.n += 1
        self.eng.wait_ge(self.sem, self.base + self.n)

    def enter(self, i, per):
        self.base, self.n, self.per = i * per, 0, per

    def leave(self):
        assert self.n == self.per, (self.n, self.per)


class Core:

    def __init__(self, nc, ctx):
        self.nc, self.ctx = nc, ctx
        self.banks = ctx.enter_context(nc.psum_tensor("banks", [P, 8, 512], F32))
        self.ident = ctx.enter_context(nc.sbuf_tensor("ident", [P, P], F32))
        self.identb = ctx.enter_context(nc.sbuf_tensor("identb", [P, P], BF16))
        self.maskb = ctx.enter_context(nc.sbuf_tensor("maskb", [P, P], BF16))
        self.maskT = ctx.enter_context(nc.sbuf_tensor("maskT", [P, P], F32))
        self.passed = ctx.enter_context(nc.semaphore("passed"))

    def semaphores(self, ctx, tag):
        held = []

        def clear():
            self.nc.clear_and_free_semaphores(held)
            self.nc.all_engine_barrier()
        ctx.callback(clear)

        def new(name):
            held.append(self.nc.alloc_semaphore(f"{tag}_{name}"))
            return held[-1]
        return new

    def hold(self, eng, sem, value):
        eng.wait_ge(sem, value)
        eng.sem_inc(self.passed, 1)


def loop(eng, count, body):
    if count > 1:
        with eng.Fori(0, count - 1) as i:
            body(i, False)
    body(count - 1, True)


def constants(core):
    nc = core.nc
    with ExitStack() as ctx:
        made = core.semaphores(ctx, "const")("made")
        block = ctx.enter_context(nc.Block())

        @block.gpsimd
        def _(pool):
            nc.gpsimd.memset(core.ident[:], 0.0).then_inc(made, 1)
            nc.gpsimd.memset(core.maskT[:], 0.0).then_inc(made, 1)
            nc.gpsimd.memset(core.maskb[:], 0.0).then_inc(made, 1)
            pool.wait_ge(made, 3)
            nc.gpsimd.affine_select(out=core.ident[:], in_=core.ident[:], compare_op=ALU.not_equal, fill=1.0,
                                    base=0, pattern=[[-1, P]], channel_multiplier=1).then_inc(made, 1)
            nc.gpsimd.affine_select(out=core.maskT[:], in_=core.maskT[:], compare_op=ALU.is_ge, fill=NEG,
                                    base=0, pattern=[[1, P]], channel_multiplier=-1).then_inc(made, 1)
            nc.gpsimd.affine_select(out=core.maskb[:], in_=core.maskb[:], compare_op=ALU.is_ge, fill=NEG,
                                    base=0, pattern=[[-1, P]], channel_multiplier=1).then_inc(made, 1)
            pool.wait_ge(made, 6)
            nc.gpsimd.tensor_copy(core.identb[:], core.ident[:]).then_inc(made, 1)


def transpose_split(core, tag, srcs, hi, lo, norm_w=None):
    nc = core.nc
    with ExitStack() as ctx:
        sb = lambda n, s, dt=F32: ctx.enter_context(nc.sbuf_tensor(f"{tag}_{n}", s, dt))
        sem = core.semaphores(ctx, f"{tag}")
        rows = sb("rows", [P, NT + 1, D])
        junk = sb("junk", [P, D])
        ss = sb("ss", [P, NT + 1])
        wb = sb("wb", [P, D])
        loaded = [sem(f"loaded{t}") for t in range(NT + 1)]
        w_loaded, summed, rooted, scaled = sem("w_loaded"), sem("summed"), sem("rooted"), sem("scaled")
        turned, hi_made, lo_made, chain, zeroed = sem("turned"), sem("hi_made"), sem("lo_made"), sem("chain"), sem("zeroed")
        cleared = sem("cleared")
        block = ctx.enter_context(nc.Block())
        width = hi.shape[2]

        @block.sync
        def _(sp):
            for t in range(NT):
                sp.dma_start(rows[:, t, :], srcs[0][t * P:(t + 1) * P, :]).then_inc(loaded[t], 16)
            sp.dma_start(rows[0:TS, NT, :], srcs[1]).then_inc(loaded[NT], 16)
            if norm_w is not None:
                sp.dma_start(wb[:], norm_w.to_broadcast([P, D])).then_inc(w_loaded, 16)

        @block.scalar
        def _(act):
            if norm_w is not None:
                for t in range(NT + 1):
                    n = P if t < NT else TS
                    act.wait_ge(loaded[t], 16)
                    if t == 0:
                        act.wait_ge(zeroed, 1)
                    if t:
                        act.wait_ge(summed, t)
                    nc.scalar.activation(junk[0:n, :], rows[0:n, t, :], ACT.Square,
                                         accum_out=ss[0:n, t:t + 1]).then_inc(summed, 1)
                act.wait_ge(chain, 1)
                nc.scalar.activation(ss[:], ss[:], ACT.Sqrt).then_inc(rooted, 1)
            if width > T:
                act.wait_ge(zeroed, 2 if norm_w is not None else 1)
            for t in range(NT + 1):
                n = P if t < NT else TS
                for half in range(2):
                    act.wait_ge(turned, 2 * t + half + 1)
                    b = (2 * t + half) % 4
                    bank = core.banks[:, b, 0:4 * n].rearrange("p (k n) -> p k n", k=4)
                    nc.scalar.activation(hi[:, 4 * half:4 * half + 4, t * P:t * P + n], bank, ACT.Copy).then_inc(hi_made, 1)

        @block.vector
        def _(dve):
            step = Chain(dve, chain)
            if norm_w is not None:
                nc.vector.memset(ss[:], 1.0).then_inc(zeroed, 1)
                dve.wait_ge(summed, NT + 1)
                step(nc.vector.tensor_scalar(ss[:], ss[:], 1.0 / D, EPS, ALU.mult, ALU.add))
                dve.wait_ge(rooted, 1)
                step(nc.vector.reciprocal(ss[:], ss[:]))
                dve.wait_ge(w_loaded, 16)
                for t in range(NT + 1):
                    n = P if t < NT else TS
                    nc.vector.scalar_tensor_tensor(out=rows[0:n, t, :], in0=rows[0:n, t, :], scalar=ss[0:n, t:t + 1],
                                                   in1=wb[0:n, :], op0=ALU.mult, op1=ALU.mult).then_inc(scaled, 1)
            if width > T:
                nc.vector.memset(hi[:, :, T:width].bitcast(F32), 0.0).then_inc(cleared, 1)
                nc.vector.memset(lo[:, :, T:width].bitcast(F32), 0.0).then_inc(zeroed, 1)
            for t in range(NT + 1):
                n = P if t < NT else TS
                for half in range(2):
                    dve.wait_ge(hi_made, 2 * t + half + 1)
                    b = (2 * t + half) % 4
                    bank = core.banks[:, b, 0:4 * n].rearrange("p (k n) -> p k n", k=4)
                    nc.vector.tensor_tensor(lo[:, 4 * half:4 * half + 4, t * P:t * P + n], bank,
                                            hi[:, 4 * half:4 * half + 4, t * P:t * P + n].bitcast(F32),
                                            ALU.subtract).then_inc(lo_made, 1)

        @block.tensor
        def _(pe):
            for t in range(NT + 1):
                n = P if t < NT else TS
                if norm_w is not None:
                    pe.wait_ge(scaled, t + 1)
                else:
                    pe.wait_ge(loaded[t], 16)
                for half in range(2):
                    i = 2 * t + half
                    if i >= 4:
                        pe.wait_ge(lo_made, i - 3)
                    for k in range(4):
                        kb = 4 * half + k
                        last = nc.tensor.transpose(core.banks[:, i % 4, k * n:(k + 1) * n],
                                                   rows[0:n, t, kb * P:(kb + 1) * P], core.ident[0:n, 0:n])
                    last.then_inc(turned, 1)


def gemm(core, tag, hi, lo, weights, pairs, kb, cols, tm, make):
    nc = core.nc
    with ExitStack() as ctx:
        sb = lambda n, s, dt=F32: ctx.enter_context(nc.sbuf_tensor(f"{tag}_{n}", s, dt))
        sem = core.semaphores(ctx, f"{tag}")
        raw = [sb(f"raw{b}", [P, kb, cols]) for b in range(2)]
        whi = [sb(f"whi{b}", [P, kb, cols], F32R) for b in range(2)]
        wlo = [sb(f"wlo{b}", [P, kb, cols], F32R) for b in range(2)]
        raw_loaded = [sem(f"raw_loaded{b}") for b in range(2)]
        hi_made = [sem(f"whi_made{b}") for b in range(2)]
        lo_made = [sem(f"wlo_made{b}") for b in range(2)]
        full, free = sem("bank_full"), sem("bank_free")
        tiles = NT + 1 if tm else 3 * (cols // P)
        nb = 6
        assert 2 * tiles % nb == 0
        ep = make(ctx, sb, sem, full, free, tiles, nb)
        block = ctx.enter_context(nc.Block())

        @block.sync
        def _(sp):
            def load(i, b, fresh):
                if not fresh:
                    sp.wait_ge(lo_made[b], i)
                sp.dma_start(raw[b][:], weights(2 * i + b).rearrange("(k p) m -> p k m", p=P)).then_inc(raw_loaded[b], 16)
            ep.start_sp(sp)
            load(0, 0, True)
            load(0, 1, True)

            def body(i, last):
                for b in range(2):
                    if not last:
                        load(i + 1, b, False)
                    ep.store(sp, i, b)
            loop(sp, pairs, body)
            ep.finish(sp, pairs)

        @block.scalar
        def _(act):
            def split(i, b, fresh):
                act.wait_ge(raw_loaded[b], 16 * (i + 1))
                if not fresh:
                    act.wait_ge(full, ((i - 1) * 2 + b + 1) * tiles)
                nc.scalar.activation(whi[b][:], raw[b][:], ACT.Copy).then_inc(hi_made[b], 1)
            ep.start_act(act)
            split(0, 0, True)
            split(0, 1, True)

            def body(i, last):
                for b in range(2):
                    ep.act(act, i, b)
                    if not last:
                        split(i + 1, b, False)
            loop(act, pairs, body)

        @block.vector
        def _(dve):
            def split(i, b):
                dve.wait_ge(hi_made[b], i + 1)
                nc.vector.tensor_tensor(wlo[b][:], raw[b][:], whi[b][:].bitcast(F32), ALU.subtract).then_inc(lo_made[b], 1)
            ep.start_dve(dve)
            split(0, 0)
            split(0, 1)

            def body(i, last):
                for b in range(2):
                    ep.vec(dve, i, b)
                    if not last:
                        split(i + 1, b)
            loop(dve, pairs, body)

        @block.tensor
        def _(pe):
            def body(i, last):
                for b in range(2):
                    pe.wait_ge(lo_made[b], i + 1)
                    for t in range(tiles):
                        n = b * tiles + t
                        pe.wait_ge(free, i * 2 * tiles + n + 1)
                        passes = [(x, w, k) for k in range(kb) for x, w in ((hi, whi[b]), (hi, wlo[b]), (lo, whi[b]))]
                        for j, (x, w, k) in enumerate(passes):
                            first, end = j == 0, j == len(passes) - 1
                            if tm:
                                ins = nc.tensor.matmul(core.banks[:, n % nb, 0:cols], x[:, k, t * P:(t + 1) * P],
                                                       w[:, k, :], start=first, stop=end)
                            else:
                                m, r = t // 3, t % 3
                                ins = nc.tensor.matmul(core.banks[:, n % nb, 0:TT], w[:, k, m * P:(m + 1) * P],
                                                       x[:, k, r * TT:(r + 1) * TT], start=first, stop=end)
                        ins.then_inc(full, 1)
            loop(pe, pairs, body)


class Epilogue:
    STORES = 0

    def __init__(self, core, ctx, sb, sem, full, free, tiles, nb):
        self.core, self.nc, self.sb, self.full, self.free, self.tiles, self.nb = core, core.nc, sb, full, free, tiles, nb
        self.done = [sem(f"out_done{b}") for b in range(2)]
        self.stored = [sem(f"out_stored{b}") for b in range(2)]
        self.chain = sem("vec_chain")
        self.ready = sem("ready")
        self.mid = sem("mid")
        self.extra = [sem(f"extra{b}") for b in range(2)]
        self.setup(sem)

    def setup(self, sem):
        pass

    def bank(self, b, t, rows, cols):
        return self.core.banks[0:rows, (b * self.tiles + t) % self.nb, 0:cols]

    def wait_full(self, eng, i, b, t):
        eng.wait_ge(self.full, (2 * i + b) * self.tiles + t + 1)

    def start_sp(self, sp):
        if self.STORES:
            for b in range(2):
                sp.sem_inc(self.stored[b], 16 * self.STORES)

    def wait_stage(self, eng, i, b):
        eng.wait_ge(self.stored[b], 16 * self.STORES * (i + 1))

    def start_act(self, act):
        act.sem_inc(self.free, self.nb)

    def start_dve(self, dve):
        pass

    def act(self, act, i, b):
        pass

    def vec(self, dve, i, b):
        pass

    def store(self, sp, i, b):
        pass

    def finish(self, sp, pairs):
        if self.STORES:
            for b in range(2):
                self.wait_stage(sp, pairs, b)


def rows_of(t):
    return P if t < NT else TS


def pointwise_tm(core, func, to_prompt, to_running):
    class Pointwise(Epilogue):
        STORES = 2

        def setup(self, sem):
            self.stage = [self.sb(f"stage{b}", [P, NT + 1, PW]) for b in range(2)]

        def act(self, act, i, b):
            self.wait_stage(act, i, b)
            for t in range(self.tiles):
                n = rows_of(t)
                self.wait_full(act, i, b, t)
                self.nc.scalar.activation(self.stage[b][0:n, t, :], self.bank(b, t, n, PW), func).then_inc(self.free, 1)

        def store(self, sp, i, b):
            sp.wait_ge(self.free, self.nb + (2 * i + b + 1) * self.tiles)
            cols = bass.ds((2 * i + b) * PW, PW)
            sp.dma_start(to_prompt[:, cols].rearrange("(t p) d -> p t d", p=P), self.stage[b][:, 0:NT, :]).then_inc(self.stored[b], 16)
            sp.dma_start(to_running[:, cols], self.stage[b][0:TS, NT, :]).then_inc(self.stored[b], 16)
    return lambda *a: Pointwise(core, *a)


def head_norm_tm(core, weight, to_prompt, to_running):
    heads = PW // HD

    class HeadNorm(Epilogue):
        STORES = 2
        STEPS = 4

        def setup(self, sem):
            self.stage = [self.sb(f"stage{b}", [P, NT + 1, PW]) for b in range(2)]
            self.sq = [self.sb(f"sq{b}", [P, NT + 1, PW]) for b in range(2)]
            self.ss = [self.sb(f"ss{b}", [P, (NT + 1) * heads]) for b in range(2)]
            self.w = self.sb("w", [P, HD])
            self.w_loaded = sem("w_loaded")
            self.cleared = sem("cleared")
            self.squared = sem("squared")

        def start_sp(self, sp):
            Epilogue.start_sp(self, sp)
            sp.dma_start(self.w[:], weight.to_broadcast([P, HD])).then_inc(self.w_loaded, 16)

        def start_dve(self, dve):
            for b in range(2):
                self.nc.vector.memset(self.stage[b][:, NT, :], 0.0).then_inc(self.cleared, 1)
                self.nc.vector.memset(self.sq[b][:, NT, :], 0.0).then_inc(self.cleared, 1)

        def start_act(self, act):
            Epilogue.start_act(self, act)
            act.wait_ge(self.cleared, 4)

        def act(self, act, i, b):
            self.wait_stage(act, i, b)
            for t in range(self.tiles):
                n = rows_of(t)
                self.wait_full(act, i, b, t)
                self.nc.scalar.activation(self.stage[b][0:n, t, :], self.bank(b, t, n, PW), ACT.Copy).then_inc(self.squared, 1)
                self.nc.scalar.activation(self.sq[b][0:n, t, :], self.bank(b, t, n, PW), ACT.Square).then_inc(self.free, 1)
            act.wait_ge(self.mid, 2 * i + b + 1)
            self.nc.scalar.activation(self.ss[b][:], self.ss[b][:], ACT.Sqrt).then_inc(self.ready, 1)

        def vec(self, dve, i, b):
            q = 2 * i + b
            nc, step = self.nc, Chain(dve, self.chain)
            step.enter(q, self.STEPS)
            dve.wait_ge(self.free, self.nb + (q + 1) * self.tiles)
            dve.wait_ge(self.squared, (q + 1) * self.tiles)
            step(nc.vector.tensor_reduce(self.ss[b][:], self.sq[b][:].rearrange("p t (h d) -> p (t h) d", d=HD), AX.X, ALU.add))
            nc.vector.tensor_scalar(self.ss[b][:], self.ss[b][:], 1.0 / HD, EPS, ALU.mult, ALU.add).then_inc(self.mid, 1)
            dve.wait_ge(self.ready, q + 1)
            step(nc.vector.reciprocal(self.ss[b][:], self.ss[b][:]))
            stage = self.stage[b][:].rearrange("p t (h d) -> p (t h) d", d=HD)
            step(nc.vector.tensor_tensor(stage, stage, self.ss[b][:, :, None].to_broadcast([P, (NT + 1) * heads, HD]), ALU.mult))
            dve.wait_ge(self.w_loaded, 16)
            step(nc.vector.tensor_tensor(stage, stage, self.w[:, None, :].to_broadcast([P, (NT + 1) * heads, HD]), ALU.mult))
            step.leave()

        def store(self, sp, i, b):
            sp.wait_ge(self.chain, (2 * i + b + 1) * self.STEPS)
            cols = bass.ds((2 * i + b) * PW, PW)
            sp.dma_start(to_prompt[:, cols].rearrange("(t p) d -> p t d", p=P), self.stage[b][:, 0:NT, :]).then_inc(self.stored[b], 16)
            sp.dma_start(to_running[:, cols], self.stage[b][0:TS, NT, :]).then_inc(self.stored[b], 16)
    return lambda *a: HeadNorm(core, *a)


def sigmoid_fm(core, to):
    class Gate(Epilogue):
        STORES = 1

        def setup(self, sem):
            self.stage = [self.sb(f"stage{b}", [P, 2, T]) for b in range(2)]

        def act(self, act, i, b):
            self.wait_stage(act, i, b)
            for t in range(self.tiles):
                self.wait_full(act, i, b, t)
                self.nc.scalar.activation(self.stage[b][:, t // 3, (t % 3) * TT:(t % 3 + 1) * TT], self.bank(b, t, P, TT),
                                          ACT.Sigmoid).then_inc(self.free, 1)

        def store(self, sp, i, b):
            sp.wait_ge(self.free, self.nb + (2 * i + b + 1) * self.tiles)
            sp.dma_start(to[bass.ds((2 * i + b) * PW, PW), :].rearrange("(m p) t -> p m t", p=P),
                         self.stage[b][:]).then_inc(self.stored[b], 16)
    return lambda *a: Gate(core, *a)


def conv_fm(core, conv_w, conv_b, state, to, tail_prompt, tail_running):
    W = CW - 1 + TP + CW - 1 + TS
    RUN = CW - 1 + TP + CW - 1
    NB = CD // P

    class Conv(Epilogue):
        STORES = 1
        STEPS = 8

        def setup(self, sem):
            self.xs = [self.sb(f"xs{b}", [P, 2, W]) for b in range(2)]
            self.co = [self.sb(f"co{b}", [P, 2, W]) for b in range(2)]
            self.stage = [self.sb(f"stage{b}", [P, 2, T]) for b in range(2)]
            self.cw = self.sb("cw", [P, CW, NB])
            self.cb = self.sb("cb", [P, NB])
            self.hist = self.sb("hist", [P, CW - 1, NB])
            self.tails = self.sb("tails", [P, 2, CW - 1, NB])
            self.p_loaded, self.cleared, self.tailed = sem("p_loaded"), sem("cleared"), sem("tailed")
            self.silued, self.tails_out = sem("silued"), sem("tails_out")

        def start_sp(self, sp):
            Epilogue.start_sp(self, sp)
            with self.nc.allow_non_contiguous_dma(reason="parameters by channel"):
                for j in range(CW):
                    sp.dma_start(self.cw[:, j, :], conv_w[j, :].rearrange("(m p) -> p m", p=P)).then_inc(self.p_loaded, 16)
                sp.dma_start(self.cb[:], conv_b.rearrange("(m p) -> p m", p=P)).then_inc(self.p_loaded, 16)
                for j in range(CW - 1):
                    sp.dma_start(self.hist[:, j, :], state[j, :].rearrange("(m p) -> p m", p=P)).then_inc(self.p_loaded, 16)

        def start_dve(self, dve):
            for b in range(2):
                self.nc.vector.memset(self.xs[b][:, :, 0:CW - 1], 0.0).then_inc(self.cleared, 1)
            dve.sem_inc(self.chain, 2 * self.STEPS)
            dve.wait_ge(self.p_loaded, 16 * 2 * CW)
            dve.wait_ge(self.cleared, 2)

        def start_act(self, act):
            Epilogue.start_act(self, act)
            act.sem_inc(self.silued, 8)
            act.wait_ge(self.p_loaded, 16 * 2 * CW)

        def act(self, act, i, b):
            nc, q = self.nc, 2 * i + b
            act.wait_ge(self.chain, (q + 1) * self.STEPS)
            for m in range(2):
                blk = q * 2 + m
                for r in range(3):
                    t = 3 * m + r
                    self.wait_full(act, i, b, t)
                    bank = self.bank(b, t, P, TT)
                    if r < 2:
                        nc.scalar.activation(self.xs[b][:, m, CW - 1 + r * TT:CW - 1 + (r + 1) * TT], bank, ACT.Copy).then_inc(self.free, 1)
                    else:
                        nc.scalar.activation(self.xs[b][:, m, CW - 1 + 2 * TT:CW - 1 + TP], bank[:, 0:TP - 2 * TT], ACT.Copy).then_inc(self.tailed, 1)
                        nc.scalar.activation(self.xs[b][:, m, RUN:W], bank[:, TP - 2 * TT:TT], ACT.Copy).then_inc(self.free, 1)
                nc.scalar.activation(self.xs[b][:, m, RUN - CW + 1:RUN], self.hist[:, :, bass.ds(blk, 1)].rearrange("p j o -> p (j o)"),
                                     ACT.Copy).then_inc(self.tailed, 1)
                act.wait_ge(self.free, self.nb + q * self.tiles + 3 * m + 3)
                act.wait_ge(self.tailed, 8 * q + 4 * m + 2)
                nc.scalar.activation(self.tails[:, 0, :, bass.ds(blk, 1)].rearrange("p j o -> p (j o)"), self.xs[b][:, m, TP:TP + CW - 1],
                                     ACT.Copy).then_inc(self.tailed, 1)
                nc.scalar.activation(self.tails[:, 1, :, bass.ds(blk, 1)].rearrange("p j o -> p (j o)"), self.xs[b][:, m, W - CW + 1:W],
                                     ACT.Copy).then_inc(self.tailed, 1)
            self.wait_stage(act, i, b)
            for m in range(2):
                act.wait_ge(self.chain, (q + 2) * self.STEPS + 4 * m + 4)
                nc.scalar.activation(self.stage[b][:, m, 0:TP], self.co[b][:, m, 0:TP], ACT.Silu).then_inc(self.silued, 1)
                nc.scalar.activation(self.stage[b][:, m, TP:T], self.co[b][:, m, RUN - CW + 1:W - CW + 1], ACT.Silu).then_inc(self.silued, 1)

        def vec(self, dve, i, b):
            nc, q = self.nc, 2 * i + b
            step = Chain(dve, self.chain)
            step.enter(q + 2, self.STEPS)
            dve.wait_ge(self.silued, 4 * q + 4)
            for m in range(2):
                blk = q * 2 + m
                dve.wait_ge(self.tailed, 8 * q + 4 * m + 4)
                L = W - CW + 1
                co, xs = self.co[b][:, m, 0:L], self.xs[b][:, m, :]
                step(nc.vector.tensor_scalar(co, xs[:, 0:L], self.cw[:, 0, bass.ds(blk, 1)], self.cb[:, bass.ds(blk, 1)], ALU.mult, ALU.add))
                for j in range(1, CW):
                    step(nc.vector.scalar_tensor_tensor(out=co, in0=xs[:, j:j + L], scalar=self.cw[:, j, bass.ds(blk, 1)], in1=co,
                                                        op0=ALU.mult, op1=ALU.add))
            step.leave()

        def store(self, sp, i, b):
            sp.wait_ge(self.silued, 4 * (2 * i + b + 1) + 8)
            sp.dma_start(to[bass.ds((2 * i + b) * PW, PW), :].rearrange("(m p) t -> p m t", p=P),
                         self.stage[b][:]).then_inc(self.stored[b], 16)

        def finish(self, sp, pairs):
            Epilogue.finish(self, sp, pairs)
            with self.nc.allow_non_contiguous_dma(reason="three rows of each stream"):
                for s, tail in enumerate((tail_prompt, tail_running)):
                    for j in range(CW - 1):
                        sp.dma_start(tail[j, :].rearrange("(m p) -> p m", p=P), self.tails[:, s, j, :]).then_inc(self.tails_out, 16)
            sp.wait_ge(self.tails_out, 16 * 2 * (CW - 1))
    return lambda *a: Conv(core, *a)


def residual_tm(core, x_prompt, x_running, to_prompt, to_running):
    class Residual(Epilogue):
        STORES = 2

        def setup(self, sem):
            self.stage = [self.sb(f"stage{b}", [P, NT + 1, PW]) for b in range(2)]
            self.loaded = [sem(f"x_loaded{b}") for b in range(2)]

        def start_dve(self, dve):
            dve.sem_inc(self.free, self.nb)

        def start_act(self, act):
            pass

        def vec(self, dve, i, b):
            dve.wait_ge(self.loaded[b], 32 * (i + 1))
            for t in range(self.tiles):
                n = rows_of(t)
                self.wait_full(dve, i, b, t)
                self.nc.vector.tensor_tensor(self.stage[b][0:n, t, :], self.bank(b, t, n, PW), self.stage[b][0:n, t, :],
                                             ALU.add).then_inc(self.free, 1)

        def store(self, sp, i, b):
            self.wait_stage(sp, i, b)
            cols = bass.ds((2 * i + b) * PW, PW)
            sp.dma_start(self.stage[b][:, 0:NT, :], x_prompt[:, cols].rearrange("(t p) d -> p t d", p=P)).then_inc(self.loaded[b], 16)
            sp.dma_start(self.stage[b][0:TS, NT, :], x_running[:, cols]).then_inc(self.loaded[b], 16)
            sp.wait_ge(self.free, self.nb + (2 * i + b + 1) * self.tiles)
            sp.dma_start(to_prompt[:, cols].rearrange("(t p) d -> p t d", p=P), self.stage[b][:, 0:NT, :]).then_inc(self.stored[b], 16)
            sp.dma_start(to_running[:, cols], self.stage[b][0:TS, NT, :]).then_inc(self.stored[b], 16)
    return lambda *a: Residual(core, *a)


def gated_fm(core, gate, into, part, add):
    class Gated(Epilogue):
        STEPS = 0

        def setup(self, sem):
            self.g = [self.sb(f"g{b}", [P, 2, T]) for b in range(2)]
            self.tmp = [self.sb(f"tmp{b}", [P, TT]) for b in range(2)]
            self.loaded = [sem(f"g_loaded{b}") for b in range(2)]
            self.g_free = [sem(f"g_free{b}") for b in range(2)]
            self.STEPS = 18 if add else 0

        def start_dve(self, dve):
            dve.sem_inc(self.free, self.nb)
            for b in range(2):
                dve.sem_inc(self.g_free[b], 6)

        def start_act(self, act):
            pass

        def vec(self, dve, i, b):
            nc, q = self.nc, 2 * i + b
            step = Chain(dve, self.chain)
            step.enter(q, self.STEPS)
            dve.wait_ge(self.loaded[b], 16 * (i + 1))
            for t in range(self.tiles):
                m, cols = t // 3, slice((t % 3) * TT, (t % 3 + 1) * TT)
                self.wait_full(dve, i, b, t)
                out = into[:, bass.ds(2 * q + m, 1), cols].rearrange("p o t -> p (o t)")
                g = self.g[b][:, m, cols]
                if not add:
                    nc.vector.tensor_tensor(out, self.bank(b, t, P, TT), g, ALU.mult).then_inc(self.free, 1)
                    continue
                tmp = self.tmp[t % 2][:]
                step(nc.vector.tensor_tensor(tmp, self.bank(b, t, P, TT), part[:, bass.ds(2 * q + m, 1), cols].rearrange("p o t -> p (o t)"), ALU.add))
                dve.sem_inc(self.free, 1)
                step(nc.vector.tensor_tensor(tmp, tmp, g, ALU.mult))
                step(nc.vector.tensor_tensor(out, out, tmp, ALU.add))
            step.leave()
            if not add:
                dve.wait_ge(self.free, self.nb + (q + 1) * self.tiles)
            dve.sem_inc(self.g_free[b], 6)

        def store(self, sp, i, b):
            sp.wait_ge(self.g_free[b], 6 * (i + 1))
            sp.dma_start(self.g[b][:], gate[bass.ds((2 * i + b) * PW, PW), :].rearrange("(m p) t -> p m t", p=P)).then_inc(self.loaded[b], 16)
    return lambda *a: Gated(core, *a)


def kept_fm(core, into):
    class Kept(Epilogue):
        def act(self, act, i, b):
            for t in range(self.tiles):
                self.wait_full(act, i, b, t)
                out = into[:, bass.ds((2 * i + b) * 2 + t // 3, 1), (t % 3) * TT:(t % 3 + 1) * TT].rearrange("p o t -> p (o t)")
                self.nc.scalar.activation(out, self.bank(b, t, P, TT), ACT.Copy).then_inc(self.free, 1)
    return lambda *a: Kept(core, *a)


def split_fm(core, src, hi, lo):
    nc = core.nc
    with ExitStack() as ctx:
        sem = core.semaphores(ctx, "split")
        hi_made, lo_made, padded = sem("hi_made"), sem("lo_made"), sem("padded")
        block = ctx.enter_context(nc.Block())

        @block.scalar
        def _(act):
            for k in range(KB):
                nc.scalar.activation(hi[:, k, 0:T], src[:, k, :], ACT.Copy).then_inc(hi_made, 1)

        @block.vector
        def _(dve):
            nc.vector.memset(hi[:, :, T:TW].bitcast(F32), 0.0).then_inc(padded, 1)
            nc.vector.memset(lo[:, :, T:TW].bitcast(F32), 0.0).then_inc(padded, 1)
            for k in range(KB):
                dve.wait_ge(hi_made, k + 1)
                nc.vector.tensor_tensor(lo[:, k, 0:T], src[:, k, :], hi[:, k, 0:T].bitcast(F32), ALU.subtract).then_inc(lo_made, 1)


def mlp(core, hi, lo, w_up, w_down, x2_prompt, x2_running, y_prompt, y_running):
    nc = core.nc
    FB = FS // P
    NB = 6
    UP, DOWN = 6, 12
    PER = 2 * UP + 2 * DOWN
    start_of = [0, UP, 2 * UP, 2 * UP + DOWN]
    SLICES = FF // FS
    with ExitStack() as ctx:
        sb = lambda n, s, dt=F32: ctx.enter_context(nc.sbuf_tensor(f"mlp_{n}", s, dt))
        sem = core.semaphores(ctx, f"mlp")
        raw = [sb(f"raw{b}", [P, KB * PW]) for b in range(2)]
        whi = [sb(f"whi{b}", [P, KB * PW], F32R) for b in range(2)]
        wlo = [sb(f"wlo{b}", [P, KB * PW], F32R) for b in range(2)]
        uhi, ulo = sb("uhi", [P, FB, T], F32R), sb("ulo", [P, FB, T], F32R)
        acc = sb("acc", [P, KB, T])
        relu = [sb(f"relu{j}", [P, TT]) for j in range(2)]
        sq = [sb(f"sq{j}", [P, TT]) for j in range(2)]
        raw_loaded = [sem(f"raw_loaded{b}") for b in range(2)]
        hi_made = [sem(f"whi_made{b}") for b in range(2)]
        lo_made = [sem(f"wlo_made{b}") for b in range(2)]
        full, free, relued, u_made = sem("bank_full"), sem("bank_free"), sem("relued"), sem("u_made")
        cleared, chain = sem("cleared"), sem("vec_chain")
        bctx = ExitStack()
        block = bctx.enter_context(nc.Block())

        def weights(s, j):
            if j < 2:
                return w_up[:, bass.ds(s * FS + j * PW, PW)].rearrange("(k p) m -> p k m", p=P)
            return w_down[bass.ds(s * FS, FS), (j - 2) * 512:(j - 1) * 512].rearrange("(k p) m -> p k m", p=P)

        def items(j):
            return (0, j + 2) if j < 2 else (1, j - 2)

        @block.sync
        def _(sp):
            def load(s, j, fresh=False):
                b = j % 2
                if not fresh:
                    sp.wait_ge(lo_made[b], 2 * s + j // 2)
                view = raw[b][:].rearrange("p (k m) -> p k m", k=KB if j < 2 else FB)
                sp.dma_start(view, weights(s, j)).then_inc(raw_loaded[b], 16)
            load(0, 0, True)
            load(0, 1, True)

            def body(s, last):
                for j in range(4):
                    on, slot = items(j)
                    if not (last and on):
                        load(s + on, slot)
            loop(sp, SLICES, body)

        @block.scalar
        def _(act):
            def split(s, j, fresh=False):
                b = j % 2
                act.wait_ge(raw_loaded[b], 16 * (2 * s + j // 2 + 1))
                if not fresh:
                    before = s * PER + start_of[1 + b] if j >= 2 else (s - 1) * PER + start_of[2] + DOWN * (1 + b)
                    act.wait_ge(full, before + 1)
                nc.scalar.activation(whi[b][:], raw[b][:], ACT.Copy).then_inc(hi_made[b], 1)
            split(0, 0, True)
            split(0, 1, True)

            def body(s, last):
                for j in range(4):
                    if j < 2:
                        for t in range(UP):
                            n = start_of[j] + t
                            act.wait_ge(full, s * PER + n + 2)
                            act.wait_ge(u_made, s * 2 * UP + j * UP + t + 1)
                            nc.scalar.activation(relu[t % 2][:], core.banks[:, n % NB, 0:TT], ACT.Relu).then_inc(relued, 1)
                    on, slot = items(j)
                    if not (last and on):
                        split(s + on, slot)
            loop(act, SLICES, body)

        @block.vector
        def _(dve):
            def split(s, j):
                b = j % 2
                dve.wait_ge(hi_made[b], 2 * s + j // 2 + 1)
                nc.vector.tensor_tensor(wlo[b][:], raw[b][:], whi[b][:].bitcast(F32), ALU.subtract).then_inc(lo_made[b], 1)
            nc.vector.memset(acc[:], 0.0).then_inc(cleared, 1)
            dve.sem_inc(free, NB)
            dve.sem_inc(u_made, 2)
            split(0, 0)
            split(0, 1)
            dve.wait_ge(cleared, 1)
            STEPS = 2 * UP

            def body(s, last):
                step = Chain(dve, chain)
                step.enter(s, STEPS)
                for j in range(4):
                    if j < 2:
                        if j == 0:
                            dve.wait_ge(full, s * PER + 1)
                        for t in range(UP):
                            dve.wait_ge(relued, s * 2 * UP + j * UP + t + 1)
                            n = start_of[j] + t
                            m, cols = 2 * j + t // 3, slice((t % 3) * TT, (t % 3 + 1) * TT)
                            step(nc.vector.tensor_tensor(sq[t % 2][:], relu[t % 2][:], relu[t % 2][:], ALU.mult))
                            nc.vector.tensor_copy(uhi[:, m, cols], sq[t % 2][:]).then_inc(free, 1)
                            dve.wait_ge(free, NB + s * PER + n + 1)
                            nc.vector.tensor_tensor(ulo[:, m, cols], sq[t % 2][:], uhi[:, m, cols].bitcast(F32), ALU.subtract).then_inc(u_made, 1)
                    else:
                        for t in range(DOWN):
                            n = start_of[j] + t
                            m, cols = 4 * (j - 2) + t // 3, slice((t % 3) * TT, (t % 3 + 1) * TT)
                            dve.wait_ge(full, s * PER + n + 2)
                            nc.vector.tensor_tensor(acc[:, m, cols], core.banks[:, n % NB, 0:TT], acc[:, m, cols], ALU.add).then_inc(free, 1)
                    on, slot = items(j)
                    if not (last and on):
                        split(s + on, slot)
                step.leave()
            loop(dve, SLICES, body)

        @block.tensor
        def _(pe):
            pe.sem_inc(full, 1)

            def body(s, last):
                for j in range(4):
                    b = j % 2
                    pe.wait_ge(lo_made[b], 2 * s + j // 2 + 1)
                    if j == 2:
                        pe.wait_ge(u_made, (s + 1) * 2 * UP + 2)
                    kb, width = (KB, PW) if j < 2 else (FB, 512)
                    xh, xl = (hi, lo) if j < 2 else (uhi, ulo)
                    wh, wl = (w[b][:].rearrange("p (k m) -> p k m", k=kb) for w in (whi, wlo))
                    for t in range(UP if j < 2 else DOWN):
                        n = start_of[j] + t
                        m, r = t // 3, t % 3
                        pe.wait_ge(free, s * PER + n + 1)
                        passes = [(x, w, k) for k in range(kb) for x, w in ((xh, wh), (xh, wl), (xl, wh))]
                        for c, (x, w, k) in enumerate(passes):
                            ins = nc.tensor.matmul(core.banks[:, n % NB, 0:TT], w[:, k, m * P:(m + 1) * P], x[:, k, r * TT:(r + 1) * TT],
                                                   start=c == 0, stop=c == len(passes) - 1)
                        ins.then_inc(full, 1)
            loop(pe, SLICES, body)

        bctx.close()

        x2 = sb("x2", [P, 2, D])
        x2_loaded = [sem(f"x2_loaded{b}") for b in range(2)]
        y_stored = [sem(f"y_stored{b}") for b in range(2)]
        turned, added = sem("turned"), sem("added")
        block = ctx.enter_context(nc.Block())
        rows_dram = lambda a, r, t: r if t == NT else a[t * P:(t + 1) * P, :]

        @block.sync
        def _(sp):
            for t in range(NT + 1):
                n = rows_of(t)
                if t >= 2:
                    sp.wait_ge(y_stored[t % 2], 16 * (t // 2))
                sp.dma_start(x2[0:n, t % 2, :], rows_dram(x2_prompt, x2_running, t)).then_inc(x2_loaded[t % 2], 16)
                if t >= 1:
                    sp.wait_ge(added, 2 * t)
                    sp.dma_start(rows_dram(y_prompt, y_running, t - 1), x2[0:rows_of(t - 1), (t - 1) % 2, :]).then_inc(y_stored[(t - 1) % 2], 16)
            sp.wait_ge(added, 2 * NT + 2)
            sp.dma_start(y_running, x2[0:TS, NT % 2, :]).then_inc(y_stored[NT % 2], 16)
            for b in range(2):
                sp.wait_ge(y_stored[b], 16 * len(range(b, NT + 1, 2)))

        @block.tensor
        def _(pe):
            for t in range(NT + 1):
                n = rows_of(t)
                for half in range(2):
                    i = 2 * t + half
                    if i >= 4:
                        pe.wait_ge(added, i - 3)
                    for k in range(4):
                        last = nc.tensor.transpose(core.banks[0:n, i % 4, k * P:(k + 1) * P],
                                                   acc[:, 4 * half + k, t * P:t * P + n], core.ident[:])
                    last.then_inc(turned, 1)

        @block.vector
        def _(dve):
            for t in range(NT + 1):
                n = rows_of(t)
                dve.wait_ge(x2_loaded[t % 2], 16 * (t // 2 + 1))
                for half in range(2):
                    i = 2 * t + half
                    dve.wait_ge(turned, i + 1)
                    part = x2[0:n, t % 2, half * 512:(half + 1) * 512]
                    nc.vector.tensor_tensor(part, core.banks[0:n, i % 4, :], part, ALU.add).then_inc(added, 1)


KEYS = TP + PAST + TS


def decays(core, hi, lo, w_in, b_f, dt_bias, a_log, cache_logf, logf_prompt, logf_running, aug_q, aug_k, acum_d, keep):
    nc = core.nc
    FR, DR = slice(0, H), slice(32, 32 + HS)
    R = 64
    dt_tm, acum_tm, w_tm, ea_tm, cdec = keep
    with ExitStack() as ctx:
        sb = lambda n, s, dt=F32: ctx.enter_context(nc.sbuf_tensor(f"dec_{n}", s, dt))
        sem = core.semaphores(ctx, f"dec")
        w = sb("w", [P, KB, P])
        whi, wlo = sb("whi", [P, KB, P], F32R), sb("wlo", [P, KB, P], F32R)
        bias, A = sb("bias", [R, 1]), sb("A", [R, 1])
        v, a, e, u, l, c, r = (sb(n, [R, T]) for n in "vaeulcr")
        both, acum = sb("both", [R, T]), sb("acum", [R, T])
        past = sb("past", [P, 2, H])
        lk = sb("lk", [H, KEYS])
        aq, ak = sb("aq", [H, 2, KEYS]), sb("ak", [H, 2, KEYS])
        ones = sb("ones", [R, P])
        logf_tm = sb("logf_tm", [P, NT + 1, H])
        last = sb("last", [R, NT + 1])
        diag = sb("diag", [R, HS, NT + 1])
        loaded, zeroed, chain, act_chain = sem("loaded"), sem("zeroed"), sem("vec_chain"), sem("act_chain")
        full, turned, out = sem("bank_full"), sem("turned"), sem("out")
        step_v = {}
        block = ctx.enter_context(nc.Block())

        @block.vector
        def _(dve):
            step = Chain(dve, chain)
            nc.vector.memset(w[:], 0.0).then_inc(zeroed, 1)
            nc.vector.memset(bias[:], 0.0).then_inc(zeroed, 1)
            nc.vector.memset(A[:], 0.0).then_inc(zeroed, 1)
            for m, x in ((acum, 0.0), (ones, 1.0), (aq, 1.0), (ak, 1.0), (dt_tm, 0.0), (acum_tm, 0.0), (logf_tm, 0.0)):
                nc.vector.memset(m[:], x).then_inc(zeroed, 1)
            dve.wait_ge(zeroed, 10)
            dve.wait_ge(loaded, 16 * 6)
            dve.wait_ge(act_chain, 1)
            step(nc.vector.tensor_tensor(wlo[:], w[:], whi[:].bitcast(F32), ALU.subtract))
            step_v["split"] = step.n
            dve.wait_ge(act_chain, 7)
            step(nc.vector.tensor_scalar(u[:], e[:], 1.0, None, ALU.add))
            step_v["u"] = step.n
            step(nc.vector.tensor_scalar(c[:], u[:], -1.0, None, ALU.add))
            step(nc.vector.tensor_tensor(c[:], e[:], c[:], ALU.subtract))
            step(nc.vector.reciprocal(r[:], u[:]))
            step(nc.vector.tensor_tensor(c[:], c[:], r[:], ALU.mult))
            dve.wait_ge(act_chain, 8)
            step(nc.vector.tensor_tensor(l[:], l[:], c[:], ALU.add))
            step(nc.vector.scalar_tensor_tensor(out=both[0:32, :], in0=v[0:32, :], scalar=0.0, in1=l[0:32, :], op0=ALU.min, op1=ALU.subtract))
            step(nc.vector.scalar_tensor_tensor(out=both[DR, :], in0=v[DR, :], scalar=0.0, in1=l[DR, :], op0=ALU.max, op1=ALU.add))
            step_v["lp"] = step.n
            dve.wait_ge(act_chain, 9)
            step(nc.vector.tensor_scalar(e[DR, :], both[DR, :], A[DR, :], -1.0, ALU.mult, ALU.mult))
            for t in range(NT + 1):
                n = rows_of(t)
                cols = slice(t * P, t * P + n)
                ins = nc.vector.tensor_tensor_scan(acum[DR, cols], ones[DR, 0:n], e[DR, cols], 0.0, ALU.mult, ALU.add)
                step(ins)
            step_v["acum"] = step.n
            step(nc.vector.tensor_copy(lk[:, 0:TP], both[FR, 0:TP]))
            dve.wait_ge(turned, 1)
            step(nc.vector.tensor_copy(lk[:, TP:TP + PAST], core.banks[0:H, 4, 0:PAST]))
            step(nc.vector.tensor_copy(lk[:, TP + PAST:KEYS], both[FR, TP:T]))
            for lo_, hi_ in ((0, TP), (TP, KEYS)):
                step(nc.vector.tensor_tensor_scan(aq[:, 1, lo_:hi_], ak[:, 1, lo_:hi_], lk[:, lo_:hi_], 0.0, ALU.mult, ALU.add))
            step(nc.vector.tensor_scalar(ak[:, 0, :], aq[:, 1, :], -1.0, None, ALU.mult))
            step_v["aug"] = step.n
            step(nc.vector.tensor_copy(last[DR, 0:NT], acum[DR, P - 1:TP:P]))
            step(nc.vector.tensor_copy(last[DR, NT:NT + 1], acum[DR, T - 1:T]))
            step(nc.vector.tensor_tensor(diag[DR, :, :], core.ident[DR, DR].rearrange("p (h o) -> p h o", o=1).to_broadcast([HS, HS, NT + 1]),
                                         last[DR, None, :].to_broadcast([HS, HS, NT + 1]), ALU.mult))
            step_v["last"] = step.n
            for t in range(NT + 1):
                n = rows_of(t)
                dve.wait_ge(turned, 2 + t)
                b = core.banks[0:n, t % 2, :]
                step(nc.vector.tensor_copy(logf_tm[0:n, t, :], b[:, 0:H]))
                step(nc.vector.tensor_copy(dt_tm[0:n, t, :], b[:, 32:64]))
                step(nc.vector.tensor_copy(acum_tm[0:n, t, :], b[:, P + 32:P + 64]))
            step_v["tm"] = step.n
            dve.wait_ge(turned, 3 + NT)
            lastb = core.banks[:, 3, 0:HS * (NT + 1)].rearrange("p (h t) -> p t h", h=HS)
            step(nc.vector.tensor_tensor(w_tm[:], lastb, acum_tm[:], ALU.subtract))
            step_v["w"] = step.n
            dve.wait_ge(act_chain, 12)
            step(nc.vector.tensor_tensor(w_tm[:], w_tm[:], dt_tm[:], ALU.mult))

        @block.sync
        def _(sp):
            sp.wait_ge(zeroed, 1)
            sp.dma_start(w[:, :, FR], w_in[:, C_F:C_F + H].rearrange("(k p) m -> p k m", p=P)).then_inc(loaded, 16)
            sp.dma_start(w[:, :, DR], w_in[:, C_DT:C_DT + HS].rearrange("(k p) m -> p k m", p=P)).then_inc(loaded, 16)
            sp.wait_ge(zeroed, 3)
            with nc.allow_non_contiguous_dma(reason="one value per head"):
                sp.dma_start(bias[FR, :], b_f.rearrange("(h o) -> h o", o=1)).then_inc(loaded, 16)
                sp.dma_start(bias[DR, :], dt_bias.rearrange("(h o) -> h o", o=1)).then_inc(loaded, 16)
                sp.dma_start(A[DR, :], a_log.rearrange("(h o) -> h o", o=1)).then_inc(loaded, 16)
            sp.dma_start(past[:], cache_logf.rearrange("(t p) h -> p t h", p=P)).then_inc(loaded, 16)
            sp.wait_ge(chain, step_v["acum"])
            sp.dma_start(acum_d, acum[DR, :]).then_inc(out, 16)
            sp.wait_ge(chain, step_v["aug"])
            sp.dma_start(aug_q, aq[:]).then_inc(out, 16)
            sp.dma_start(aug_k, ak[:]).then_inc(out, 16)
            sp.wait_ge(chain, step_v["tm"])
            sp.dma_start(logf_prompt.rearrange("(t p) h -> p t h", p=P), logf_tm[:, 0:NT, :]).then_inc(out, 16)
            sp.dma_start(logf_running, logf_tm[0:TS, NT, :]).then_inc(out, 16)
            sp.wait_ge(out, 5 * 16)

        @block.scalar
        def _(act):
            step = Chain(act, act_chain)
            act.wait_ge(loaded, 16 * 6)
            act.wait_ge(zeroed, 3)
            step(nc.scalar.activation(whi[:], w[:], ACT.Copy))
            for j in range(3):
                act.wait_ge(full, j + 1)
                step(nc.scalar.activation(v[:, j * TT:(j + 1) * TT], core.banks[0:R, j, 0:TT], ACT.Identity, bias=bias[:]))
            step(nc.scalar.activation(a[:], v[:], ACT.Abs))
            step(nc.scalar.activation(a[:], a[:], ACT.Copy, scale=-1.0))
            step(nc.scalar.activation(e[:], a[:], ACT.Exp))
            act.wait_ge(chain, step_v["u"])
            step(nc.scalar.activation(l[:], u[:], ACT.Ln))
            step(nc.scalar.activation(A[DR, :], A[DR, :], ACT.Exp))
            act.wait_ge(chain, step_v["tm"])
            step(nc.scalar.activation(ea_tm[:], acum_tm[:], ACT.Exp))
            act.wait_ge(chain, step_v["w"])
            step(nc.scalar.activation(cdec[:], core.banks[:, 3, 0:HS * (NT + 1)].rearrange("p (h t) -> p h t", h=HS), ACT.Exp))
            step(nc.scalar.activation(w_tm[:], w_tm[:], ACT.Exp))

        @block.tensor
        def _(pe):
            pe.wait_ge(chain, step_v["split"])
            for j in range(3):
                passes = [(x, y, k) for k in range(KB) for x, y in ((hi, whi), (hi, wlo), (lo, whi))]
                for n, (x, y, k) in enumerate(passes):
                    ins = nc.tensor.matmul(core.banks[:, j, 0:TT], y[:, k, :], x[:, k, j * TT:(j + 1) * TT], start=n == 0, stop=n == len(passes) - 1)
                ins.then_inc(full, 1)
            for t in range(2):
                ins = nc.tensor.transpose(core.banks[0:H, 4, t * P:(t + 1) * P], past[:, t, :], core.ident[:])
            ins.then_inc(turned, 1)
            pe.wait_ge(chain, step_v["acum"])
            pe.wait_ge(act_chain, 4)
            for t in range(NT + 1):
                n = rows_of(t)
                if t >= 2:
                    pe.wait_ge(chain, step_v["last"] + 3 * (t - 1))
                for s, x in enumerate((both, acum)):
                    ins = nc.tensor.transpose(core.banks[0:n, t % 2, s * P:s * P + R], x[:, t * P:t * P + n], core.ident[0:R, 0:R])
                ins.then_inc(turned, 1)
            pe.wait_ge(chain, step_v["last"])
            nc.tensor.matmul(core.banks[:, 3, 0:HS * (NT + 1)], ones[DR, :], diag[DR, :, :].rearrange("p h t -> p (h t)"),
                             start=True, stop=True).then_inc(turned, 1)


def attention(core, q_d, k_prompt, k_running, v_prompt, v_running, cache_k, cache_v, aug_q, aug_k, att_d):
    nc = core.nc
    KX = HD + 2
    ST = NT + 1
    nkeys = [P * (s + 1) for s in range(NT)] + [PAST + TS]
    koff = [0] * NT + [TP]
    blocks = [[(j * P, min(P, n - j * P)) for j in range((n + P - 1) // P)] for n in nkeys]
    groups = [[b[g:g + 4] for g in range(0, len(b), 4)] for b in blocks]
    first_group = [sum(len(g) for g in groups[:s]) for s in range(ST + 1)]
    NG = first_group[ST]
    assert NG % 2 == 1
    PREP = 5
    with ExitStack() as ctx:
        sb = lambda n, s, dt=F32: ctx.enter_context(nc.sbuf_tensor(f"att_{n}", s, dt))
        sem = core.semaphores(ctx, f"att")
        two = lambda n, s: [sb(f"{n}{b}", s) for b in range(2)]
        q = two("q", [P, NT + 1, HD])
        k = two("k", [P, NT + 3, HD])
        v = two("v", [P, NT + 3, HD])
        qT = two("qT", [KX, TP + TS])
        kT = two("kT", [KX, KEYS])
        pr = two("pr", [P, TP])
        prT = two("prT", [P, 512])
        o = two("o", [P, ST, HD])
        nmax = two("nmax", [P, 1])
        rsum = two("rsum", [P, 1])
        rinv = two("rinv", [P, 1])
        loaded = [sem(f"loaded{b}") for b in range(2)]
        aug_loaded = [sem(f"aug_loaded{b}") for b in range(2)]
        stored = [sem(f"stored{b}") for b in range(2)]
        prep_full, prep_free = sem("prep_full"), sem("prep_free")
        s_full, s_max, s_exp = sem("scores_full"), sem("max_made"), sem("exp_made")
        t_full, t_dve = sem("probs_turned"), sem("probs_copied")
        pv, o_made = sem("pv_done"), sem("o_made")
        chain = sem("vec_chain")
        block = ctx.enter_context(nc.Block())

        @block.sync
        def _(sp):
            def load(i, b, fresh):
                h = 2 * i + b
                cols = bass.ds(h * HD, HD)
                if not fresh:
                    sp.wait_ge(pv, (h - 1) * ST + 2)
                sp.dma_start(q[b][:, 0:NT, :], q_d[0:TP, cols].rearrange("(t p) d -> p t d", p=P)).then_inc(loaded[b], 16)
                sp.dma_start(q[b][0:TS, NT, :], q_d[TP:T, cols]).then_inc(loaded[b], 16)
                for x, prompt, cache, running in ((k, k_prompt, cache_k, k_running), (v, v_prompt, cache_v, v_running)):
                    sp.dma_start(x[b][:, 0:NT, :], prompt[:, cols].rearrange("(t p) d -> p t d", p=P)).then_inc(loaded[b], 16)
                    sp.dma_start(x[b][:, NT:NT + 2, :], cache[:, cols].rearrange("(t p) d -> p t d", p=P)).then_inc(loaded[b], 16)
                    sp.dma_start(x[b][0:TS, NT + 2, :], running[:, cols]).then_inc(loaded[b], 16)
                hh = bass.ds(h, 1)
                sp.dma_start(qT[b][HD:KX, 0:TP], aug_q[hh, :, 0:TP].rearrange("o a t -> (o a) t")).then_inc(aug_loaded[b], 16)
                sp.dma_start(qT[b][HD:KX, TP:T], aug_q[hh, :, TP + PAST:KEYS].rearrange("o a t -> (o a) t")).then_inc(aug_loaded[b], 16)
                sp.dma_start(kT[b][HD:KX, :], aug_k[hh, :, :].rearrange("o a t -> (o a) t")).then_inc(aug_loaded[b], 16)

            def store(i, b):
                h = 2 * i + b
                cols = bass.ds(h * HD, HD)
                sp.wait_ge(o_made, (h + 1) * ST + 2)
                sp.dma_start(att_d[0:TP, cols].rearrange("(t p) d -> p t d", p=P), o[b][:, 0:NT, :]).then_inc(stored[b], 16)
                sp.dma_start(att_d[TP:T, cols], o[b][0:TS, NT, :]).then_inc(stored[b], 16)
            for b in range(2):
                sp.sem_inc(stored[b], 32)
            load(0, 0, True)
            load(0, 1, True)

            def body(i, last):
                for b in range(2):
                    if not last:
                        load(i + 1, b, False)
                    store(i, b)
            loop(sp, H // 2, body)
            for b in range(2):
                sp.wait_ge(stored[b], 32 * (H // 2 + 1))

        def prep_parts(b):
            def tiles(x, lo_, hi_):
                return [(x[b][0:P, t, :], P, (t - lo_) * P) for t in range(lo_, hi_)]
            return [(tiles(q, 0, 4), qT, 0, 512, True), (tiles(k, 0, 4), kT, 0, 512, False),
                    (tiles(q, 4, 8), qT, 512, 512, True), (tiles(k, 4, 8), kT, 512, 512, False),
                    (tiles(k, NT, NT + 2) + [(k[b][0:TS, NT + 2, :], TS, PAST), (q[b][0:TS, NT, :], TS, PAST + TS)], None, 0, 0, None)]

        @block.tensor
        def _(pe):
            def prep(i, b, g):
                h = 2 * i + b
                pe.wait_ge(loaded[b], 16 * 8 * (i + 1))
                core.hold(pe, prep_free, h * (PREP + 1) + g + 1)
                for src, n, col in prep_parts(b)[g][0]:
                    ins = nc.tensor.transpose(core.banks[0:HD, 6, col:col + n], src, core.ident[0:n, 0:n])
                ins.then_inc(prep_full, 1)

            def scores(i, b, s):
                h = 2 * i + b
                m, n, off = rows_of(s), nkeys[s], koff[s]
                pe.wait_ge(s_exp, h * ST + s + 1)
                for c in range(0, n, 512):
                    w = min(512, n - c)
                    bank = core.banks[0:m, 2 * ((b * ST + s) % 2) + c // 512, 0:w]
                    end = c + w == n
                    ins = nc.tensor.matmul(bank, qT[b][:, s * P:s * P + m], kT[b][:, off + c:off + c + w], start=True, stop=not end)
                    if end:
                        ins = nc.tensor.matmul(bank[:, w - m:w], core.identb[0:m, 0:m], core.maskb[0:m, 0:m], start=False, stop=True)
                ins.then_inc(s_full, 1)

            def values(i, b, s):
                h, m, par = 2 * i + b, rows_of(s), (b * ST + s) % 2
                pe.wait_ge(s_exp, h * ST + s + 3)
                pe.wait_ge(o_made, h * ST + s + 1)

                def turn(g):
                    n = h * NG + first_group[s] + g
                    slot = 4 + (b * NG + first_group[s] + g) % 2
                    core.hold(pe, t_dve, n + 1)
                    for j, (off, w) in enumerate(groups[s][g]):
                        ins = nc.tensor.transpose(core.banks[0:w, slot, j * m:(j + 1) * m], pr[(b * ST + s) % 2][0:m, off:off + w], core.ident[0:m, 0:m])
                    ins.then_inc(t_full, 1)

                def product(g):
                    n = h * NG + first_group[s] + g
                    slot = (b * NG + first_group[s] + g) % 2
                    core.hold(pe, t_dve, n + 3)
                    for j, (off, w) in enumerate(groups[s][g]):
                        tile = (off // P) + (NT if s == NT else 0)
                        first, end = off == 0, off + w == nkeys[s]
                        ins = nc.tensor.matmul(core.banks[0:m, 7, par * HD:(par + 1) * HD],
                                               prT[slot][0:w, j * m:(j + 1) * m], v[b][0:w, tile, :], start=first, stop=end)
                    if end:
                        ins.then_inc(pv, 1)
                ng = len(groups[s])
                turn(0)
                for g in range(ng):
                    if g + 1 < ng:
                        turn(g + 1)
                    product(g)

            pe.sem_inc(pv, 2)
            for g in range(PREP):
                prep(0, 0, g)

            def body(i, last):
                for b in range(2):
                    h = 2 * i + b
                    pe.wait_ge(prep_free, (h + 1) * (PREP + 1) + 1)
                    pe.wait_ge(aug_loaded[b], 48 * (i + 1))
                    for s in range(ST):
                        scores(i, b, s)
                        if s >= ST - PREP and not (last and b == 1):
                            prep(i + b, 1 - b, s - (ST - PREP))
                        if s:
                            values(i, b, s - 1)
                    values(i, b, ST - 1)
            loop(pe, H // 2, body)

        @block.scalar
        def _(act):
            act.sem_inc(prep_free, 1)
            act.sem_inc(s_exp, 2)

            def prep_copy(i, b, g):
                h = 2 * i + b
                act.wait_ge(prep_full, h * PREP + g + 1)
                _, dst, col, n, is_q = prep_parts(b)[g]
                if dst is not None:
                    nc.scalar.activation(dst[b][0:HD, col:col + n], core.banks[0:HD, 6, 0:n], ACT.Copy, scale=HD ** -0.5 if is_q else 1.0).then_inc(prep_free, 1)
                else:
                    nc.scalar.activation(kT[b][0:HD, TP:KEYS], core.banks[0:HD, 6, 0:PAST + TS], ACT.Copy).then_inc(prep_free, 1)
                    nc.scalar.activation(qT[b][0:HD, TP:T], core.banks[0:HD, 6, PAST + TS:PAST + 2 * TS], ACT.Copy, scale=HD ** -0.5).then_inc(prep_free, 1)
            for g in range(PREP):
                prep_copy(0, 0, g)

            def body(i, last):
                for b in range(2):
                    h = 2 * i + b
                    for s in range(ST):
                        m, n = rows_of(s), nkeys[s]
                        par = (b * ST + s) % 2
                        act.wait_ge(s_max, h * ST + s + 1)
                        act.wait_ge(pv, h * ST + s + 1)
                        act.wait_ge(chain, h * ST + s + 1)
                        nc.scalar.activation(pr[par][0:m, 0:n], core.banks[0:m, 2 * par:2 * par + 2, :].rearrange("p a n -> p (a n)")[:, 0:n],
                                             ACT.Exp, bias=nmax[par][0:m, :], accum_out=rsum[par][0:m, :]).then_inc(s_exp, 1)
                        if s >= ST - PREP and not (last and b == 1):
                            prep_copy(i + b, 1 - b, s - (ST - PREP))
            loop(act, H // 2, body)

        @block.vector
        def _(dve):
            dve.sem_inc(t_dve, 2)
            dve.sem_inc(o_made, 2)
            dve.sem_inc(chain, 2)

            def body(i, last):
                for b in range(2):
                    h = 2 * i + b

                    def top(s):
                        m, n = rows_of(s), nkeys[s]
                        par = (b * ST + s) % 2
                        dve.wait_ge(s_full, h * ST + s + 1)
                        nc.vector.tensor_reduce(nmax[par][0:m, :], core.banks[0:m, 2 * par:2 * par + 2, :].rearrange("p a n -> p (a n)")[:, 0:n],
                                                AX.X, ALU.max, negate=True).then_inc(s_max, 1)

                    def rest(s):
                        m = rows_of(s)
                        par = (b * ST + s) % 2
                        for g in range(len(groups[s])):
                            n = h * NG + first_group[s] + g
                            slot = (b * NG + first_group[s] + g) % 2
                            dve.wait_ge(t_full, n + 1)
                            wide = len(groups[s][g]) * m
                            nc.vector.tensor_copy(prT[slot][:, 0:wide], core.banks[:, 4 + slot, 0:wide]).then_inc(t_dve, 1)
                        if s == 0:
                            dve.wait_ge(stored[b], 32 * (i + 1))
                        dve.wait_ge(s_exp, h * ST + s + 3)
                        nc.vector.reciprocal(rinv[par][0:m, :], rsum[par][0:m, :]).then_inc(chain, 1)
                        dve.wait_ge(chain, h * ST + s + 3)
                        dve.wait_ge(pv, h * ST + s + 3)
                        nc.vector.tensor_scalar(o[b][0:m, s, :], core.banks[0:m, 7, par * HD:(par + 1) * HD], rinv[par][0:m, :], None, ALU.mult).then_inc(o_made, 1)
                    for s in range(ST):
                        top(s)
                        if s:
                            rest(s - 1)
                    rest(ST - 1)
            loop(dve, H // 2, body)


def ssd(core, xbc_d, z_d, y_d, acum_d, state_in, d_skip, norm_w, ssm_prompt, ssm_running, keep):
    nc = core.nc
    NC = NT + 1
    dt_tm, acum_tm, w_tm, ea_tm, cdec = keep
    with ExitStack() as ctx:
        sb = lambda n, s, dt=F32: ctx.enter_context(nc.sbuf_tensor(f"ssd_{n}", s, dt))
        sem = core.semaphores(ctx, f"ssd")
        two = lambda n, s: [sb(f"{n}{b}", s) for b in range(2)]
        xT, BT, CT = two("xT", [P, 2, T]), two("BT", [P, T]), two("CT", [P, T])
        z, ab = two("z", [P, NC, GW]), two("ab", [P, GH, T])
        st_in = two("st_in", [P, 2, N])
        Y = two("Y", [P, NC, GW])
        dsk, wn = sb("dsk", [P, HS]), sb("wn", [P, DI])
        h = [sb("h_prompt", [P, GW]), sb("h_running", [P, GW])]
        st_out = two("st_out", [P, 2, N])
        xb = two("xb", [P, GW + N])
        xdt, xw, xd = two("xdt", [P, GW]), two("xw", [P, GW]), two("xd", [P, GW])
        L = two("L", [P, GH, P])
        M = two("M", [P, GH, P])
        t1 = two("t1", [P, GW])
        junk = sb("junk", [P, GW])
        ss = two("ss", [P, NC])
        sems = lambda n: [sem(f"{n}{b}") for b in range(2)]
        loaded, y_stored = sems("loaded"), sems("y_stored")
        par_loaded, st_stored, cleared = sem("par_loaded"), sem("st_stored"), sem("cleared")
        turned, xb_made, cb_made = sem("turned"), sem("xb_made"), sem("cb_made")
        L_in, L_made, M_made = sem("L_in"), sem("L_made"), sem("M_made")
        off_made, st_made, diag_made = sem("off_made"), sem("st_made"), sem("diag_made")
        x_scaled, gated, summed = sem("x_scaled"), sem("gated"), sem("summed")
        mean_made, rooted = sem("mean_made"), sem("rooted")
        in_turned, out_turned, st_copied, chain = sem("in_turned"), sem("out_turned"), sem("st_copied"), sem("vec_chain")
        block = ctx.enter_context(nc.Block())
        LOADS = 7
        STEPS = 2 + 5 * NC + 4
        H_AT = lambda c: 4 + 5 * c
        Y_READ = lambda c: H_AT(c) + 2
        Y_SUM = lambda c: H_AT(c) + 3
        spread = lambda x, n: x.rearrange("p (h o) -> p h o", o=1).to_broadcast([n, GH, HD])
        heads = lambda x: x.rearrange("p (h d) -> p h d", h=GH)

        @block.sync
        def _(sp):
            sp.dma_start(dsk[:], d_skip.to_broadcast([P, HS])).then_inc(par_loaded, 16)
            sp.dma_start(wn[:], norm_w.to_broadcast([P, DI])).then_inc(par_loaded, 16)

            def load(i, b):
                g = 2 * i + b
                cols = bass.ds(g * GW, GW)
                sp.dma_start(xT[b][:], xbc_d[cols, :].rearrange("(m p) t -> p m t", p=P)).then_inc(loaded[b], 16)
                sp.dma_start(BT[b][:], xbc_d[bass.ds(g * N + DI, N), :]).then_inc(loaded[b], 16)
                sp.dma_start(CT[b][:], xbc_d[bass.ds(g * N + DI + G * N, N), :]).then_inc(loaded[b], 16)
                sp.dma_start(z[b][:, 0:NT, :], z_d[0:TP, cols].rearrange("(t p) d -> p t d", p=P)).then_inc(loaded[b], 16)
                sp.dma_start(z[b][0:TS, NT, :], z_d[TP:T, cols]).then_inc(loaded[b], 16)
                sp.dma_start(ab[b][:], acum_d[:, bass.ds(g * GH, GH), :].to_broadcast([P, GH, T])).then_inc(loaded[b], 16)
                sp.dma_start(st_in[b][:], state_in[cols, :].rearrange("(m p) n -> p m n", p=P)).then_inc(loaded[b], 16)

            def store(i, b):
                g = 2 * i + b
                cols = bass.ds(g * GW, GW)
                core.hold(sp, st_copied, 2 * g + 2)
                sp.dma_start(ssm_prompt[cols, :].rearrange("(m p) n -> p m n", p=P), st_out[0][:]).then_inc(st_stored, 16)
                sp.dma_start(ssm_running[cols, :].rearrange("(m p) n -> p m n", p=P), st_out[1][:]).then_inc(st_stored, 16)
                core.hold(sp, chain, (g + 1) * STEPS)
                sp.dma_start(y_d[0:TP, cols].rearrange("(t p) d -> p t d", p=P), Y[b][:, 0:NT, :]).then_inc(y_stored[b], 16)
                sp.dma_start(y_d[TP:T, cols], Y[b][0:TS, NT, :]).then_inc(y_stored[b], 16)
            for b in range(2):
                sp.sem_inc(y_stored[b], 32)
            sp.sem_inc(st_stored, 32)
            load(0, 0)
            load(0, 1)

            def body(i, last):
                for b in range(2):
                    store(i, b)
                    if not last:
                        load(i + 1, b)
            loop(sp, G // 2, body)
            for b in range(2):
                sp.wait_ge(y_stored[b], 32 * (G // 2 + 1))
            sp.wait_ge(st_stored, 32 * (G + 1))

        @block.tensor
        def _(pe):
            pe.sem_inc(st_made, 2)
            pe.sem_inc(diag_made, 2)

            def turn(i, b, c):
                e, n, par = (2 * i + b) * NC + c, rows_of(c), (b * NC + c) % 2
                cols = slice(c * P, c * P + n)
                pe.wait_ge(xb_made, e + 1)
                nc.tensor.transpose(core.banks[0:n, par, 0:P], xT[b][:, 0, cols], core.ident[:])
                nc.tensor.transpose(core.banks[0:n, par, P:2 * P], xT[b][:, 1, cols], core.ident[:])
                nc.tensor.transpose(core.banks[0:n, par, 2 * P:3 * P], BT[b][:, cols], core.ident[:]).then_inc(turned, 1)
                pe.wait_ge(M_made, e + 1)
                nc.tensor.matmul(core.banks[0:n, 2 + par, 0:n], BT[b][:, cols], CT[b][:, cols], start=True, stop=True).then_inc(cb_made, 1)

            def body(i, last):
                for b in range(2):
                    g = 2 * i + b
                    pe.wait_ge(loaded[b], 16 * LOADS * (i + 1))
                    pe.wait_ge(chain, g * STEPS + 1)
                    for m in range(2):
                        ins = nc.tensor.transpose(core.banks[:, 4, m * P:(m + 1) * P], st_in[b][:, m, :], core.ident[:])
                    ins.then_inc(in_turned, 1)
                    turn(i, b, 0)
                    for c in range(NC):
                        e, n, par = g * NC + c, rows_of(c), (b * NC + c) % 2
                        cols = slice(c * P, c * P + n)
                        before = 2 if c in (0, NT) else H_AT(c - 1)
                        pe.wait_ge(chain, g * STEPS + max(before, Y_READ(c - 2) if c >= 2 else 0))
                        nc.tensor.matmul(core.banks[0:n, 4 + par, 0:GW], CT[b][:, cols], h[c == NT][:], start=True, stop=True).then_inc(off_made, 1)
                        pe.wait_ge(x_scaled, 3 * e + 9)
                        nc.tensor.matmul(core.banks[:, 4 + par, GW:2 * GW], xb[par][0:n, GW:GW + N], xw[par][0:n, :], start=True, stop=True).then_inc(st_made, 1)
                        if c + 1 < NC:
                            turn(i, b, c + 1)
                        core.hold(pe, M_made, e + 3)
                        for k in range(GH):
                            ins = nc.tensor.matmul(core.banks[0:n, 6 + par, k * HD:(k + 1) * HD], M[par][0:n, k, 0:n],
                                                   xdt[par][0:n, k * HD:(k + 1) * HD], start=True, stop=True)
                        ins.then_inc(diag_made, 1)
                    pe.wait_ge(chain, g * STEPS + Y_READ(NC - 1))
                    for s in range(2):
                        for m in range(2):
                            ins = nc.tensor.transpose(core.banks[:, 6 + s, m * P:(m + 1) * P], h[s][:, m * P:(m + 1) * P], core.ident[:])
                        ins.then_inc(out_turned, 1)
                    pe.wait_ge(st_copied, 2 * g + 2)
            loop(pe, G // 2, body)

        @block.scalar
        def _(act):
            act.sem_inc(xb_made, 2)
            act.sem_inc(summed, 1)
            act.wait_ge(cleared, 4)

            def square(i, b, c):
                e, n = (2 * i + b) * NC + c, rows_of(c)
                act.wait_ge(gated, e + 3)
                act.wait_ge(summed, e + 1)
                nc.scalar.activation(junk[0:n, :], Y[b][0:n, c, :], ACT.Square, accum_out=ss[b][0:n, c:c + 1]).then_inc(summed, 1)

            def body(i, last):
                for b in range(2):
                    g = 2 * i + b
                    for c in range(NC):
                        e, n, par = g * NC + c, rows_of(c), (b * NC + c) % 2
                        act.wait_ge(turned, e + 1)
                        act.wait_ge(st_made, e + 1)
                        act.wait_ge(x_scaled, 3 * e + 3)
                        nc.scalar.activation(xb[par][0:n, :], core.banks[0:n, par, 0:GW + N], ACT.Copy).then_inc(xb_made, 1)
                        act.wait_ge(L_in, e + 1)
                        nc.scalar.activation(L[par][0:n, :, 0:n], L[par][0:n, :, 0:n], ACT.Exp).then_inc(L_made, 1)
                        if c:
                            square(i, b, c - 1)
                    square(i, b, NC - 1)
                    act.wait_ge(st_stored, 32 * (g + 1))
                    for s in range(2):
                        act.wait_ge(out_turned, 2 * g + s + 2)
                        nc.scalar.activation(st_out[s][:], core.banks[:, 6 + s, 0:2 * P].rearrange("p (m n) -> p m n", m=2), ACT.Copy).then_inc(st_copied, 1)
                    act.wait_ge(mean_made, g + 1)
                    nc.scalar.activation(ss[b][:], ss[b][:], ACT.Sqrt).then_inc(rooted, 1)
            loop(act, G // 2, body)

        @block.gpsimd
        def _(pool):
            pool.sem_inc(x_scaled, 6)
            pool.sem_inc(gated, 2)
            core.hold(pool, par_loaded, 32)
            core.hold(pool, cleared, 4)

            def gate(i, b, c):
                e, n, par = (2 * i + b) * NC + c, rows_of(c), (b * NC + c) % 2
                core.hold(pool, chain, (2 * i + b) * STEPS + Y_SUM(c))
                nc.gpsimd.tensor_tensor(Y[b][0:n, c, :], t1[par][0:n, :], z[b][0:n, c, :], ALU.mult).then_inc(gated, 1)

            def body(i, last):
                for b in range(2):
                    g = 2 * i + b
                    gh = bass.ds(g * GH, GH)
                    core.hold(pool, loaded[b], 16 * LOADS * (i + 1))
                    core.hold(pool, y_stored[b], 32 * (i + 1))
                    for c in range(NC):
                        e, n, par = g * NC + c, rows_of(c), (b * NC + c) % 2
                        core.hold(pool, xb_made, e + 3)
                        x = heads(xb[par][0:n, 0:GW])
                        core.hold(pool, st_made, e + 1)
                        nc.gpsimd.tensor_tensor(heads(xw[par][0:n, :]), x, spread(w_tm[0:n, c, gh], n), ALU.mult).then_inc(x_scaled, 1)
                        core.hold(pool, diag_made, e + 1)
                        nc.gpsimd.tensor_tensor(heads(xdt[par][0:n, :]), x, spread(dt_tm[0:n, c, gh], n), ALU.mult).then_inc(x_scaled, 1)
                        core.hold(pool, chain, g * STEPS + (Y_SUM(c - 2) if c >= 2 else 1))
                        nc.gpsimd.tensor_tensor(heads(xd[par][0:n, :]), x, spread(dsk[0:n, gh], n), ALU.mult).then_inc(x_scaled, 1)
                        if c:
                            gate(i, b, c - 1)
                    gate(i, b, NC - 1)
            loop(pool, G // 2, body)

        @block.vector
        def _(dve):
            for b in range(2):
                nc.vector.memset(ss[b][:], 1.0).then_inc(cleared, 1)
                nc.vector.memset(Y[b][:, NT, :], 0.0).then_inc(cleared, 1)
            dve.sem_inc(M_made, 2)
            dve.sem_inc(out_turned, 1)
            dve.wait_ge(par_loaded, 32)

            def body(i, last):
                for b in range(2):
                    g = 2 * i + b
                    gh = bass.ds(g * GH, GH)
                    step = Chain(dve, chain)
                    step.enter(g, STEPS)

                    def y_sum(c):
                        e, n, par = g * NC + c, rows_of(c), (b * NC + c) % 2
                        dve.wait_ge(off_made, e + 1)
                        dve.wait_ge(gated, e + 1)
                        y = t1[par][0:n, :]
                        step(nc.vector.tensor_tensor(heads(y), heads(core.banks[0:n, 4 + par, 0:GW]), spread(ea_tm[0:n, c, gh], n), ALU.mult))
                        dve.wait_ge(diag_made, e + 3)
                        step(nc.vector.tensor_tensor(y, core.banks[0:n, 6 + par, 0:GW], y, ALU.add))
                        assert step.n == Y_READ(c)
                        dve.wait_ge(x_scaled, 3 * e + 9)
                        step(nc.vector.tensor_tensor(y, y, xd[par][0:n, :], ALU.add))

                    dve.wait_ge(loaded[b], 16 * LOADS * (i + 1))
                    dve.wait_ge(out_turned, 2 * g + 1)
                    step(nc.vector.memset(h[0][:], 0.0))
                    dve.wait_ge(in_turned, g + 1)
                    step(nc.vector.tensor_copy(h[1][:], core.banks[:, 4, 0:GW]))
                    for c in range(NC):
                        e, n, par = g * NC + c, rows_of(c), (b * NC + c) % 2
                        cols = slice(c * P, c * P + n)
                        dve.wait_ge(M_made, e + 1)
                        for k in range(GH):
                            ins = nc.vector.scalar_tensor_tensor(out=L[par][0:n, k, 0:n], in0=ab[b][0:n, k, cols],
                                                                 scalar=acum_tm[0:n, c, bass.ds(g * GH + k, 1)],
                                                                 in1=core.maskT[0:n, 0:n], op0=ALU.subtract, op1=ALU.add)
                        ins.then_inc(L_in, 1)
                        if c:
                            y_sum(c - 1)
                        hc = heads(h[c == NT][:])
                        dve.wait_ge(off_made, e + 1)
                        step(nc.vector.tensor_tensor(hc, hc, spread(cdec[:, gh, c], P), ALU.mult))
                        dve.wait_ge(st_made, e + 3)
                        step(nc.vector.tensor_tensor(hc, heads(core.banks[:, 4 + par, GW:2 * GW]), hc, ALU.add))
                        assert step.n == H_AT(c)
                        dve.wait_ge(L_made, e + 1)
                        dve.wait_ge(cb_made, e + 1)
                        dve.wait_ge(diag_made, e + 1)
                        nc.vector.tensor_tensor(M[par][0:n, :, 0:n], L[par][0:n, :, 0:n],
                                                core.banks[0:n, 2 + par, 0:n].rearrange("p (o l) -> p o l", o=1).to_broadcast([n, GH, n]),
                                                ALU.mult).then_inc(M_made, 1)
                    y_sum(NC - 1)
                    dve.wait_ge(summed, (g + 1) * NC + 1)
                    step(nc.vector.tensor_scalar(ss[b][:], ss[b][:], 1.0 / GW, EPS, ALU.mult, ALU.add))
                    dve.sem_inc(mean_made, 1)
                    dve.wait_ge(rooted, g + 1)
                    step(nc.vector.reciprocal(ss[b][:], ss[b][:]))
                    step(nc.vector.tensor_tensor(Y[b][:], Y[b][:], ss[b][:].rearrange("p (c o) -> p c o", o=1).to_broadcast([P, NC, GW]), ALU.mult))
                    step(nc.vector.tensor_tensor(Y[b][:], Y[b][:], wn[:, bass.ds(g * GW, GW)].rearrange("p (o d) -> p o d", o=1).to_broadcast([P, NC, GW]), ALU.mult))
                    step.leave()
            loop(dve, G // 2, body)


def hybrid_layer(nc, I, O):
    scratch = lambda n, s: nc.dram_tensor(f"scratch_{n}", s, F32, kind="Internal").ap()
    q_d, att_d = scratch("q", [T, D]), scratch("att", [T, D])
    z_d, y_d = scratch("z", [T, DI]), scratch("y", [T, DI])
    xbc_d = scratch("xbc", [CD, T])
    ga_d, gs_d = scratch("gate_att", [D, T]), scratch("gate_ssm", [D, T])
    x2_d = scratch("x2", [T, D])
    aug_q, aug_k = scratch("aug_q", [H, 2, KEYS]), scratch("aug_k", [H, 2, KEYS])
    acum_d = scratch("acum", [1, HS, T])

    x_p, x_s = I["x_prompt"][0], I["x_sample"][0]
    w_in = I["w_in"][0]
    flat = lambda a: a[0, 0].rearrange("t h d -> t (h d)")
    row = lambda a: a
    columns = lambda w, c0, rows, width: (lambda p: w[rows, bass.ds(p * width + c0, width)])
    every = slice(0, D)
    with ExitStack() as ctx:
        core = Core(nc, ctx)
        constants(core)
        with ExitStack() as keep_ctx:
            keep = [keep_ctx.enter_context(nc.sbuf_tensor(f"keep_{n}", s, F32)) for n, s in
                    (("dt", [P, NT + 1, HS]), ("acum", [P, NT + 1, HS]), ("w", [P, NT + 1, HS]), ("ea", [P, NT + 1, HS]), ("cdec", [P, HS, NT + 1]))]
            with ExitStack() as x_ctx:
                hi = x_ctx.enter_context(nc.sbuf_tensor("xn_hi", [P, KB, TW], F32R))
                lo = x_ctx.enter_context(nc.sbuf_tensor("xn_lo", [P, KB, TW], F32R))
                transpose_split(core, "norm1", (x_p, x_s), hi, lo, I["norm1_w"])
                decays(core, hi, lo, w_in, I["b_f"][0], I["dt_bias"][0], I["A_log"][0], I["cache_logf"][0, 0],
                       O["logf_prompt"][0, 0], O["logf_sample"][0, 0], aug_q, aug_k, acum_d[0], keep)
                gemm(core, "q", hi, lo, columns(w_in, C_Q, every, PW), 2, KB, PW, True,
                     head_norm_tm(core, I["q_norm_w"], q_d[0:TP, :], q_d[TP:T, :]))
                gemm(core, "k", hi, lo, columns(w_in, C_K, every, PW), 2, KB, PW, True,
                     head_norm_tm(core, I["k_norm_w"], flat(O["k_prompt"]), flat(O["k_sample"])))
                gemm(core, "v", hi, lo, columns(w_in, C_V, every, PW), 2, KB, PW, True,
                     pointwise_tm(core, ACT.Copy, flat(O["v_prompt"]), flat(O["v_sample"])))
                gemm(core, "z", hi, lo, columns(w_in, C_Z, every, PW), 4, KB, PW, True,
                     pointwise_tm(core, ACT.Silu, z_d[0:TP, :], z_d[TP:T, :]))
                gemm(core, "xbc", hi, lo, columns(w_in, C_X, every, PW), 8, KB, PW, False,
                     conv_fm(core, I["conv_w"][0], I["conv_b"][0], I["state_conv"][0, 0], xbc_d,
                             O["conv_prompt"][0, 0], O["conv_sample"][0, 0]))
                gemm(core, "ga", hi, lo, columns(w_in, C_GA, every, PW), 2, KB, PW, False, sigmoid_fm(core, ga_d))
                gemm(core, "gs", hi, lo, columns(w_in, C_GA + D, every, PW), 2, KB, PW, False, sigmoid_fm(core, gs_d))
            attention(core, q_d, flat(O["k_prompt"]), flat(O["k_sample"]), flat(O["v_prompt"]), flat(O["v_sample"]),
                      flat(I["cache_k"]), flat(I["cache_v"]), aug_q, aug_k, att_d)
            state = lambda a: a[0, 0].rearrange("h p n -> (h p) n")
            ssd(core, xbc_d, z_d, y_d, acum_d, state(I["state_ssm"]), I["D_skip"], I["ssm_norm_w"],
                state(O["ssm_prompt"]), state(O["ssm_sample"]), keep)
        with ExitStack() as m_ctx:
            merged = m_ctx.enter_context(nc.sbuf_tensor("merged", [P, KB, T], F32))
            with ExitStack() as a_ctx:
                hi = a_ctx.enter_context(nc.sbuf_tensor("branch_hi", [P, KB, T], F32R))
                lo = a_ctx.enter_context(nc.sbuf_tensor("branch_lo", [P, KB, T], F32R))
                transpose_split(core, "att_t", (att_d[0:TP, :], att_d[TP:T, :]), hi, lo)
                gemm(core, "pa", hi, lo, columns(I["w_pa"][0], 0, every, PW), 2, KB, PW, False, gated_fm(core, ga_d, merged, None, False))
                transpose_split(core, "y_t0", (y_d[0:TP, 0:D], y_d[TP:T, 0:D]), hi, lo)
                part = a_ctx.enter_context(nc.sbuf_tensor("pb_part", [P, KB, T], F32))
                gemm(core, "pb0", hi, lo, columns(I["w_pb"][0], 0, every, PW), 2, KB, PW, False, kept_fm(core, part))
                transpose_split(core, "y_t1", (y_d[0:TP, D:DI], y_d[TP:T, D:DI]), hi, lo)
                gemm(core, "pb1", hi, lo, columns(I["w_pb"][0], 0, slice(D, DI), PW), 2, KB, PW, False, gated_fm(core, gs_d, merged, part, True))
            with ExitStack() as o_ctx:
                hi = o_ctx.enter_context(nc.sbuf_tensor("merged_hi", [P, KB, TW], F32R))
                lo = o_ctx.enter_context(nc.sbuf_tensor("merged_lo", [P, KB, TW], F32R))
                split_fm(core, merged, hi, lo)
                gemm(core, "out", hi, lo, columns(I["w_out"][0], 0, every, PW), 2, KB, PW, True,
                     residual_tm(core, x_p, x_s, x2_d[0:TP, :], x2_d[TP:T, :]))
        with ExitStack() as f_ctx:
            hi = f_ctx.enter_context(nc.sbuf_tensor("h_hi", [P, KB, T], F32R))
            lo = f_ctx.enter_context(nc.sbuf_tensor("h_lo", [P, KB, T], F32R))
            transpose_split(core, "norm2", (x2_d[0:TP, :], x2_d[TP:T, :]), hi, lo, I["norm2_w"])
            mlp(core, hi, lo, I["w_up"][0], I["w_down"][0], x2_d[0:TP, :], x2_d[TP:T, :], O["y_prompt"][0], O["y_sample"][0])


_INS = ["x_prompt", "x_sample", "cache_k", "cache_v", "cache_logf", "state_conv", "state_ssm", "norm1_w", "w_in", "b_f",
        "q_norm_w", "k_norm_w", "conv_w", "conv_b", "dt_bias", "A_log", "D_skip", "ssm_norm_w", "w_pa", "w_pb", "w_out",
        "norm2_w", "w_up", "w_down"]
_OUTS = [("y_prompt", (1, TP, D)), ("y_sample", (1, TS, D)),
         ("k_prompt", (1, 1, TP, H, HD)), ("v_prompt", (1, 1, TP, H, HD)), ("logf_prompt", (1, 1, TP, H)),
         ("conv_prompt", (1, 1, CW - 1, CD)), ("ssm_prompt", (1, 1, HS, HD, N)),
         ("k_sample", (1, 1, TS, H, HD)), ("v_sample", (1, 1, TS, H, HD)), ("logf_sample", (1, 1, TS, H)),
         ("conv_sample", (1, 1, CW - 1, CD)), ("ssm_sample", (1, 1, HS, HD, N))]


def kernel(**inputs):
    import concourse.bacc as bacc
    from concourse.bass_utils import run_bass_kernel_spmd

    nc = bacc.Bacc("TRN2", target_bir_lowering=False, num_devices=1)
    arrays = {f"in_{n}": np.ascontiguousarray(inputs[n]) for n in _INS}
    I = {n: nc.dram_tensor(f"in_{n}", arrays[f"in_{n}"].shape, F32, kind="ExternalInput").ap() for n in _INS}
    O = {n: nc.dram_tensor(f"out_{n}", s, F32, kind="ExternalOutput").ap() for n, s in _OUTS}
    hybrid_layer(nc, I, O)
    r = run_bass_kernel_spmd(nc, [arrays], core_ids=[0])
    return tuple(r.results[0][f"out_{n}"] for n, _ in _OUTS)
```

```python
from contextlib import ExitStack

import numpy as np
import concourse.bass as bass
from concourse import mybir

F32 = mybir.dt.float32
F32R = mybir.dt.float32r
BF16 = mybir.dt.bfloat16
ALU = mybir.AluOpType
ACT = mybir.ActivationFunctionType
AX = mybir.AxisListType

P = 128
D = 1024
KB = D // P
TP = 1024
TS = 32
PAST = 256
T = TP + TS
NT = TP // P
TW = (NT + 1) * P
TT = T // 3
H = 16
HD = 64
DI = 2048
HS = 32
G = 8
N = 128
GH = HS // G
GW = DI // G
CW = 4
CD = DI + 2 * G * N
FF = 4 * D
FS = 512
EPS = 1e-6
NEG = -1e30
C_Q, C_K, C_V, C_F = 0, D, 2 * D, 3 * D
C_Z = C_F + H
C_X = C_Z + DI
C_B = C_X + DI
C_C = C_B + G * N
C_DT = C_X + CD
C_GA = C_DT + HS
DPROJ = C_GA + 2 * D
PW = 256


class Chain:

    def __init__(self, eng, sem):
        self.eng, self.sem, self.base, self.n = eng, sem, 0, 0

    def __call__(self, ins):
        ins.then_inc(self.sem, 1)
        self.n += 1
        self.eng.wait_ge(self.sem, self.base + self.n)

    def enter(self, i, per):
        self.base, self.n, self.per = i * per, 0, per

    def leave(self):
        assert self.n == self.per, (self.n, self.per)


class Core:

    def __init__(self, nc, ctx):
        self.nc, self.ctx = nc, ctx
        self.banks = ctx.enter_context(nc.psum_tensor("banks", [P, 8, 512], F32))
        self.ident = ctx.enter_context(nc.sbuf_tensor("ident", [P, P], F32))
        self.identb = ctx.enter_context(nc.sbuf_tensor("identb", [P, P], BF16))
        self.maskb = ctx.enter_context(nc.sbuf_tensor("maskb", [P, P], BF16))
        self.maskT = ctx.enter_context(nc.sbuf_tensor("maskT", [P, P], F32))
        self.passed = ctx.enter_context(nc.semaphore("passed"))

    def semaphores(self, ctx, tag):
        held = []

        def clear():
            self.nc.clear_and_free_semaphores(held)
            self.nc.all_engine_barrier()
        ctx.callback(clear)

        def new(name):
            held.append(self.nc.alloc_semaphore(f"{tag}_{name}"))
            return held[-1]
        return new

    def hold(self, eng, sem, value):
        eng.wait_ge(sem, value)
        eng.sem_inc(self.passed, 1)


def loop(eng, count, body):
    if count > 1:
        with eng.Fori(0, count - 1) as i:
            body(i, False)
    body(count - 1, True)


def constants(core):
    nc = core.nc
    with ExitStack() as ctx:
        made = core.semaphores(ctx, "const")("made")
        block = ctx.enter_context(nc.Block())

        @block.gpsimd
        def _(pool):
            nc.gpsimd.memset(core.ident[:], 0.0).then_inc(made, 1)
            nc.gpsimd.memset(core.maskT[:], 0.0).then_inc(made, 1)
            nc.gpsimd.memset(core.maskb[:], 0.0).then_inc(made, 1)
            pool.wait_ge(made, 3)
            nc.gpsimd.affine_select(out=core.ident[:], in_=core.ident[:], compare_op=ALU.not_equal, fill=1.0,
                                    base=0, pattern=[[-1, P]], channel_multiplier=1).then_inc(made, 1)
            nc.gpsimd.affine_select(out=core.maskT[:], in_=core.maskT[:], compare_op=ALU.is_ge, fill=NEG,
                                    base=0, pattern=[[1, P]], channel_multiplier=-1).then_inc(made, 1)
            nc.gpsimd.affine_select(out=core.maskb[:], in_=core.maskb[:], compare_op=ALU.is_ge, fill=NEG,
                                    base=0, pattern=[[-1, P]], channel_multiplier=1).then_inc(made, 1)
            pool.wait_ge(made, 6)
            nc.gpsimd.tensor_copy(core.identb[:], core.ident[:]).then_inc(made, 1)


def transpose_split(core, tag, srcs, hi, lo, norm_w=None):
    nc = core.nc
    with ExitStack() as ctx:
        sb = lambda n, s, dt=F32: ctx.enter_context(nc.sbuf_tensor(f"{tag}_{n}", s, dt))
        sem = core.semaphores(ctx, f"{tag}")
        rows = sb("rows", [P, NT + 1, D])
        junk = sb("junk", [P, D])
        ss = sb("ss", [P, NT + 1])
        wb = sb("wb", [P, D])
        loaded = [sem(f"loaded{t}") for t in range(NT + 1)]
        w_loaded, summed, rooted, scaled = sem("w_loaded"), sem("summed"), sem("rooted"), sem("scaled")
        turned, hi_made, lo_made, chain, zeroed = sem("turned"), sem("hi_made"), sem("lo_made"), sem("chain"), sem("zeroed")
        cleared = sem("cleared")
        block = ctx.enter_context(nc.Block())
        width = hi.shape[2]

        @block.sync
        def _(sp):
            for t in range(NT):
                sp.dma_start(rows[:, t, :], srcs[0][t * P:(t + 1) * P, :]).then_inc(loaded[t], 16)
            sp.dma_start(rows[0:TS, NT, :], srcs[1]).then_inc(loaded[NT], 16)
            if norm_w is not None:
                sp.dma_start(wb[:], norm_w.to_broadcast([P, D])).then_inc(w_loaded, 16)

        @block.scalar
        def _(act):
            if norm_w is not None:
                for t in range(NT + 3):
                    if t <= NT:
                        n = rows_of(t)
                        act.wait_ge(loaded[t], 16)
                        if t:
                            act.wait_ge(summed, t)
                        nc.scalar.activation(junk[0:n, :], rows[0:n, t, :], ACT.Square,
                                             accum_out=ss[0:n, t:t + 1]).then_inc(summed, 1)
                    if t >= 2:
                        n = rows_of(t - 2)
                        act.wait_ge(chain, 2 * (t - 2) + 1)
                        nc.scalar.activation(ss[0:n, t - 2:t - 1], ss[0:n, t - 2:t - 1], ACT.Sqrt).then_inc(rooted, 1)
            for t in range(NT + 1):
                n = P if t < NT else TS
                for half in range(2):
                    act.wait_ge(turned, 2 * t + half + 1)
                    b = (2 * t + half) % 4
                    bank = core.banks[:, b, 0:4 * n].rearrange("p (k n) -> p k n", k=4)
                    nc.scalar.activation(hi[:, 4 * half:4 * half + 4, t * P:t * P + n], bank, ACT.Copy).then_inc(hi_made, 1)

        @block.vector
        def _(dve):
            step = Chain(dve, chain)
            if norm_w is not None:
                dve.wait_ge(w_loaded, 16)
                for t in range(NT + 1):
                    n = rows_of(t)
                    ms = ss[0:n, t:t + 1]
                    dve.wait_ge(summed, t + 1)
                    step(nc.vector.tensor_scalar(ms, ms, 1.0 / D, EPS, ALU.mult, ALU.add))
                    dve.wait_ge(rooted, t + 1)
                    step(nc.vector.reciprocal(ms, ms))
                    nc.vector.scalar_tensor_tensor(out=rows[0:n, t, :], in0=rows[0:n, t, :], scalar=ss[0:n, t:t + 1],
                                                   in1=wb[0:n, :], op0=ALU.mult, op1=ALU.mult).then_inc(scaled, 1)
            if width > T:
                nc.vector.memset(hi[:, :, T:width].bitcast(F32), 0.0).then_inc(cleared, 1)
                nc.vector.memset(lo[:, :, T:width].bitcast(F32), 0.0).then_inc(zeroed, 1)
            for t in range(NT + 1):
                n = P if t < NT else TS
                for half in range(2):
                    dve.wait_ge(hi_made, 2 * t + half + 1)
                    b = (2 * t + half) % 4
                    bank = core.banks[:, b, 0:4 * n].rearrange("p (k n) -> p k n", k=4)
                    nc.vector.tensor_tensor(lo[:, 4 * half:4 * half + 4, t * P:t * P + n], bank,
                                            hi[:, 4 * half:4 * half + 4, t * P:t * P + n].bitcast(F32),
                                            ALU.subtract).then_inc(lo_made, 1)

        @block.tensor
        def _(pe):
            for t in range(NT + 1):
                n = P if t < NT else TS
                if norm_w is not None:
                    pe.wait_ge(scaled, t + 1)
                else:
                    pe.wait_ge(loaded[t], 16)
                for half in range(2):
                    i = 2 * t + half
                    if i >= 4:
                        pe.wait_ge(lo_made, i - 3)
                    for k in range(4):
                        kb = 4 * half + k
                        last = nc.tensor.transpose(core.banks[:, i % 4, k * n:(k + 1) * n],
                                                   rows[0:n, t, kb * P:(kb + 1) * P], core.ident[0:n, 0:n])
                    last.then_inc(turned, 1)


def gemm(core, tag, hi, lo, weights, pairs, kb, cols, tm, make):
    nc = core.nc
    with ExitStack() as ctx:
        sb = lambda n, s, dt=F32: ctx.enter_context(nc.sbuf_tensor(f"{tag}_{n}", s, dt))
        sem = core.semaphores(ctx, f"{tag}")
        raw = [sb(f"raw{b}", [P, kb, cols]) for b in range(2)]
        whi = [sb(f"whi{b}", [P, kb, cols], F32R) for b in range(2)]
        wlo = [sb(f"wlo{b}", [P, kb, cols], F32R) for b in range(2)]
        raw_loaded = [sem(f"raw_loaded{b}") for b in range(2)]
        hi_made = [sem(f"whi_made{b}") for b in range(2)]
        lo_made = [sem(f"wlo_made{b}") for b in range(2)]
        full, free = sem("bank_full"), sem("bank_free")
        tiles = NT + 1 if tm else 3 * (cols // P)
        nb = 6
        assert 2 * tiles % nb == 0
        ep = make(ctx, sb, sem, full, free, tiles, nb)
        block = ctx.enter_context(nc.Block())

        @block.sync
        def _(sp):
            def load(i, b, fresh):
                if not fresh:
                    sp.wait_ge(lo_made[b], i)
                sp.dma_start(raw[b][:], weights(2 * i + b).rearrange("(k p) m -> p k m", p=P)).then_inc(raw_loaded[b], 16)
            ep.start_sp(sp)
            load(0, 0, True)
            load(0, 1, True)

            def body(i, last):
                for b in range(2):
                    if not last:
                        load(i + 1, b, False)
                    ep.store(sp, i, b)
            loop(sp, pairs, body)
            ep.finish(sp, pairs)

        @block.scalar
        def _(act):
            def split(i, b, fresh):
                act.wait_ge(raw_loaded[b], 16 * (i + 1))
                if not fresh:
                    act.wait_ge(full, ((i - 1) * 2 + b + 1) * tiles)
                nc.scalar.activation(whi[b][:], raw[b][:], ACT.Copy).then_inc(hi_made[b], 1)
            ep.start_act(act)
            split(0, 0, True)
            split(0, 1, True)

            def body(i, last):
                for b in range(2):
                    ep.act(act, i, b)
                    if not last:
                        split(i + 1, b, False)
            loop(act, pairs, body)

        @block.vector
        def _(dve):
            def split(i, b):
                dve.wait_ge(hi_made[b], i + 1)
                nc.vector.tensor_tensor(wlo[b][:], raw[b][:], whi[b][:].bitcast(F32), ALU.subtract).then_inc(lo_made[b], 1)
            ep.start_dve(dve)
            split(0, 0)
            split(0, 1)

            def body(i, last):
                for b in range(2):
                    ep.vec(dve, i, b)
                    if not last:
                        split(i + 1, b)
            loop(dve, pairs, body)

        @block.tensor
        def _(pe):
            def body(i, last):
                for b in range(2):
                    pe.wait_ge(lo_made[b], i + 1)
                    for t in range(tiles):
                        n = b * tiles + t
                        pe.wait_ge(free, i * 2 * tiles + n + 1)
                        passes = [(x, w, k) for k in range(kb) for x, w in ((hi, whi[b]), (hi, wlo[b]), (lo, whi[b]))]
                        for j, (x, w, k) in enumerate(passes):
                            first, end = j == 0, j == len(passes) - 1
                            if tm:
                                ins = nc.tensor.matmul(core.banks[:, n % nb, 0:cols], x[:, k, t * P:(t + 1) * P],
                                                       w[:, k, :], start=first, stop=end)
                            else:
                                m, r = t // 3, t % 3
                                ins = nc.tensor.matmul(core.banks[:, n % nb, 0:TT], w[:, k, m * P:(m + 1) * P],
                                                       x[:, k, r * TT:(r + 1) * TT], start=first, stop=end)
                        ins.then_inc(full, 1)
            loop(pe, pairs, body)


class Stream:

    def __init__(self, core, tag, sb, sem, hi, lo, panels, rounds, banks, raws=1):
        self.core, self.nc, self.hi, self.lo, self.rounds, self.banks = core, core.nc, hi, lo, rounds, banks
        self.panels, self.raws = panels, raws
        self.raw = [sb(f"{tag}_raw{r}", [P, KB, PW]) for r in range(raws)]
        self.whi = [sb(f"{tag}_whi{b}", [P, KB, PW], F32R) for b in range(2)]
        self.wlo = [sb(f"{tag}_wlo{b}", [P, KB, PW], F32R) for b in range(2)]
        self.raw_loaded = [sem(f"{tag}_raw_loaded{r}") for r in range(raws)]
        self.hi_made, self.lo_made = sem(f"{tag}_whi_made"), sem(f"{tag}_wlo_made")
        self.full, self.free = sem(f"{tag}_bank_full"), sem(f"{tag}_bank_free")
        self.tiles = [(j, t) for j, p in enumerate(panels) for t in range(NT + 1 if p[0] else 6)]
        self.slots = len(self.tiles)
        self.ends = [sum(1 for jj, _ in self.tiles if jj < j) for j in range(len(panels) + 1)]
        assert self.slots % len(banks) == 0 and len(panels) % 2 == 0

    def mine(self, ep, n):
        if not 0 <= n < self.slots:
            return []
        j, t = self.tiles[n]
        return [(self.panels[j][3], t)] if self.panels[j][2] is ep else []

    def bank(self, n, rows, cols):
        return self.core.banks[0:rows, self.banks[n % len(self.banks)], 0:cols]

    def wait_full(self, eng, i, n):
        eng.wait_ge(self.full, i * self.slots + n + 1)

    def wait_free(self, eng, i, n):
        eng.wait_ge(self.free, len(self.banks) + i * self.slots + n + 1)

    def epilogues(self):
        return list(dict.fromkeys(p[2] for p in self.panels))

    def load(self, sp, i, j, first=False):
        np_, r = len(self.panels), j % self.raws
        if not first:
            self.core.hold(sp, self.lo_made, 4 * (i * np_ + j - self.raws + 1))
        src = self.panels[j % np_][1](i + j // np_)
        sp.dma_start(self.raw[r][:], src.rearrange("(k p) m -> p k m", p=P)).then_inc(self.raw_loaded[r], 16)

    def split_hi(self, act, i, j, c, first=False):
        q = slice(c * KB // 4, (c + 1) * KB // 4)
        if c == 0:
            np_ = len(self.panels)
            act.wait_ge(self.raw_loaded[j % self.raws], 16 * (i * (np_ // self.raws) + j // self.raws + 1))
            if not first and not (isinstance(i, int) and i * np_ + j < 2):
                act.wait_ge(self.full, i * self.slots + self.ends[j - 1])
        self.nc.scalar.activation(self.whi[j % 2][:, q, :], self.raw[j % self.raws][:, q, :], ACT.Copy).then_inc(self.hi_made, 1)

    def split_lo(self, dve, i, j, c):
        q = slice(c * KB // 4, (c + 1) * KB // 4)
        dve.wait_ge(self.hi_made, 4 * (i * len(self.panels) + j) + c + 1)
        self.nc.vector.tensor_tensor(self.wlo[j % 2][:, q, :], self.raw[j % self.raws][:, q, :],
                                     self.whi[j % 2][:, q, :].bitcast(F32), ALU.subtract).then_inc(self.lo_made, 1)

    def start_sp(self, sp):
        self.load(sp, 0, 0, True)
        for ep in self.epilogues():
            ep.start_sp(sp)
        self.load(sp, 0, 1, self.raws == 2)

    def start_act(self, act):
        act.sem_inc(self.free, len(self.banks))
        for c in range(4):
            self.split_hi(act, 0, 0, c, True)
        for ep in self.epilogues():
            ep.start_act(act)

    def start_dve(self, dve):
        for c in range(4):
            self.split_lo(dve, 0, 0, c)
        for ep in self.epilogues():
            ep.start_dve(dve)

    def sp(self, sp, i, n, last):
        j, t = self.tiles[n]
        if t == 5 and not (last and j + 2 >= len(self.panels)):
            self.load(sp, i, j + 2)
        for ep in self.epilogues():
            ep.sp(sp, i, n)

    def act(self, act, i, n, last):
        j, t = self.tiles[n]
        for ep in self.epilogues():
            ep.act(act, i, n)
        if t < 4 and not (last and j + 1 == len(self.panels)):
            self.split_hi(act, i, j + 1, t)

    def dve(self, dve, i, n, last):
        j, t = self.tiles[n]
        if 1 <= t < 5 and not (last and j + 1 == len(self.panels)):
            self.split_lo(dve, i, j + 1, t - 1)
        for ep in self.epilogues():
            ep.dve(dve, i, n)

    def pe(self, pe, i, n):
        j, t = self.tiles[n]
        if t == 0:
            pe.wait_ge(self.lo_made, 4 * (i * len(self.panels) + j + 1))
        pe.wait_ge(self.free, i * self.slots + n + 1)
        wh, wl = self.whi[j % 2], self.wlo[j % 2]
        passes = [(x, w, k) for k in range(KB) for x, w in ((self.hi, wh), (self.hi, wl), (self.lo, wh))]
        for c, (x, w, k) in enumerate(passes):
            first, end = c == 0, c == len(passes) - 1
            if self.panels[j][0]:
                ins = self.nc.tensor.matmul(self.bank(n, P, PW), x[:, k, t * P:(t + 1) * P], w[:, k, :], start=first, stop=end)
            else:
                m, r = t // 3, t % 3
                ins = self.nc.tensor.matmul(self.bank(n, P, TT), w[:, k, m * P:(m + 1) * P], x[:, k, r * TT:(r + 1) * TT],
                                            start=first, stop=end)
        ins.then_inc(self.full, 1)


class SiluTm:

    def __init__(self, sb, sem, per, to_prompt, to_running):
        self.per, self.to = per, (to_prompt, to_running)
        self.stage = sb("z_stage", [P, NT + 1, PW])
        self.tanh = [sb(f"z_tanh{j}", [P, PW]) for j in range(2)]
        self.tanhed, self.made, self.stored = sem("z_tanhed"), sem("z_made"), sem("z_stored")
        assert per * (NT + 1) % 2 == 0

    def start_sp(self, sp):
        sp.sem_inc(self.stored, 32)

    def start_act(self, act):
        pass

    def start_dve(self, dve):
        dve.sem_inc(self.made, 2)

    def act(self, act, i, n):
        s = self.stream
        for k, t in s.mine(self, n):
            q, m = i * self.per + k, rows_of(t)
            if t == 0:
                act.wait_ge(self.stored, 32 * (q + 1))
            s.wait_full(act, i, n)
            act.wait_ge(self.made, q * (NT + 1) + t + 1)
            s.nc.scalar.activation(self.tanh[(k * (NT + 1) + t) % 2][0:m, :], s.bank(n, m, PW), ACT.Tanh, scale=0.5).then_inc(self.tanhed, 1)
            s.nc.scalar.activation(self.stage[0:m, t, :], s.bank(n, m, PW), ACT.Copy).then_inc(s.free, 1)

    def dve(self, dve, i, n):
        s = self.stream
        for k, t in s.mine(self, n):
            q, m = i * self.per + k, rows_of(t)
            dve.wait_ge(self.tanhed, q * (NT + 1) + t + 1)
            s.wait_free(dve, i, n)
            s.nc.vector.scalar_tensor_tensor(out=self.stage[0:m, t, :], in0=self.tanh[(k * (NT + 1) + t) % 2][0:m, :], scalar=1.0,
                                             in1=self.stage[0:m, t, :], op0=ALU.add, op1=ALU.mult).then_inc(self.made, 1)

    def sp(self, sp, i, n):
        for k, t in self.stream.mine(self, n):
            if t == NT:
                q = i * self.per + k
                self.stream.core.hold(sp, self.made, (q + 1) * (NT + 1) + 2)
                cols = bass.ds(q * PW, PW)
                sp.dma_start(self.to[0][:, cols].rearrange("(t p) d -> p t d", p=P), self.stage[:, 0:NT, :]).then_inc(self.stored, 16)
                sp.dma_start(self.to[1][:, cols], self.stage[0:TS, NT, :]).then_inc(self.stored, 16)

    def finish(self, sp):
        sp.wait_ge(self.stored, 32 * (self.stream.rounds * self.per + 1))


class ConvFm:
    W = CW - 1 + TP + CW - 1 + TS
    RUN = CW - 1 + TP + CW - 1
    L = W - CW + 1
    NB = CD // P

    def __init__(self, sb, sem, per, conv_w, conv_b, state, to, tail_prompt, tail_running):
        self.per, self.params, self.to, self.tails_to = per, (conv_w, conv_b, state), to, (tail_prompt, tail_running)
        self.xs = [sb(f"xs{m}", [P, self.W]) for m in range(2)]
        self.co = [sb(f"co{m}", [P, self.L]) for m in range(2)]
        self.tanh = sb("co_tanh", [P, self.L])
        self.rows = [sb(f"conv_rows{j}", [P, P]) for j in range(2)]
        self.taps, self.past = sb("taps", [P, CW * self.NB]), sb("past_bias", [P, CW * self.NB])
        self.tails = sb("tails", [P, 2, CW - 1, self.NB])
        self.p_loaded, self.p_turned, self.p_made, self.cleared = sem("p_loaded"), sem("p_turned"), sem("p_made"), sem("cleared")
        self.copied, self.chain = sem("xs_copied"), sem("conv_chain")
        self.tanhed, self.made = sem("co_tanhed"), sem("co_made")
        self.stored = [sem(f"co_stored{m}") for m in range(2)]
        self.tails_turned, self.tails_copied, self.tails_out = sem("tails_turned"), sem("tails_copied"), sem("tails_out")

    def ended(self, n):
        return [(k, t // 3) for k, t in self.stream.mine(self, n) if t % 3 == 2]

    def start_sp(self, sp):
        w, b, state = self.params
        NB = self.NB
        sp.dma_start(self.rows[0][:], w.rearrange("j (m p) -> (j m) p", p=P)).then_inc(self.p_loaded, 16)
        sp.dma_start(self.rows[1][0:(CW - 1) * NB, :], state.rearrange("j (m p) -> (j m) p", p=P)).then_inc(self.p_loaded, 16)
        sp.dma_start(self.rows[1][(CW - 1) * NB:CW * NB, :], b.rearrange("(m p) -> m p", p=P)).then_inc(self.p_loaded, 16)
        for m in range(2):
            sp.sem_inc(self.stored[m], 32)

    def start_pe(self, pe, bank):
        pe.wait_ge(self.p_loaded, 48)
        for j in range(2):
            ins = self.stream.nc.tensor.transpose(bank[:, 256 + j * P:256 + (j + 1) * P], self.rows[j][:], self.stream.core.ident[:])
        ins.then_inc(self.p_turned, 1)

    def start_act(self, act, bank=None):
        NB, copy = self.NB, self.stream.nc.scalar.activation
        act.wait_ge(self.p_turned, 1)
        past = (CW - 1) * NB
        bank = self.bank
        copy(self.taps[:], bank[:, 256:384], ACT.Copy, scale=0.5).then_inc(self.p_made, 1)
        copy(self.past[:, 0:past], bank[:, 384:384 + past], ACT.Copy).then_inc(self.p_made, 1)
        copy(self.past[:, past:CW * NB], bank[:, 384 + past:384 + CW * NB], ACT.Copy, scale=0.5).then_inc(self.p_made, 1)
        act.wait_ge(self.p_made, 3)

    def start_dve(self, dve):
        for m in range(2):
            self.stream.nc.vector.memset(self.xs[m][:, 0:CW - 1], 0.0).then_inc(self.cleared, 1)
        dve.sem_inc(self.chain, 8)
        dve.sem_inc(self.made, 1)
        dve.wait_ge(self.cleared, 2)
        dve.wait_ge(self.p_made, 3)

    def act(self, act, i, n):
        s, NB = self.stream, self.NB
        copy = s.nc.scalar.activation
        for k, m in self.ended(n - 4):
            B = (i * self.per + k) * 2 + m
            act.wait_ge(self.chain, 4 * B + 12)
            act.wait_ge(self.made, B + 1)
            copy(self.tanh[:], self.co[m][:], ACT.Tanh).then_inc(self.tanhed, 1)
        for k, t in s.mine(self, n):
            m, r = t // 3, t % 3
            B = (i * self.per + k) * 2 + m
            xs, bank = self.xs[m], s.bank(n, P, TT)
            if r == 0:
                act.wait_ge(self.chain, 4 * B + 4)
                copy(xs[:, self.RUN - CW + 1:self.RUN], self.past[:, 0:(CW - 1) * NB].rearrange("p (j m) -> p j m", m=NB)[:, :, bass.ds(B, 1)]
                     .rearrange("p j o -> p (j o)"), ACT.Copy).then_inc(self.copied, 1)
            s.wait_full(act, i, n)
            if r < 2:
                copy(xs[:, CW - 1 + r * TT:CW - 1 + (r + 1) * TT], bank, ACT.Copy).then_inc(s.free, 1)
                continue
            own = TP - 2 * TT
            for st, end in ((0, own), (1, TT)):
                copy(self.tails[:, st, :, bass.ds(B, 1)].rearrange("p j o -> p (j o)"), bank[:, end - CW + 1:end], ACT.Copy).then_inc(self.copied, 1)
            copy(xs[:, CW - 1 + 2 * TT:CW - 1 + TP], bank[:, 0:own], ACT.Copy).then_inc(self.copied, 1)
            copy(xs[:, self.RUN:self.W], bank[:, own:TT], ACT.Copy).then_inc(s.free, 1)

    def dve(self, dve, i, n):
        s, NB, L = self.stream, self.NB, self.L
        for lag, taps in ((1, (0, 1)), (2, (2,)), (3, (3,))):
            for k, m in self.ended(n - lag):
                B = (i * self.per + k) * 2 + m
                co, xs = self.co[m][:], self.xs[m]
                if lag == 1:
                    dve.wait_ge(self.copied, 4 * B + 4)
                    s.wait_free(dve, i, n - 1)
                    dve.wait_ge(self.stored[m], 32 * (i * self.per + k + 1))
                step = Chain(dve, self.chain)
                step.enter(B + 2, 4)
                step.n = taps[0]
                for j in taps:
                    if j == 0:
                        step(s.nc.vector.tensor_scalar(co, xs[:, 0:L], self.taps[:, bass.ds(B, 1)], self.past[:, bass.ds(B + (CW - 1) * NB, 1)],
                                                       ALU.mult, ALU.add))
                    else:
                        step(s.nc.vector.scalar_tensor_tensor(out=co, in0=xs[:, j:j + L], scalar=self.taps[:, bass.ds(B + j * NB, 1)], in1=co,
                                                              op0=ALU.mult, op1=ALU.add))
        for k, m in self.ended(n - 5):
            B = (i * self.per + k) * 2 + m
            dve.wait_ge(self.tanhed, B + 1)
            s.nc.vector.scalar_tensor_tensor(out=self.co[m][:], in0=self.tanh[:], scalar=1.0, in1=self.co[m][:],
                                             op0=ALU.add, op1=ALU.mult).then_inc(self.made, 1)

    def sp(self, sp, i, n):
        for k, m in self.ended(n - 5):
            B = (i * self.per + k) * 2 + m
            self.stream.core.hold(sp, self.made, B + 2)
            rows = bass.ds(B * P, P)
            sp.dma_start(self.to[rows, 0:TP], self.co[m][:, 0:TP]).then_inc(self.stored[m], 16)
            sp.dma_start(self.to[rows, TP:T], self.co[m][:, self.RUN - CW + 1:self.L]).then_inc(self.stored[m], 16)

    def finish_pe(self, pe, bank):
        s = self.stream
        s.wait_free(pe, s.rounds - 1, s.slots - 1)
        pe.wait_ge(self.copied, 4 * self.NB)
        rows = (CW - 1) * self.NB
        for st in range(2):
            ins = s.nc.tensor.transpose(bank[0:rows, 256 + st * P:256 + (st + 1) * P], self.tails[:, st, :, :].rearrange("p j m -> p (j m)"), s.core.ident[:])
        ins.then_inc(self.tails_turned, 1)

    def finish_act(self, act, bank):
        rows = (CW - 1) * self.NB
        act.wait_ge(self.tails_turned, 1)
        for st in range(2):
            self.stream.nc.scalar.activation(self.rows[st][0:rows, :], bank[0:rows, 256 + st * P:256 + (st + 1) * P], ACT.Copy).then_inc(self.tails_copied, 1)

    def finish(self, sp):
        rows = (CW - 1) * self.NB
        sp.wait_ge(self.tails_copied, 2)
        for st in range(2):
            sp.dma_start(self.tails_to[st].rearrange("j (m p) -> (j m) p", p=P), self.rows[st][0:rows, :]).then_inc(self.tails_out, 16)
        sp.wait_ge(self.tails_out, 32)
        for m in range(2):
            sp.wait_ge(self.stored[m], 32 * (self.stream.rounds * self.per + 1))


class Epilogue:
    STORES = 0

    def __init__(self, core, ctx, sb, sem, full, free, tiles, nb):
        self.core, self.nc, self.sb, self.full, self.free, self.tiles, self.nb = core, core.nc, sb, full, free, tiles, nb
        self.done = [sem(f"out_done{b}") for b in range(2)]
        self.stored = [sem(f"out_stored{b}") for b in range(2)]
        self.chain = sem("vec_chain")
        self.ready = sem("ready")
        self.mid = sem("mid")
        self.extra = [sem(f"extra{b}") for b in range(2)]
        self.setup(sem)

    def setup(self, sem):
        pass

    def bank(self, b, t, rows, cols):
        return self.core.banks[0:rows, (b * self.tiles + t) % self.nb, 0:cols]

    def wait_full(self, eng, i, b, t):
        eng.wait_ge(self.full, (2 * i + b) * self.tiles + t + 1)

    def start_sp(self, sp):
        if self.STORES:
            for b in range(2):
                sp.sem_inc(self.stored[b], 16 * self.STORES)

    def wait_stage(self, eng, i, b):
        eng.wait_ge(self.stored[b], 16 * self.STORES * (i + 1))

    def start_act(self, act):
        act.sem_inc(self.free, self.nb)

    def start_dve(self, dve):
        pass

    def act(self, act, i, b):
        pass

    def vec(self, dve, i, b):
        pass

    def store(self, sp, i, b):
        pass

    def finish(self, sp, pairs):
        if self.STORES:
            for b in range(2):
                self.wait_stage(sp, pairs, b)


def rows_of(t):
    return P if t < NT else TS


def pointwise_tm(core, func, to_prompt, to_running):
    class Pointwise(Epilogue):
        STORES = 2

        def setup(self, sem):
            self.stage = [self.sb(f"stage{b}", [P, NT + 1, PW]) for b in range(2)]

        def act(self, act, i, b):
            self.wait_stage(act, i, b)
            for t in range(self.tiles):
                n = rows_of(t)
                self.wait_full(act, i, b, t)
                self.nc.scalar.activation(self.stage[b][0:n, t, :], self.bank(b, t, n, PW), func).then_inc(self.free, 1)

        def store(self, sp, i, b):
            sp.wait_ge(self.free, self.nb + (2 * i + b + 1) * self.tiles)
            cols = bass.ds((2 * i + b) * PW, PW)
            sp.dma_start(to_prompt[:, cols].rearrange("(t p) d -> p t d", p=P), self.stage[b][:, 0:NT, :]).then_inc(self.stored[b], 16)
            sp.dma_start(to_running[:, cols], self.stage[b][0:TS, NT, :]).then_inc(self.stored[b], 16)
    return lambda *a: Pointwise(core, *a)


def head_norm_tm(core, weight, to_prompt, to_running):
    heads = PW // HD

    class HeadNorm(Epilogue):
        STORES = 2
        STEPS = 4

        def setup(self, sem):
            self.stage = [self.sb(f"stage{b}", [P, NT + 1, PW]) for b in range(2)]
            self.sq = [self.sb(f"sq{b}", [P, NT + 1, PW]) for b in range(2)]
            self.ss = [self.sb(f"ss{b}", [P, (NT + 1) * heads]) for b in range(2)]
            self.w = self.sb("w", [P, HD])
            self.w_loaded = sem("w_loaded")
            self.cleared = sem("cleared")
            self.squared = sem("squared")

        def start_sp(self, sp):
            Epilogue.start_sp(self, sp)
            sp.dma_start(self.w[:], weight.to_broadcast([P, HD])).then_inc(self.w_loaded, 16)

        def start_dve(self, dve):
            for b in range(2):
                self.nc.vector.memset(self.stage[b][:, NT, :], 0.0).then_inc(self.cleared, 1)
                self.nc.vector.memset(self.sq[b][:, NT, :], 0.0).then_inc(self.cleared, 1)

        def start_act(self, act):
            Epilogue.start_act(self, act)
            act.wait_ge(self.cleared, 4)

        def act(self, act, i, b):
            self.wait_stage(act, i, b)
            for t in range(self.tiles):
                n = rows_of(t)
                self.wait_full(act, i, b, t)
                self.nc.scalar.activation(self.stage[b][0:n, t, :], self.bank(b, t, n, PW), ACT.Copy).then_inc(self.squared, 1)
                self.nc.scalar.activation(self.sq[b][0:n, t, :], self.bank(b, t, n, PW), ACT.Square).then_inc(self.free, 1)
            act.wait_ge(self.mid, 2 * i + b + 1)
            self.nc.scalar.activation(self.ss[b][:], self.ss[b][:], ACT.Sqrt).then_inc(self.ready, 1)

        def vec(self, dve, i, b):
            q = 2 * i + b
            nc, step = self.nc, Chain(dve, self.chain)
            step.enter(q, self.STEPS)
            dve.wait_ge(self.free, self.nb + (q + 1) * self.tiles)
            dve.wait_ge(self.squared, (q + 1) * self.tiles)
            step(nc.vector.tensor_reduce(self.ss[b][:], self.sq[b][:].rearrange("p t (h d) -> p (t h) d", d=HD), AX.X, ALU.add))
            nc.vector.tensor_scalar(self.ss[b][:], self.ss[b][:], 1.0 / HD, EPS, ALU.mult, ALU.add).then_inc(self.mid, 1)
            dve.wait_ge(self.ready, q + 1)
            step(nc.vector.reciprocal(self.ss[b][:], self.ss[b][:]))
            stage = self.stage[b][:].rearrange("p t (h d) -> p (t h) d", d=HD)
            step(nc.vector.tensor_tensor(stage, stage, self.ss[b][:, :, None].to_broadcast([P, (NT + 1) * heads, HD]), ALU.mult))
            dve.wait_ge(self.w_loaded, 16)
            step(nc.vector.tensor_tensor(stage, stage, self.w[:, None, :].to_broadcast([P, (NT + 1) * heads, HD]), ALU.mult))
            step.leave()

        def store(self, sp, i, b):
            sp.wait_ge(self.chain, (2 * i + b + 1) * self.STEPS)
            cols = bass.ds((2 * i + b) * PW, PW)
            sp.dma_start(to_prompt[:, cols].rearrange("(t p) d -> p t d", p=P), self.stage[b][:, 0:NT, :]).then_inc(self.stored[b], 16)
            sp.dma_start(to_running[:, cols], self.stage[b][0:TS, NT, :]).then_inc(self.stored[b], 16)
    return lambda *a: HeadNorm(core, *a)


def sigmoid_fm(core, to):
    class Gate(Epilogue):
        STORES = 1

        def setup(self, sem):
            self.stage = [self.sb(f"stage{b}", [P, 2, T]) for b in range(2)]

        def act(self, act, i, b):
            self.wait_stage(act, i, b)
            for t in range(self.tiles):
                self.wait_full(act, i, b, t)
                self.nc.scalar.activation(self.stage[b][:, t // 3, (t % 3) * TT:(t % 3 + 1) * TT], self.bank(b, t, P, TT),
                                          ACT.Sigmoid).then_inc(self.free, 1)

        def store(self, sp, i, b):
            sp.wait_ge(self.free, self.nb + (2 * i + b + 1) * self.tiles)
            sp.dma_start(to[bass.ds((2 * i + b) * PW, PW), :].rearrange("(m p) t -> p m t", p=P),
                         self.stage[b][:]).then_inc(self.stored[b], 16)
    return lambda *a: Gate(core, *a)


def residual_tm(core, x_prompt, x_running, to_prompt, to_running):
    class Residual(Epilogue):
        STORES = 2

        def setup(self, sem):
            self.stage = [self.sb(f"stage{b}", [P, NT + 1, PW]) for b in range(2)]
            self.loaded = [sem(f"x_loaded{b}") for b in range(2)]

        def start_dve(self, dve):
            dve.sem_inc(self.free, self.nb)

        def start_act(self, act):
            pass

        def vec(self, dve, i, b):
            dve.wait_ge(self.loaded[b], 32 * (i + 1))
            for t in range(self.tiles):
                n = rows_of(t)
                self.wait_full(dve, i, b, t)
                self.nc.vector.tensor_tensor(self.stage[b][0:n, t, :], self.bank(b, t, n, PW), self.stage[b][0:n, t, :],
                                             ALU.add).then_inc(self.free, 1)

        def store(self, sp, i, b):
            self.wait_stage(sp, i, b)
            cols = bass.ds((2 * i + b) * PW, PW)
            sp.dma_start(self.stage[b][:, 0:NT, :], x_prompt[:, cols].rearrange("(t p) d -> p t d", p=P)).then_inc(self.loaded[b], 16)
            sp.dma_start(self.stage[b][0:TS, NT, :], x_running[:, cols]).then_inc(self.loaded[b], 16)
            sp.wait_ge(self.free, self.nb + (2 * i + b + 1) * self.tiles)
            sp.dma_start(to_prompt[:, cols].rearrange("(t p) d -> p t d", p=P), self.stage[b][:, 0:NT, :]).then_inc(self.stored[b], 16)
            sp.dma_start(to_running[:, cols], self.stage[b][0:TS, NT, :]).then_inc(self.stored[b], 16)
    return lambda *a: Residual(core, *a)


def gated_fm(core, gate, into, part, add):
    class Gated(Epilogue):
        STEPS = 0

        def setup(self, sem):
            self.g = [self.sb(f"g{b}", [P, 2, T]) for b in range(2)]
            self.tmp = [self.sb(f"tmp{b}", [P, TT]) for b in range(2)]
            self.loaded = [sem(f"g_loaded{b}") for b in range(2)]
            self.g_free = [sem(f"g_free{b}") for b in range(2)]
            self.STEPS = 18 if add else 0

        def start_dve(self, dve):
            dve.sem_inc(self.free, self.nb)
            for b in range(2):
                dve.sem_inc(self.g_free[b], 6)

        def start_act(self, act):
            pass

        def vec(self, dve, i, b):
            nc, q = self.nc, 2 * i + b
            step = Chain(dve, self.chain)
            step.enter(q, self.STEPS)
            dve.wait_ge(self.loaded[b], 16 * (i + 1))
            for t in range(self.tiles):
                m, cols = t // 3, slice((t % 3) * TT, (t % 3 + 1) * TT)
                self.wait_full(dve, i, b, t)
                out = into[:, bass.ds(2 * q + m, 1), cols].rearrange("p o t -> p (o t)")
                g = self.g[b][:, m, cols]
                if not add:
                    nc.vector.tensor_tensor(out, self.bank(b, t, P, TT), g, ALU.mult).then_inc(self.free, 1)
                    continue
                tmp = self.tmp[t % 2][:]
                step(nc.vector.tensor_tensor(tmp, self.bank(b, t, P, TT), part[:, bass.ds(2 * q + m, 1), cols].rearrange("p o t -> p (o t)"), ALU.add))
                dve.sem_inc(self.free, 1)
                step(nc.vector.tensor_tensor(tmp, tmp, g, ALU.mult))
                step(nc.vector.tensor_tensor(out, out, tmp, ALU.add))
            step.leave()
            if not add:
                dve.wait_ge(self.free, self.nb + (q + 1) * self.tiles)
            dve.sem_inc(self.g_free[b], 6)

        def store(self, sp, i, b):
            sp.wait_ge(self.g_free[b], 6 * (i + 1))
            sp.dma_start(self.g[b][:], gate[bass.ds((2 * i + b) * PW, PW), :].rearrange("(m p) t -> p m t", p=P)).then_inc(self.loaded[b], 16)
    return lambda *a: Gated(core, *a)


def kept_fm(core, into):
    class Kept(Epilogue):
        def act(self, act, i, b):
            for t in range(self.tiles):
                self.wait_full(act, i, b, t)
                out = into[:, bass.ds((2 * i + b) * 2 + t // 3, 1), (t % 3) * TT:(t % 3 + 1) * TT].rearrange("p o t -> p (o t)")
                self.nc.scalar.activation(out, self.bank(b, t, P, TT), ACT.Copy).then_inc(self.free, 1)
    return lambda *a: Kept(core, *a)


def split_fm(core, src, hi, lo):
    nc = core.nc
    with ExitStack() as ctx:
        sem = core.semaphores(ctx, "split")
        hi_made, lo_made, padded = sem("hi_made"), sem("lo_made"), sem("padded")
        block = ctx.enter_context(nc.Block())

        @block.scalar
        def _(act):
            for k in range(KB):
                nc.scalar.activation(hi[:, k, 0:T], src[:, k, :], ACT.Copy).then_inc(hi_made, 1)

        @block.vector
        def _(dve):
            nc.vector.memset(hi[:, :, T:TW].bitcast(F32), 0.0).then_inc(padded, 1)
            nc.vector.memset(lo[:, :, T:TW].bitcast(F32), 0.0).then_inc(padded, 1)
            for k in range(KB):
                dve.wait_ge(hi_made, k + 1)
                nc.vector.tensor_tensor(lo[:, k, 0:T], src[:, k, :], hi[:, k, 0:T].bitcast(F32), ALU.subtract).then_inc(lo_made, 1)


def mlp(core, hi, lo, w_up, w_down, x2_prompt, x2_running, y_prompt, y_running):
    nc = core.nc
    FB = FS // P
    NB = 6
    UP, DOWN = 6, 12
    PER = 2 * UP + 2 * DOWN
    start_of = [0, UP, 2 * UP, 2 * UP + DOWN]
    SLICES = FF // FS
    with ExitStack() as ctx:
        sb = lambda n, s, dt=F32: ctx.enter_context(nc.sbuf_tensor(f"mlp_{n}", s, dt))
        sem = core.semaphores(ctx, f"mlp")
        raw = [sb(f"raw{b}", [P, KB * PW]) for b in range(2)]
        whi = [sb(f"whi{b}", [P, KB * PW], F32R) for b in range(2)]
        wlo = [sb(f"wlo{b}", [P, KB * PW], F32R) for b in range(2)]
        uhi, ulo = sb("uhi", [P, FB, T], F32R), sb("ulo", [P, FB, T], F32R)
        acc = sb("acc", [P, KB, T])
        relu = [sb(f"relu{j}", [P, TT]) for j in range(2)]
        sq = [sb(f"sq{j}", [P, TT]) for j in range(2)]
        raw_loaded = [sem(f"raw_loaded{b}") for b in range(2)]
        hi_made = [sem(f"whi_made{b}") for b in range(2)]
        lo_made = [sem(f"wlo_made{b}") for b in range(2)]
        full, free, relued, u_made = sem("bank_full"), sem("bank_free"), sem("relued"), sem("u_made")
        cleared, chain = sem("cleared"), sem("vec_chain")
        bctx = ExitStack()
        block = bctx.enter_context(nc.Block())

        def weights(s, j):
            if j < 2:
                return w_up[:, bass.ds(s * FS + j * PW, PW)].rearrange("(k p) m -> p k m", p=P)
            return w_down[bass.ds(s * FS, FS), (j - 2) * 512:(j - 1) * 512].rearrange("(k p) m -> p k m", p=P)

        def items(j):
            return (0, j + 2) if j < 2 else (1, j - 2)

        @block.sync
        def _(sp):
            def load(s, j, fresh=False):
                b = j % 2
                if not fresh:
                    sp.wait_ge(lo_made[b], 2 * s + j // 2)
                view = raw[b][:].rearrange("p (k m) -> p k m", k=KB if j < 2 else FB)
                sp.dma_start(view, weights(s, j)).then_inc(raw_loaded[b], 16)
            load(0, 0, True)
            load(0, 1, True)

            def body(s, last):
                for j in range(4):
                    on, slot = items(j)
                    if not (last and on):
                        load(s + on, slot)
            loop(sp, SLICES, body)

        @block.scalar
        def _(act):
            def split(s, j, fresh=False):
                b = j % 2
                act.wait_ge(raw_loaded[b], 16 * (2 * s + j // 2 + 1))
                if not fresh:
                    before = s * PER + start_of[1 + b] if j >= 2 else (s - 1) * PER + start_of[2] + DOWN * (1 + b)
                    act.wait_ge(full, before + 1)
                nc.scalar.activation(whi[b][:], raw[b][:], ACT.Copy).then_inc(hi_made[b], 1)
            split(0, 0, True)
            split(0, 1, True)

            def body(s, last):
                for j in range(4):
                    if j < 2:
                        for t in range(UP):
                            n = start_of[j] + t
                            act.wait_ge(full, s * PER + n + 2)
                            act.wait_ge(u_made, s * 2 * UP + j * UP + t + 1)
                            nc.scalar.activation(relu[t % 2][:], core.banks[:, n % NB, 0:TT], ACT.Relu).then_inc(relued, 1)
                    on, slot = items(j)
                    if not (last and on):
                        split(s + on, slot)
            loop(act, SLICES, body)

        @block.vector
        def _(dve):
            def split(s, j):
                b = j % 2
                dve.wait_ge(hi_made[b], 2 * s + j // 2 + 1)
                nc.vector.tensor_tensor(wlo[b][:], raw[b][:], whi[b][:].bitcast(F32), ALU.subtract).then_inc(lo_made[b], 1)
            nc.vector.memset(acc[:], 0.0).then_inc(cleared, 1)
            dve.sem_inc(free, NB)
            dve.sem_inc(u_made, 2)
            split(0, 0)
            split(0, 1)
            dve.wait_ge(cleared, 1)
            STEPS = 2 * UP

            def body(s, last):
                step = Chain(dve, chain)
                step.enter(s, STEPS)
                for j in range(4):
                    if j < 2:
                        if j == 0:
                            dve.wait_ge(full, s * PER + 1)
                        for t in range(UP):
                            dve.wait_ge(relued, s * 2 * UP + j * UP + t + 1)
                            n = start_of[j] + t
                            m, cols = 2 * j + t // 3, slice((t % 3) * TT, (t % 3 + 1) * TT)
                            step(nc.vector.tensor_tensor(sq[t % 2][:], relu[t % 2][:], relu[t % 2][:], ALU.mult))
                            nc.vector.tensor_copy(uhi[:, m, cols], sq[t % 2][:]).then_inc(free, 1)
                            dve.wait_ge(free, NB + s * PER + n + 1)
                            nc.vector.tensor_tensor(ulo[:, m, cols], sq[t % 2][:], uhi[:, m, cols].bitcast(F32), ALU.subtract).then_inc(u_made, 1)
                    else:
                        for t in range(DOWN):
                            n = start_of[j] + t
                            m, cols = 4 * (j - 2) + t // 3, slice((t % 3) * TT, (t % 3 + 1) * TT)
                            dve.wait_ge(full, s * PER + n + 2)
                            nc.vector.tensor_tensor(acc[:, m, cols], core.banks[:, n % NB, 0:TT], acc[:, m, cols], ALU.add).then_inc(free, 1)
                    on, slot = items(j)
                    if not (last and on):
                        split(s + on, slot)
                step.leave()
            loop(dve, SLICES, body)

        @block.tensor
        def _(pe):
            pe.sem_inc(full, 1)

            def body(s, last):
                for j in range(4):
                    b = j % 2
                    pe.wait_ge(lo_made[b], 2 * s + j // 2 + 1)
                    if j == 2:
                        pe.wait_ge(u_made, (s + 1) * 2 * UP + 2)
                    kb, width = (KB, PW) if j < 2 else (FB, 512)
                    xh, xl = (hi, lo) if j < 2 else (uhi, ulo)
                    wh, wl = (w[b][:].rearrange("p (k m) -> p k m", k=kb) for w in (whi, wlo))
                    for t in range(UP if j < 2 else DOWN):
                        n = start_of[j] + t
                        m, r = t // 3, t % 3
                        pe.wait_ge(free, s * PER + n + 1)
                        passes = [(x, w, k) for k in range(kb) for x, w in ((xh, wh), (xh, wl), (xl, wh))]
                        for c, (x, w, k) in enumerate(passes):
                            ins = nc.tensor.matmul(core.banks[:, n % NB, 0:TT], w[:, k, m * P:(m + 1) * P], x[:, k, r * TT:(r + 1) * TT],
                                                   start=c == 0, stop=c == len(passes) - 1)
                        ins.then_inc(full, 1)
            loop(pe, SLICES, body)

        bctx.close()

        x2 = sb("x2", [P, 2, D])
        x2_loaded = [sem(f"x2_loaded{b}") for b in range(2)]
        y_stored = [sem(f"y_stored{b}") for b in range(2)]
        turned, added = sem("turned"), sem("added")
        block = ctx.enter_context(nc.Block())
        rows_dram = lambda a, r, t: r if t == NT else a[t * P:(t + 1) * P, :]

        @block.sync
        def _(sp):
            for t in range(NT + 1):
                n = rows_of(t)
                if t >= 2:
                    sp.wait_ge(y_stored[t % 2], 16 * (t // 2))
                sp.dma_start(x2[0:n, t % 2, :], rows_dram(x2_prompt, x2_running, t)).then_inc(x2_loaded[t % 2], 16)
                if t >= 1:
                    sp.wait_ge(added, 2 * t)
                    sp.dma_start(rows_dram(y_prompt, y_running, t - 1), x2[0:rows_of(t - 1), (t - 1) % 2, :]).then_inc(y_stored[(t - 1) % 2], 16)
            sp.wait_ge(added, 2 * NT + 2)
            sp.dma_start(y_running, x2[0:TS, NT % 2, :]).then_inc(y_stored[NT % 2], 16)
            for b in range(2):
                sp.wait_ge(y_stored[b], 16 * len(range(b, NT + 1, 2)))

        @block.tensor
        def _(pe):
            for t in range(NT + 1):
                n = rows_of(t)
                for half in range(2):
                    i = 2 * t + half
                    if i >= 4:
                        pe.wait_ge(added, i - 3)
                    for k in range(4):
                        last = nc.tensor.transpose(core.banks[0:n, i % 4, k * P:(k + 1) * P],
                                                   acc[:, 4 * half + k, t * P:t * P + n], core.ident[:])
                    last.then_inc(turned, 1)

        @block.vector
        def _(dve):
            for t in range(NT + 1):
                n = rows_of(t)
                dve.wait_ge(x2_loaded[t % 2], 16 * (t // 2 + 1))
                for half in range(2):
                    i = 2 * t + half
                    dve.wait_ge(turned, i + 1)
                    part = x2[0:n, t % 2, half * 512:(half + 1) * 512]
                    nc.vector.tensor_tensor(part, core.banks[0:n, i % 4, :], part, ALU.add).then_inc(added, 1)


KEYS = TP + PAST + TS


def decays(core, hi, lo, w_in, b_f, dt_bias, a_log, cache_logf, logf_prompt, logf_running, aug_q, aug_k, acum_d, keep):
    nc = core.nc
    FR, DR = slice(0, H), slice(32, 32 + HS)
    R = 64
    dt_tm, acum_tm, w_tm, ea_tm, cdec = keep
    with ExitStack() as ctx:
        sb = lambda n, s, dt=F32: ctx.enter_context(nc.sbuf_tensor(f"dec_{n}", s, dt))
        sem = core.semaphores(ctx, f"dec")
        w = sb("w", [P, KB, P])
        whi, wlo = sb("whi", [P, KB, P], F32R), sb("wlo", [P, KB, P], F32R)
        bias, A = sb("bias", [R, 1]), sb("A", [R, 1])
        v, a, e, u, l, c, r = (sb(n, [R, T]) for n in "vaeulcr")
        both, acum = sb("both", [R, T]), sb("acum", [R, T])
        past = sb("past", [P, 2, H])
        lk = sb("lk", [H, KEYS])
        aq, ak = sb("aq", [H, 2, KEYS]), sb("ak", [H, 2, KEYS])
        ones = sb("ones", [R, P])
        logf_tm = sb("logf_tm", [P, NT + 1, H])
        last = sb("last", [R, NT + 1])
        diag = sb("diag", [R, HS, NT + 1])
        loaded, zeroed, chain, act_chain = sem("loaded"), sem("zeroed"), sem("vec_chain"), sem("act_chain")
        full, turned, out = sem("bank_full"), sem("turned"), sem("out")
        step_v = {}
        block = ctx.enter_context(nc.Block())

        @block.vector
        def _(dve):
            step = Chain(dve, chain)
            nc.vector.memset(w[:], 0.0).then_inc(zeroed, 1)
            nc.vector.memset(bias[:], 0.0).then_inc(zeroed, 1)
            nc.vector.memset(A[:], 0.0).then_inc(zeroed, 1)
            for m, x in ((acum, 0.0), (ones, 1.0), (aq, 1.0), (ak, 1.0), (dt_tm, 0.0), (acum_tm, 0.0), (logf_tm, 0.0)):
                nc.vector.memset(m[:], x).then_inc(zeroed, 1)
            dve.wait_ge(zeroed, 10)
            dve.wait_ge(loaded, 16 * 6)
            dve.wait_ge(act_chain, 1)
            step(nc.vector.tensor_tensor(wlo[:], w[:], whi[:].bitcast(F32), ALU.subtract))
            step_v["split"] = step.n
            dve.wait_ge(act_chain, 7)
            step(nc.vector.tensor_scalar(u[:], e[:], 1.0, None, ALU.add))
            step_v["u"] = step.n
            step(nc.vector.tensor_scalar(c[:], u[:], -1.0, None, ALU.add))
            step(nc.vector.tensor_tensor(c[:], e[:], c[:], ALU.subtract))
            step(nc.vector.reciprocal(r[:], u[:]))
            step(nc.vector.tensor_tensor(c[:], c[:], r[:], ALU.mult))
            dve.wait_ge(act_chain, 8)
            step(nc.vector.tensor_tensor(l[:], l[:], c[:], ALU.add))
            step(nc.vector.scalar_tensor_tensor(out=both[0:32, :], in0=v[0:32, :], scalar=0.0, in1=l[0:32, :], op0=ALU.min, op1=ALU.subtract))
            step(nc.vector.scalar_tensor_tensor(out=both[DR, :], in0=v[DR, :], scalar=0.0, in1=l[DR, :], op0=ALU.max, op1=ALU.add))
            step_v["lp"] = step.n
            dve.wait_ge(act_chain, 9)
            step(nc.vector.tensor_scalar(e[DR, :], both[DR, :], A[DR, :], -1.0, ALU.mult, ALU.mult))
            for t in range(NT + 1):
                n = rows_of(t)
                cols = slice(t * P, t * P + n)
                ins = nc.vector.tensor_tensor_scan(acum[DR, cols], ones[DR, 0:n], e[DR, cols], 0.0, ALU.mult, ALU.add)
                step(ins)
            step_v["acum"] = step.n
            step(nc.vector.tensor_copy(lk[:, 0:TP], both[FR, 0:TP]))
            dve.wait_ge(turned, 1)
            step(nc.vector.tensor_copy(lk[:, TP:TP + PAST], core.banks[0:H, 4, 0:PAST]))
            step(nc.vector.tensor_copy(lk[:, TP + PAST:KEYS], both[FR, TP:T]))
            for lo_, hi_ in ((0, TP), (TP, KEYS)):
                step(nc.vector.tensor_tensor_scan(aq[:, 1, lo_:hi_], ak[:, 1, lo_:hi_], lk[:, lo_:hi_], 0.0, ALU.mult, ALU.add))
            step(nc.vector.tensor_scalar(ak[:, 0, :], aq[:, 1, :], -1.0, None, ALU.mult))
            step_v["aug"] = step.n
            step(nc.vector.tensor_copy(last[DR, 0:NT], acum[DR, P - 1:TP:P]))
            step(nc.vector.tensor_copy(last[DR, NT:NT + 1], acum[DR, T - 1:T]))
            step(nc.vector.tensor_tensor(diag[DR, :, :], core.ident[DR, DR].rearrange("p (h o) -> p h o", o=1).to_broadcast([HS, HS, NT + 1]),
                                         last[DR, None, :].to_broadcast([HS, HS, NT + 1]), ALU.mult))
            step_v["last"] = step.n
            for t in range(NT + 1):
                n = rows_of(t)
                dve.wait_ge(turned, 2 + t)
                b = core.banks[0:n, t % 2, :]
                step(nc.vector.tensor_copy(logf_tm[0:n, t, :], b[:, 0:H]))
                step(nc.vector.tensor_copy(dt_tm[0:n, t, :], b[:, 32:64]))
                step(nc.vector.tensor_copy(acum_tm[0:n, t, :], b[:, P + 32:P + 64]))
            step_v["tm"] = step.n
            dve.wait_ge(turned, 3 + NT)
            lastb = core.banks[:, 3, 0:HS * (NT + 1)].rearrange("p (h t) -> p t h", h=HS)
            step(nc.vector.tensor_tensor(w_tm[:], lastb, acum_tm[:], ALU.subtract))
            step_v["w"] = step.n
            dve.wait_ge(act_chain, 12)
            step(nc.vector.tensor_tensor(w_tm[:], w_tm[:], dt_tm[:], ALU.mult))

        @block.sync
        def _(sp):
            sp.wait_ge(zeroed, 1)
            sp.dma_start(w[:, :, FR], w_in[:, C_F:C_F + H].rearrange("(k p) m -> p k m", p=P)).then_inc(loaded, 16)
            sp.dma_start(w[:, :, DR], w_in[:, C_DT:C_DT + HS].rearrange("(k p) m -> p k m", p=P)).then_inc(loaded, 16)
            sp.wait_ge(zeroed, 3)
            with nc.allow_non_contiguous_dma(reason="one value per head"):
                sp.dma_start(bias[FR, :], b_f.rearrange("(h o) -> h o", o=1)).then_inc(loaded, 16)
                sp.dma_start(bias[DR, :], dt_bias.rearrange("(h o) -> h o", o=1)).then_inc(loaded, 16)
                sp.dma_start(A[DR, :], a_log.rearrange("(h o) -> h o", o=1)).then_inc(loaded, 16)
            sp.dma_start(past[:], cache_logf.rearrange("(t p) h -> p t h", p=P)).then_inc(loaded, 16)
            sp.wait_ge(chain, step_v["acum"])
            sp.dma_start(acum_d, acum[DR, :]).then_inc(out, 16)
            sp.wait_ge(chain, step_v["aug"])
            sp.dma_start(aug_q, aq[:]).then_inc(out, 16)
            sp.dma_start(aug_k, ak[:]).then_inc(out, 16)
            sp.wait_ge(chain, step_v["tm"])
            sp.dma_start(logf_prompt.rearrange("(t p) h -> p t h", p=P), logf_tm[:, 0:NT, :]).then_inc(out, 16)
            sp.dma_start(logf_running, logf_tm[0:TS, NT, :]).then_inc(out, 16)
            sp.wait_ge(out, 5 * 16)

        @block.scalar
        def _(act):
            step = Chain(act, act_chain)
            act.wait_ge(loaded, 16 * 6)
            act.wait_ge(zeroed, 3)
            step(nc.scalar.activation(whi[:], w[:], ACT.Copy))
            for j in range(3):
                act.wait_ge(full, j + 1)
                step(nc.scalar.activation(v[:, j * TT:(j + 1) * TT], core.banks[0:R, j, 0:TT], ACT.Identity, bias=bias[:]))
            step(nc.scalar.activation(a[:], v[:], ACT.Abs))
            step(nc.scalar.activation(a[:], a[:], ACT.Copy, scale=-1.0))
            step(nc.scalar.activation(e[:], a[:], ACT.Exp))
            act.wait_ge(chain, step_v["u"])
            step(nc.scalar.activation(l[:], u[:], ACT.Ln))
            step(nc.scalar.activation(A[DR, :], A[DR, :], ACT.Exp))
            act.wait_ge(chain, step_v["tm"])
            step(nc.scalar.activation(ea_tm[:], acum_tm[:], ACT.Exp))
            act.wait_ge(chain, step_v["w"])
            step(nc.scalar.activation(cdec[:], core.banks[:, 3, 0:HS * (NT + 1)].rearrange("p (h t) -> p h t", h=HS), ACT.Exp))
            step(nc.scalar.activation(w_tm[:], w_tm[:], ACT.Exp))

        @block.tensor
        def _(pe):
            pe.wait_ge(chain, step_v["split"])
            for j in range(3):
                passes = [(x, y, k) for k in range(KB) for x, y in ((hi, whi), (hi, wlo), (lo, whi))]
                for n, (x, y, k) in enumerate(passes):
                    ins = nc.tensor.matmul(core.banks[:, j, 0:TT], y[:, k, :], x[:, k, j * TT:(j + 1) * TT], start=n == 0, stop=n == len(passes) - 1)
                ins.then_inc(full, 1)
            for t in range(2):
                ins = nc.tensor.transpose(core.banks[0:H, 4, t * P:(t + 1) * P], past[:, t, :], core.ident[:])
            ins.then_inc(turned, 1)
            pe.wait_ge(chain, step_v["acum"])
            pe.wait_ge(act_chain, 4)
            for t in range(NT + 1):
                n = rows_of(t)
                if t >= 2:
                    pe.wait_ge(chain, step_v["last"] + 3 * (t - 1))
                for s, x in enumerate((both, acum)):
                    ins = nc.tensor.transpose(core.banks[0:n, t % 2, s * P:s * P + R], x[:, t * P:t * P + n], core.ident[0:R, 0:R])
                ins.then_inc(turned, 1)
            pe.wait_ge(chain, step_v["last"])
            nc.tensor.matmul(core.banks[:, 3, 0:HS * (NT + 1)], ones[DR, :], diag[DR, :, :].rearrange("p h t -> p (h t)"),
                             start=True, stop=True).then_inc(turned, 1)


def attention_z_xbc(core, hi, lo, w_in, z_d, xbc_d, conv, q_d, k_prompt, k_running, v_prompt, v_running, cache_k, cache_v,
                    aug_q, aug_k, att_d):
    nc = core.nc
    KX = HD + 2
    ST = NT + 1
    HR = 4
    ROUNDS = H // HR
    nkeys = [P * (s + 1) for s in range(NT)] + [PAST + TS]
    koff = [0] * NT + [TP]
    blocks = [[(j * P, min(P, n - j * P)) for j in range((n + P - 1) // P)] for n in nkeys]
    groups = [[b[g:g + 4] for g in range(0, len(b), 4)] for b in blocks]
    first_group = [sum(len(g) for g in groups[:s]) for s in range(ST + 1)]
    NG = first_group[ST]
    PREP = 5
    PREP_AT = 3
    B_SCORES, B_TURNED, B_PREP, B_OUT, B_TILES = 0, 2, 4, 5, (6, 7)
    with ExitStack() as ctx:
        sb = lambda n, s, dt=F32: ctx.enter_context(nc.sbuf_tensor(f"att_{n}", s, dt))
        sem = core.semaphores(ctx, f"att")
        two = lambda n, s: [sb(f"{n}{b}", s) for b in range(2)]
        XP, ZP = CD // PW // ROUNDS, DI // PW // ROUNDS
        xbc = ConvFm(sb, sem, XP, *conv["params"], xbc_d, *conv["tails"])
        z = SiluTm(sb, sem, ZP, z_d[0:TP, :], z_d[TP:T, :])
        x_panel = lambda k: (False, lambda i: w_in[:, bass.ds((i * XP + k) * PW + C_X, PW)], xbc, k)
        z_panel = lambda k: (True, lambda i: w_in[:, bass.ds((i * ZP + k) * PW + C_Z, PW)], z, k)
        stream = Stream(core, "tiles", sb, sem, hi, lo, [x_panel(0), x_panel(1), z_panel(0), x_panel(2), x_panel(3), z_panel(1)],
                        ROUNDS, B_TILES)
        xbc.stream = z.stream = stream
        out_bank = core.banks[:, B_OUT, :]
        xbc.bank = out_bank
        q = two("q", [P, NT + 1, HD])
        k = two("k", [P, NT + 3, HD])
        v = two("v", [P, NT + 3, HD])
        qT = two("qT", [KX, TP + TS])
        kT = two("kT", [KX, KEYS])
        pr = two("pr", [P, TP])
        prT = two("prT", [P, 512])
        o = two("o", [P, ST, HD])
        nmax = two("nmax", [P, 1])
        rsum = two("rsum", [P, 1])
        rinv = two("rinv", [P, 1])
        loaded = [sem(f"loaded{b}") for b in range(2)]
        aug_loaded = [sem(f"aug_loaded{b}") for b in range(2)]
        stored = [sem(f"stored{b}") for b in range(2)]
        prep_full, prep_free = sem("prep_full"), sem("prep_free")
        s_full, s_max, s_exp = sem("scores_full"), sem("max_made"), sem("exp_made")
        t_full, t_dve = sem("probs_turned"), sem("probs_copied")
        pv, o_made = sem("pv_done"), sem("o_made")
        chain = sem("vec_chain")
        block = ctx.enter_context(nc.Block())

        order = [(hb, s) for hb in range(HR) for s in range(ST)]
        spare = stream.slots // (stream.slots - len(order))
        steps = [None if n % spare == spare - 1 else order[n - n // spare] for n in range(stream.slots)]
        assert [x for x in steps if x] == order

        def after(hb, s):
            return (hb, s + 1) if s + 1 < ST else (hb + 1, 0)

        def exists(hb, last):
            return not (last and hb == HR)

        def prep_parts(b):
            def tiles(x, lo_, hi_):
                return [(x[b][0:P, t, :], P, (t - lo_) * P) for t in range(lo_, hi_)]
            return [(tiles(q, 0, 4), qT, 0, 512, True), (tiles(k, 0, 4), kT, 0, 512, False),
                    (tiles(q, 4, 8), qT, 512, 512, True), (tiles(k, 4, 8), kT, 512, 512, False),
                    (tiles(k, NT, NT + 2) + [(k[b][0:TS, NT + 2, :], TS, PAST), (q[b][0:TS, NT, :], TS, PAST + TS)], None, 0, 0, None)]

        @block.sync
        def _(sp):
            def load(i, hb, first=False):
                h, b = HR * i + hb, hb % 2
                cols = bass.ds(h * HD, HD)
                if not first:
                    core.hold(sp, pv, (h - 1) * ST + 2)
                sp.dma_start(q[b][:, 0:NT, :], q_d[0:TP, cols].rearrange("(t p) d -> p t d", p=P)).then_inc(loaded[b], 16)
                sp.dma_start(q[b][0:TS, NT, :], q_d[TP:T, cols]).then_inc(loaded[b], 16)
                for x, prompt, cache, running in ((k, k_prompt, cache_k, k_running), (v, v_prompt, cache_v, v_running)):
                    sp.dma_start(x[b][:, 0:NT, :], prompt[:, cols].rearrange("(t p) d -> p t d", p=P)).then_inc(loaded[b], 16)
                    sp.dma_start(x[b][:, NT:NT + 2, :], cache[:, cols].rearrange("(t p) d -> p t d", p=P)).then_inc(loaded[b], 16)
                    sp.dma_start(x[b][0:TS, NT + 2, :], running[:, cols]).then_inc(loaded[b], 16)
                hh = bass.ds(h, 1)
                sp.dma_start(qT[b][HD:KX, 0:TP], aug_q[hh, :, 0:TP].rearrange("o a t -> (o a) t")).then_inc(aug_loaded[b], 16)
                sp.dma_start(qT[b][HD:KX, TP:T], aug_q[hh, :, TP + PAST:KEYS].rearrange("o a t -> (o a) t")).then_inc(aug_loaded[b], 16)
                sp.dma_start(kT[b][HD:KX, :], aug_k[hh, :, :].rearrange("o a t -> (o a) t")).then_inc(aug_loaded[b], 16)

            def store(i, hb):
                h, b = HR * i + hb, hb % 2
                cols = bass.ds(h * HD, HD)
                core.hold(sp, o_made, (h + 1) * ST + 2)
                sp.dma_start(att_d[0:TP, cols].rearrange("(t p) d -> p t d", p=P), o[b][:, 0:NT, :]).then_inc(stored[b], 16)
                sp.dma_start(att_d[TP:T, cols], o[b][0:TS, NT, :]).then_inc(stored[b], 16)
            for b in range(2):
                sp.sem_inc(stored[b], 32)
            load(0, 0, True)
            stream.start_sp(sp)

            def body(i, last):
                for n in range(stream.slots):
                    if steps[n]:
                        hb, s = steps[n]
                        if s == 1 and exists(hb + 1, last):
                            load(i, hb + 1)
                    stream.sp(sp, i, n, last)
                    if steps[n] and s == ST - 1:
                        store(i, hb)
            loop(sp, ROUNDS, body)
            for b in range(2):
                sp.wait_ge(stored[b], 32 * (H // 2 + 1))
            z.finish(sp)
            xbc.finish(sp)

        @block.tensor
        def _(pe):
            def prep(i, hb, g):
                h, b = HR * i + hb, hb % 2
                pe.wait_ge(loaded[b], 16 * 8 * (HR // 2 * i + hb // 2 + 1))
                core.hold(pe, prep_free, h * (PREP + 1) + g + 1)
                for src, n, col in prep_parts(b)[g][0]:
                    ins = nc.tensor.transpose(core.banks[0:HD, B_PREP, col:col + n], src, core.ident[0:n, 0:n])
                ins.then_inc(prep_full, 1)

            def scores(i, hb, s):
                h, b = HR * i + hb, hb % 2
                m, n, off = rows_of(s), nkeys[s], koff[s]
                if s == 0:
                    pe.wait_ge(prep_free, (h + 1) * (PREP + 1) + 1)
                    pe.wait_ge(aug_loaded[b], 48 * (HR // 2 * i + hb // 2 + 1))
                pe.wait_ge(s_exp, h * ST + s + 2)
                for c in range(0, n, 512):
                    w = min(512, n - c)
                    bank = core.banks[0:m, B_SCORES + c // 512, 0:w]
                    end = c + w == n
                    ins = nc.tensor.matmul(bank, qT[b][:, s * P:s * P + m], kT[b][:, off + c:off + c + w], start=True, stop=not end)
                    if end:
                        ins = nc.tensor.matmul(bank[:, w - m:w], core.identb[0:m, 0:m], core.maskb[0:m, 0:m], start=False, stop=True)
                ins.then_inc(s_full, 1)

            def turn(i, hb, s, g):
                h, m, par = HR * i + hb, rows_of(s), (hb * ST + s) % 2
                n = h * NG + first_group[s] + g
                slot = B_TURNED + (hb * NG + first_group[s] + g) % 2
                if g == 0:
                    pe.wait_ge(s_exp, h * ST + s + 3)
                core.hold(pe, t_dve, n + 1)
                for j, (off, w) in enumerate(groups[s][g]):
                    ins = nc.tensor.transpose(core.banks[0:w, slot, j * m:(j + 1) * m], pr[par][0:m, off:off + w], core.ident[0:m, 0:m])
                ins.then_inc(t_full, 1)

            def product(i, hb, s, g):
                h, b, m, par = HR * i + hb, hb % 2, rows_of(s), (hb * ST + s) % 2
                n = h * NG + first_group[s] + g
                slot = (hb * NG + first_group[s] + g) % 2
                pe.wait_ge(o_made, h * ST + s + 1)
                core.hold(pe, t_dve, n + 3)
                for j, (off, w) in enumerate(groups[s][g]):
                    tile = (off // P) + (NT if s == NT else 0)
                    first, end = off == 0, off + w == nkeys[s]
                    ins = nc.tensor.matmul(out_bank[0:m, par * HD:(par + 1) * HD],
                                           prT[slot][0:w, j * m:(j + 1) * m], v[b][0:w, tile, :], start=first, stop=end)
                if end:
                    ins.then_inc(pv, 1)

            pe.sem_inc(pv, 2)
            xbc.start_pe(pe, out_bank)
            for g in range(PREP):
                prep(0, 0, g)
            scores(0, 0, 0)

            def body(i, last):
                for n in range(stream.slots):
                    if steps[n] is None:
                        stream.pe(pe, i, n)
                        continue
                    hb, s = steps[n]
                    for g in range(len(groups[s])):
                        turn(i, hb, s, g)
                    hn, sn = after(hb, s)
                    if exists(hn, last):
                        scores(i, hn, sn)
                    stream.pe(pe, i, n)
                    if PREP_AT <= s < PREP_AT + PREP and exists(hb + 1, last):
                        prep(i, hb + 1, s - PREP_AT)
                    for g in range(len(groups[s])):
                        product(i, hb, s, g)
            loop(pe, ROUNDS, body)
            pe.wait_ge(o_made, H * ST + 2)
            xbc.finish_pe(pe, out_bank)

        @block.scalar
        def _(act):
            act.sem_inc(prep_free, 1)
            act.sem_inc(s_exp, 2)

            def prep_copy(i, hb, g):
                h, b = HR * i + hb, hb % 2
                act.wait_ge(prep_full, h * PREP + g + 1)
                _, dst, col, n, is_q = prep_parts(b)[g]
                if dst is not None:
                    nc.scalar.activation(dst[b][0:HD, col:col + n], core.banks[0:HD, B_PREP, 0:n], ACT.Copy, scale=HD ** -0.5 if is_q else 1.0).then_inc(prep_free, 1)
                else:
                    nc.scalar.activation(kT[b][0:HD, TP:KEYS], core.banks[0:HD, B_PREP, 0:PAST + TS], ACT.Copy).then_inc(prep_free, 1)
                    nc.scalar.activation(qT[b][0:HD, TP:T], core.banks[0:HD, B_PREP, PAST + TS:PAST + 2 * TS], ACT.Copy, scale=HD ** -0.5).then_inc(prep_free, 1)

            def exp(i, hb, s):
                e, m, n, par = (HR * i + hb) * ST + s, rows_of(s), nkeys[s], (hb * ST + s) % 2
                act.wait_ge(s_max, e + 1)
                act.wait_ge(pv, e + 1)
                act.wait_ge(chain, e + 1)
                nc.scalar.activation(pr[par][0:m, 0:n], core.banks[0:m, B_SCORES:B_SCORES + 2, :].rearrange("p a n -> p (a n)")[:, 0:n],
                                     ACT.Exp, bias=nmax[par][0:m, :], accum_out=rsum[par][0:m, :]).then_inc(s_exp, 1)
            stream.start_act(act)
            for g in range(PREP):
                prep_copy(0, 0, g)
            exp(0, 0, 0)

            def body(i, last):
                for n in range(stream.slots):
                    if steps[n]:
                        hb, s = steps[n]
                        hn, sn = after(hb, s)
                        if exists(hn, last):
                            exp(i, hn, sn)
                    stream.act(act, i, n, last)
                    if steps[n] and PREP_AT <= s < PREP_AT + PREP and exists(hb + 1, last):
                        prep_copy(i, hb + 1, s - PREP_AT)
            loop(act, ROUNDS, body)
            xbc.finish_act(act, out_bank)

        @block.vector
        def _(dve):
            dve.sem_inc(t_dve, 2)
            dve.sem_inc(o_made, 2)
            dve.sem_inc(chain, 2)

            def top(i, hb, s):
                e, m, n, par = (HR * i + hb) * ST + s, rows_of(s), nkeys[s], (hb * ST + s) % 2
                dve.wait_ge(s_full, e + 1)
                nc.vector.tensor_reduce(nmax[par][0:m, :], core.banks[0:m, B_SCORES:B_SCORES + 2, :].rearrange("p a n -> p (a n)")[:, 0:n],
                                        AX.X, ALU.max, negate=True).then_inc(s_max, 1)

            def copies(i, hb, s):
                h, m = HR * i + hb, rows_of(s)
                for g in range(len(groups[s])):
                    n = h * NG + first_group[s] + g
                    slot = (hb * NG + first_group[s] + g) % 2
                    dve.wait_ge(t_full, n + 1)
                    wide = len(groups[s][g]) * m
                    nc.vector.tensor_copy(prT[slot][:, 0:wide], core.banks[:, B_TURNED + slot, 0:wide]).then_inc(t_dve, 1)

            def scale(i, hb, s):
                e, b, m, par = (HR * i + hb) * ST + s, hb % 2, rows_of(s), (hb * ST + s) % 2
                if s == 0:
                    dve.wait_ge(stored[b], 32 * (HR // 2 * i + hb // 2 + 1))
                dve.wait_ge(s_exp, e + 3)
                nc.vector.reciprocal(rinv[par][0:m, :], rsum[par][0:m, :]).then_inc(chain, 1)
                dve.wait_ge(chain, e + 3)
                dve.wait_ge(pv, e + 3)
                nc.vector.tensor_scalar(o[b][0:m, s, :], out_bank[0:m, par * HD:(par + 1) * HD], rinv[par][0:m, :], None, ALU.mult).then_inc(o_made, 1)
            stream.start_dve(dve)
            top(0, 0, 0)

            def body(i, last):
                for n in range(stream.slots):
                    if steps[n]:
                        hb, s = steps[n]
                        copies(i, hb, s)
                        hn, sn = after(hb, s)
                        if exists(hn, last):
                            top(i, hn, sn)
                    stream.dve(dve, i, n, last)
                    if steps[n]:
                        scale(i, hb, s)
            loop(dve, ROUNDS, body)


def ssd(core, xbc_d, z_d, y_d, acum_d, state_in, d_skip, norm_w, ssm_prompt, ssm_running, keep):
    nc = core.nc
    NC = NT + 1
    dt_tm, acum_tm, w_tm, ea_tm, cdec = keep
    with ExitStack() as ctx:
        sb = lambda n, s, dt=F32: ctx.enter_context(nc.sbuf_tensor(f"ssd_{n}", s, dt))
        sem = core.semaphores(ctx, f"ssd")
        two = lambda n, s: [sb(f"{n}{b}", s) for b in range(2)]
        xT, BT, CT = two("xT", [P, 2, T]), two("BT", [P, T]), two("CT", [P, T])
        z, ab = two("z", [P, NC, GW]), two("ab", [P, GH, T])
        st_in = two("st_in", [P, 2, N])
        Y = two("Y", [P, NC, GW])
        dsk, wn = sb("dsk", [P, HS]), sb("wn", [P, DI])
        h = [sb("h_prompt", [P, GW]), sb("h_running", [P, GW])]
        st_out = two("st_out", [P, 2, N])
        xb = two("xb", [P, GW + N])
        xdt, xw, xd = two("xdt", [P, GW]), two("xw", [P, GW]), two("xd", [P, GW])
        L = two("L", [P, GH, P])
        M = two("M", [P, GH, P])
        t1 = two("t1", [P, GW])
        junk = sb("junk", [P, GW])
        ss = two("ss", [P, NC])
        sems = lambda n: [sem(f"{n}{b}") for b in range(2)]
        loaded, y_stored = sems("loaded"), sems("y_stored")
        par_loaded, st_stored, cleared = sem("par_loaded"), sem("st_stored"), sem("cleared")
        turned, xb_made, cb_made = sem("turned"), sem("xb_made"), sem("cb_made")
        L_in, L_made, M_made = sem("L_in"), sem("L_made"), sem("M_made")
        off_made, st_made, diag_made = sem("off_made"), sem("st_made"), sem("diag_made")
        x_scaled, gated, summed = sem("x_scaled"), sem("gated"), sem("summed")
        mean_made, rooted = sem("mean_made"), sem("rooted")
        in_turned, out_turned, st_copied, chain = sem("in_turned"), sem("out_turned"), sem("st_copied"), sem("vec_chain")
        block = ctx.enter_context(nc.Block())
        LOADS = 7
        STEPS = 2 + 5 * NC + 4
        H_AT = lambda c: 4 + 5 * c
        Y_READ = lambda c: H_AT(c) + 2
        Y_SUM = lambda c: H_AT(c) + 3
        spread = lambda x, n: x.rearrange("p (h o) -> p h o", o=1).to_broadcast([n, GH, HD])
        heads = lambda x: x.rearrange("p (h d) -> p h d", h=GH)

        @block.sync
        def _(sp):
            sp.dma_start(dsk[:], d_skip.to_broadcast([P, HS])).then_inc(par_loaded, 16)
            sp.dma_start(wn[:], norm_w.to_broadcast([P, DI])).then_inc(par_loaded, 16)

            def load(i, b):
                g = 2 * i + b
                cols = bass.ds(g * GW, GW)
                sp.dma_start(xT[b][:], xbc_d[cols, :].rearrange("(m p) t -> p m t", p=P)).then_inc(loaded[b], 16)
                sp.dma_start(BT[b][:], xbc_d[bass.ds(g * N + DI, N), :]).then_inc(loaded[b], 16)
                sp.dma_start(CT[b][:], xbc_d[bass.ds(g * N + DI + G * N, N), :]).then_inc(loaded[b], 16)
                sp.dma_start(z[b][:, 0:NT, :], z_d[0:TP, cols].rearrange("(t p) d -> p t d", p=P)).then_inc(loaded[b], 16)
                sp.dma_start(z[b][0:TS, NT, :], z_d[TP:T, cols]).then_inc(loaded[b], 16)
                sp.dma_start(ab[b][:], acum_d[:, bass.ds(g * GH, GH), :].to_broadcast([P, GH, T])).then_inc(loaded[b], 16)
                sp.dma_start(st_in[b][:], state_in[cols, :].rearrange("(m p) n -> p m n", p=P)).then_inc(loaded[b], 16)

            def store(i, b):
                g = 2 * i + b
                cols = bass.ds(g * GW, GW)
                core.hold(sp, st_copied, 2 * g + 2)
                sp.dma_start(ssm_prompt[cols, :].rearrange("(m p) n -> p m n", p=P), st_out[0][:]).then_inc(st_stored, 16)
                sp.dma_start(ssm_running[cols, :].rearrange("(m p) n -> p m n", p=P), st_out[1][:]).then_inc(st_stored, 16)
                core.hold(sp, chain, (g + 1) * STEPS)
                sp.dma_start(y_d[0:TP, cols].rearrange("(t p) d -> p t d", p=P), Y[b][:, 0:NT, :]).then_inc(y_stored[b], 16)
                sp.dma_start(y_d[TP:T, cols], Y[b][0:TS, NT, :]).then_inc(y_stored[b], 16)
            for b in range(2):
                sp.sem_inc(y_stored[b], 32)
            sp.sem_inc(st_stored, 32)
            load(0, 0)
            load(0, 1)

            def body(i, last):
                for b in range(2):
                    store(i, b)
                    if not last:
                        load(i + 1, b)
            loop(sp, G // 2, body)
            for b in range(2):
                sp.wait_ge(y_stored[b], 32 * (G // 2 + 1))
            sp.wait_ge(st_stored, 32 * (G + 1))

        @block.tensor
        def _(pe):
            pe.sem_inc(st_made, 2)
            pe.sem_inc(diag_made, 2)

            def turn(i, b, c):
                e, n, par = (2 * i + b) * NC + c, rows_of(c), (b * NC + c) % 2
                cols = slice(c * P, c * P + n)
                pe.wait_ge(xb_made, e + 1)
                nc.tensor.transpose(core.banks[0:n, par, 0:P], xT[b][:, 0, cols], core.ident[:])
                nc.tensor.transpose(core.banks[0:n, par, P:2 * P], xT[b][:, 1, cols], core.ident[:])
                nc.tensor.transpose(core.banks[0:n, par, 2 * P:3 * P], BT[b][:, cols], core.ident[:]).then_inc(turned, 1)
                pe.wait_ge(M_made, e + 1)
                nc.tensor.matmul(core.banks[0:n, 2 + par, 0:n], BT[b][:, cols], CT[b][:, cols], start=True, stop=True).then_inc(cb_made, 1)

            def body(i, last):
                for b in range(2):
                    g = 2 * i + b
                    pe.wait_ge(loaded[b], 16 * LOADS * (i + 1))
                    pe.wait_ge(chain, g * STEPS + 1)
                    for m in range(2):
                        ins = nc.tensor.transpose(core.banks[:, 4, m * P:(m + 1) * P], st_in[b][:, m, :], core.ident[:])
                    ins.then_inc(in_turned, 1)
                    turn(i, b, 0)
                    for c in range(NC):
                        e, n, par = g * NC + c, rows_of(c), (b * NC + c) % 2
                        cols = slice(c * P, c * P + n)
                        before = 2 if c in (0, NT) else H_AT(c - 1)
                        pe.wait_ge(chain, g * STEPS + max(before, Y_READ(c - 2) if c >= 2 else 0))
                        nc.tensor.matmul(core.banks[0:n, 4 + par, 0:GW], CT[b][:, cols], h[c == NT][:], start=True, stop=True).then_inc(off_made, 1)
                        pe.wait_ge(x_scaled, 3 * e + 9)
                        nc.tensor.matmul(core.banks[:, 4 + par, GW:2 * GW], xb[par][0:n, GW:GW + N], xw[par][0:n, :], start=True, stop=True).then_inc(st_made, 1)
                        if c + 1 < NC:
                            turn(i, b, c + 1)
                        core.hold(pe, M_made, e + 3)
                        for k in range(GH):
                            ins = nc.tensor.matmul(core.banks[0:n, 6 + par, k * HD:(k + 1) * HD], M[par][0:n, k, 0:n],
                                                   xdt[par][0:n, k * HD:(k + 1) * HD], start=True, stop=True)
                        ins.then_inc(diag_made, 1)
                    pe.wait_ge(chain, g * STEPS + Y_READ(NC - 1))
                    for s in range(2):
                        for m in range(2):
                            ins = nc.tensor.transpose(core.banks[:, 6 + s, m * P:(m + 1) * P], h[s][:, m * P:(m + 1) * P], core.ident[:])
                        ins.then_inc(out_turned, 1)
                    pe.wait_ge(st_copied, 2 * g + 2)
            loop(pe, G // 2, body)

        @block.scalar
        def _(act):
            act.sem_inc(xb_made, 2)
            act.sem_inc(summed, 1)
            act.wait_ge(cleared, 4)

            def square(i, b, c):
                e, n = (2 * i + b) * NC + c, rows_of(c)
                act.wait_ge(gated, e + 3)
                act.wait_ge(summed, e + 1)
                nc.scalar.activation(junk[0:n, :], Y[b][0:n, c, :], ACT.Square, accum_out=ss[b][0:n, c:c + 1]).then_inc(summed, 1)

            def body(i, last):
                for b in range(2):
                    g = 2 * i + b
                    for c in range(NC):
                        e, n, par = g * NC + c, rows_of(c), (b * NC + c) % 2
                        act.wait_ge(turned, e + 1)
                        act.wait_ge(st_made, e + 1)
                        act.wait_ge(x_scaled, 3 * e + 3)
                        nc.scalar.activation(xb[par][0:n, :], core.banks[0:n, par, 0:GW + N], ACT.Copy).then_inc(xb_made, 1)
                        act.wait_ge(L_in, e + 1)
                        nc.scalar.activation(L[par][0:n, :, 0:n], L[par][0:n, :, 0:n], ACT.Exp).then_inc(L_made, 1)
                        if c:
                            square(i, b, c - 1)
                    square(i, b, NC - 1)
                    act.wait_ge(st_stored, 32 * (g + 1))
                    for s in range(2):
                        act.wait_ge(out_turned, 2 * g + s + 2)
                        nc.scalar.activation(st_out[s][:], core.banks[:, 6 + s, 0:2 * P].rearrange("p (m n) -> p m n", m=2), ACT.Copy).then_inc(st_copied, 1)
                    act.wait_ge(mean_made, g + 1)
                    nc.scalar.activation(ss[b][:], ss[b][:], ACT.Sqrt).then_inc(rooted, 1)
            loop(act, G // 2, body)

        @block.gpsimd
        def _(pool):
            pool.sem_inc(x_scaled, 6)
            pool.sem_inc(gated, 2)
            core.hold(pool, par_loaded, 32)
            core.hold(pool, cleared, 4)

            def gate(i, b, c):
                e, n, par = (2 * i + b) * NC + c, rows_of(c), (b * NC + c) % 2
                core.hold(pool, chain, (2 * i + b) * STEPS + Y_SUM(c))
                nc.gpsimd.tensor_tensor(Y[b][0:n, c, :], t1[par][0:n, :], z[b][0:n, c, :], ALU.mult).then_inc(gated, 1)

            def body(i, last):
                for b in range(2):
                    g = 2 * i + b
                    gh = bass.ds(g * GH, GH)
                    core.hold(pool, loaded[b], 16 * LOADS * (i + 1))
                    core.hold(pool, y_stored[b], 32 * (i + 1))
                    for c in range(NC):
                        e, n, par = g * NC + c, rows_of(c), (b * NC + c) % 2
                        core.hold(pool, xb_made, e + 3)
                        x = heads(xb[par][0:n, 0:GW])
                        core.hold(pool, st_made, e + 1)
                        nc.gpsimd.tensor_tensor(heads(xw[par][0:n, :]), x, spread(w_tm[0:n, c, gh], n), ALU.mult).then_inc(x_scaled, 1)
                        core.hold(pool, diag_made, e + 1)
                        nc.gpsimd.tensor_tensor(heads(xdt[par][0:n, :]), x, spread(dt_tm[0:n, c, gh], n), ALU.mult).then_inc(x_scaled, 1)
                        core.hold(pool, chain, g * STEPS + (Y_SUM(c - 2) if c >= 2 else 1))
                        nc.gpsimd.tensor_tensor(heads(xd[par][0:n, :]), x, spread(dsk[0:n, gh], n), ALU.mult).then_inc(x_scaled, 1)
                        if c:
                            gate(i, b, c - 1)
                    gate(i, b, NC - 1)
            loop(pool, G // 2, body)

        @block.vector
        def _(dve):
            for b in range(2):
                nc.vector.memset(ss[b][:], 1.0).then_inc(cleared, 1)
                nc.vector.memset(Y[b][:, NT, :], 0.0).then_inc(cleared, 1)
            dve.sem_inc(M_made, 2)
            dve.sem_inc(out_turned, 1)
            dve.wait_ge(par_loaded, 32)
            nc.vector.tensor_scalar(wn[:], wn[:], 0.5, None, ALU.mult).then_inc(cleared, 1)
            dve.wait_ge(cleared, 5)

            def body(i, last):
                for b in range(2):
                    g = 2 * i + b
                    gh = bass.ds(g * GH, GH)
                    step = Chain(dve, chain)
                    step.enter(g, STEPS)

                    def y_sum(c):
                        e, n, par = g * NC + c, rows_of(c), (b * NC + c) % 2
                        dve.wait_ge(off_made, e + 1)
                        dve.wait_ge(gated, e + 1)
                        y = t1[par][0:n, :]
                        step(nc.vector.tensor_tensor(heads(y), heads(core.banks[0:n, 4 + par, 0:GW]), spread(ea_tm[0:n, c, gh], n), ALU.mult))
                        dve.wait_ge(diag_made, e + 3)
                        step(nc.vector.tensor_tensor(y, core.banks[0:n, 6 + par, 0:GW], y, ALU.add))
                        assert step.n == Y_READ(c)
                        dve.wait_ge(x_scaled, 3 * e + 9)
                        step(nc.vector.tensor_tensor(y, y, xd[par][0:n, :], ALU.add))

                    dve.wait_ge(loaded[b], 16 * LOADS * (i + 1))
                    dve.wait_ge(out_turned, 2 * g + 1)
                    step(nc.vector.memset(h[0][:], 0.0))
                    dve.wait_ge(in_turned, g + 1)
                    step(nc.vector.tensor_copy(h[1][:], core.banks[:, 4, 0:GW]))
                    for c in range(NC):
                        e, n, par = g * NC + c, rows_of(c), (b * NC + c) % 2
                        cols = slice(c * P, c * P + n)
                        dve.wait_ge(M_made, e + 1)
                        for k in range(GH):
                            ins = nc.vector.scalar_tensor_tensor(out=L[par][0:n, k, 0:n], in0=ab[b][0:n, k, cols],
                                                                 scalar=acum_tm[0:n, c, bass.ds(g * GH + k, 1)],
                                                                 in1=core.maskT[0:n, 0:n], op0=ALU.subtract, op1=ALU.add)
                        ins.then_inc(L_in, 1)
                        if c:
                            y_sum(c - 1)
                        hc = heads(h[c == NT][:])
                        dve.wait_ge(off_made, e + 1)
                        step(nc.vector.tensor_tensor(hc, hc, spread(cdec[:, gh, c], P), ALU.mult))
                        dve.wait_ge(st_made, e + 3)
                        step(nc.vector.tensor_tensor(hc, heads(core.banks[:, 4 + par, GW:2 * GW]), hc, ALU.add))
                        assert step.n == H_AT(c)
                        dve.wait_ge(L_made, e + 1)
                        dve.wait_ge(cb_made, e + 1)
                        dve.wait_ge(diag_made, e + 1)
                        nc.vector.tensor_tensor(M[par][0:n, :, 0:n], L[par][0:n, :, 0:n],
                                                core.banks[0:n, 2 + par, 0:n].rearrange("p (o l) -> p o l", o=1).to_broadcast([n, GH, n]),
                                                ALU.mult).then_inc(M_made, 1)
                    y_sum(NC - 1)
                    dve.wait_ge(summed, (g + 1) * NC + 1)
                    step(nc.vector.tensor_scalar(ss[b][:], ss[b][:], 0.25 / GW, EPS, ALU.mult, ALU.add))
                    dve.sem_inc(mean_made, 1)
                    dve.wait_ge(rooted, g + 1)
                    step(nc.vector.reciprocal(ss[b][:], ss[b][:]))
                    step(nc.vector.tensor_tensor(Y[b][:], Y[b][:], ss[b][:].rearrange("p (c o) -> p c o", o=1).to_broadcast([P, NC, GW]), ALU.mult))
                    step(nc.vector.tensor_tensor(Y[b][:], Y[b][:], wn[:, bass.ds(g * GW, GW)].rearrange("p (o d) -> p o d", o=1).to_broadcast([P, NC, GW]), ALU.mult))
                    step.leave()
            loop(dve, G // 2, body)


def hybrid_layer(nc, I, O):
    scratch = lambda n, s: nc.dram_tensor(f"scratch_{n}", s, F32, kind="Internal").ap()
    q_d, att_d = scratch("q", [T, D]), scratch("att", [T, D])
    z_d, y_d = scratch("z", [T, DI]), scratch("y", [T, DI])
    xbc_d = scratch("xbc", [CD, T])
    ga_d, gs_d = scratch("gate_att", [D, T]), scratch("gate_ssm", [D, T])
    x2_d = scratch("x2", [T, D])
    aug_q, aug_k = scratch("aug_q", [H, 2, KEYS]), scratch("aug_k", [H, 2, KEYS])
    acum_d = scratch("acum", [1, HS, T])

    x_p, x_s = I["x_prompt"][0], I["x_sample"][0]
    w_in = I["w_in"][0]
    flat = lambda a: a[0, 0].rearrange("t h d -> t (h d)")
    row = lambda a: a
    columns = lambda w, c0, rows, width: (lambda p: w[rows, bass.ds(p * width + c0, width)])
    every = slice(0, D)
    with ExitStack() as ctx:
        core = Core(nc, ctx)
        constants(core)
        with ExitStack() as keep_ctx:
            keep = [keep_ctx.enter_context(nc.sbuf_tensor(f"keep_{n}", s, F32)) for n, s in
                    (("dt", [P, NT + 1, HS]), ("acum", [P, NT + 1, HS]), ("w", [P, NT + 1, HS]), ("ea", [P, NT + 1, HS]), ("cdec", [P, HS, NT + 1]))]
            with ExitStack() as x_ctx:
                hi = x_ctx.enter_context(nc.sbuf_tensor("xn_hi", [P, KB, TW], F32R))
                lo = x_ctx.enter_context(nc.sbuf_tensor("xn_lo", [P, KB, TW], F32R))
                transpose_split(core, "norm1", (x_p, x_s), hi, lo, I["norm1_w"])
                decays(core, hi, lo, w_in, I["b_f"][0], I["dt_bias"][0], I["A_log"][0], I["cache_logf"][0, 0],
                       O["logf_prompt"][0, 0], O["logf_sample"][0, 0], aug_q, aug_k, acum_d[0], keep)
                gemm(core, "q", hi, lo, columns(w_in, C_Q, every, PW), 2, KB, PW, True,
                     head_norm_tm(core, I["q_norm_w"], q_d[0:TP, :], q_d[TP:T, :]))
                gemm(core, "k", hi, lo, columns(w_in, C_K, every, PW), 2, KB, PW, True,
                     head_norm_tm(core, I["k_norm_w"], flat(O["k_prompt"]), flat(O["k_sample"])))
                gemm(core, "v", hi, lo, columns(w_in, C_V, every, PW), 2, KB, PW, True,
                     pointwise_tm(core, ACT.Copy, flat(O["v_prompt"]), flat(O["v_sample"])))
                gemm(core, "ga", hi, lo, columns(w_in, C_GA, every, PW), 2, KB, PW, False, sigmoid_fm(core, ga_d))
                gemm(core, "gs", hi, lo, columns(w_in, C_GA + D, every, PW), 2, KB, PW, False, sigmoid_fm(core, gs_d))
                attention_z_xbc(core, hi, lo, w_in, z_d, xbc_d,
                                dict(params=(I["conv_w"][0], I["conv_b"][0], I["state_conv"][0, 0]),
                                     tails=(O["conv_prompt"][0, 0], O["conv_sample"][0, 0])),
                                q_d, flat(O["k_prompt"]), flat(O["k_sample"]), flat(O["v_prompt"]), flat(O["v_sample"]),
                                flat(I["cache_k"]), flat(I["cache_v"]), aug_q, aug_k, att_d)
            state = lambda a: a[0, 0].rearrange("h p n -> (h p) n")
            ssd(core, xbc_d, z_d, y_d, acum_d, state(I["state_ssm"]), I["D_skip"], I["ssm_norm_w"],
                state(O["ssm_prompt"]), state(O["ssm_sample"]), keep)
        with ExitStack() as m_ctx:
            merged = m_ctx.enter_context(nc.sbuf_tensor("merged", [P, KB, T], F32))
            with ExitStack() as a_ctx:
                hi = a_ctx.enter_context(nc.sbuf_tensor("branch_hi", [P, KB, T], F32R))
                lo = a_ctx.enter_context(nc.sbuf_tensor("branch_lo", [P, KB, T], F32R))
                transpose_split(core, "att_t", (att_d[0:TP, :], att_d[TP:T, :]), hi, lo)
                gemm(core, "pa", hi, lo, columns(I["w_pa"][0], 0, every, PW), 2, KB, PW, False, gated_fm(core, ga_d, merged, None, False))
                transpose_split(core, "y_t0", (y_d[0:TP, 0:D], y_d[TP:T, 0:D]), hi, lo)
                part = a_ctx.enter_context(nc.sbuf_tensor("pb_part", [P, KB, T], F32))
                gemm(core, "pb0", hi, lo, columns(I["w_pb"][0], 0, every, PW), 2, KB, PW, False, kept_fm(core, part))
                transpose_split(core, "y_t1", (y_d[0:TP, D:DI], y_d[TP:T, D:DI]), hi, lo)
                gemm(core, "pb1", hi, lo, columns(I["w_pb"][0], 0, slice(D, DI), PW), 2, KB, PW, False, gated_fm(core, gs_d, merged, part, True))
            with ExitStack() as o_ctx:
                hi = o_ctx.enter_context(nc.sbuf_tensor("merged_hi", [P, KB, TW], F32R))
                lo = o_ctx.enter_context(nc.sbuf_tensor("merged_lo", [P, KB, TW], F32R))
                split_fm(core, merged, hi, lo)
                gemm(core, "out", hi, lo, columns(I["w_out"][0], 0, every, PW), 2, KB, PW, True,
                     residual_tm(core, x_p, x_s, x2_d[0:TP, :], x2_d[TP:T, :]))
        with ExitStack() as f_ctx:
            hi = f_ctx.enter_context(nc.sbuf_tensor("h_hi", [P, KB, T], F32R))
            lo = f_ctx.enter_context(nc.sbuf_tensor("h_lo", [P, KB, T], F32R))
            transpose_split(core, "norm2", (x2_d[0:TP, :], x2_d[TP:T, :]), hi, lo, I["norm2_w"])
            mlp(core, hi, lo, I["w_up"][0], I["w_down"][0], x2_d[0:TP, :], x2_d[TP:T, :], O["y_prompt"][0], O["y_sample"][0])


_INS = ["x_prompt", "x_sample", "cache_k", "cache_v", "cache_logf", "state_conv", "state_ssm", "norm1_w", "w_in", "b_f",
        "q_norm_w", "k_norm_w", "conv_w", "conv_b", "dt_bias", "A_log", "D_skip", "ssm_norm_w", "w_pa", "w_pb", "w_out",
        "norm2_w", "w_up", "w_down"]
_OUTS = [("y_prompt", (1, TP, D)), ("y_sample", (1, TS, D)),
         ("k_prompt", (1, 1, TP, H, HD)), ("v_prompt", (1, 1, TP, H, HD)), ("logf_prompt", (1, 1, TP, H)),
         ("conv_prompt", (1, 1, CW - 1, CD)), ("ssm_prompt", (1, 1, HS, HD, N)),
         ("k_sample", (1, 1, TS, H, HD)), ("v_sample", (1, 1, TS, H, HD)), ("logf_sample", (1, 1, TS, H)),
         ("conv_sample", (1, 1, CW - 1, CD)), ("ssm_sample", (1, 1, HS, HD, N))]


def kernel(**inputs):
    import concourse.bacc as bacc
    from concourse.bass_utils import run_bass_kernel_spmd

    nc = bacc.Bacc("TRN2", target_bir_lowering=False, num_devices=1)
    arrays = {f"in_{n}": np.ascontiguousarray(inputs[n]) for n in _INS}
    I = {n: nc.dram_tensor(f"in_{n}", arrays[f"in_{n}"].shape, F32, kind="ExternalInput").ap() for n in _INS}
    O = {n: nc.dram_tensor(f"out_{n}", s, F32, kind="ExternalOutput").ap() for n, s in _OUTS}
    hybrid_layer(nc, I, O)
    r = run_bass_kernel_spmd(nc, [arrays], core_ids=[0])
    return tuple(r.results[0][f"out_{n}"] for n, _ in _OUTS)
```

```python
from contextlib import ExitStack

import numpy as np
import concourse.bass as bass
from concourse import mybir

F32 = mybir.dt.float32
F32R = mybir.dt.float32r
BF16 = mybir.dt.bfloat16
ALU = mybir.AluOpType
ACT = mybir.ActivationFunctionType
AX = mybir.AxisListType

P = 128
D = 1024
KB = D // P
TP = 1024
TS = 32
PAST = 256
T = TP + TS
NT = TP // P
TW = (NT + 1) * P
TT = T // 3
H = 16
HD = 64
DI = 2048
HS = 32
G = 8
N = 128
GH = HS // G
GW = DI // G
CW = 4
CD = DI + 2 * G * N
FF = 4 * D
KEYS = TP + PAST + TS
FS = 512
EPS = 1e-6
NEG = -1e30
C_Q, C_K, C_V, C_F = 0, D, 2 * D, 3 * D
C_Z = C_F + H
C_X = C_Z + DI
C_B = C_X + DI
C_C = C_B + G * N
C_DT = C_X + CD
C_GA = C_DT + HS
DPROJ = C_GA + 2 * D
PW = 256


class Chain:

    def __init__(self, eng, sem):
        self.eng, self.sem, self.base, self.n = eng, sem, 0, 0

    def __call__(self, ins):
        ins.then_inc(self.sem, 1)
        self.n += 1
        self.eng.wait_ge(self.sem, self.base + self.n)

    def enter(self, i, per):
        self.base, self.n, self.per = i * per, 0, per

    def leave(self):
        assert self.n == self.per, (self.n, self.per)


class Core:

    def __init__(self, nc, ctx):
        self.nc, self.ctx = nc, ctx
        self.banks = ctx.enter_context(nc.psum_tensor("banks", [P, 8, 512], F32))
        self.ident = ctx.enter_context(nc.sbuf_tensor("ident", [P, P], F32))
        self.identb = ctx.enter_context(nc.sbuf_tensor("identb", [P, P], BF16))
        self.maskb = ctx.enter_context(nc.sbuf_tensor("maskb", [P, P], BF16))
        self.maskT = ctx.enter_context(nc.sbuf_tensor("maskT", [P, P], F32))
        self.raw = ctx.enter_context(nc.sbuf_tensor("w_raw", [P, KB * PW], F32))
        self.whi = [ctx.enter_context(nc.sbuf_tensor(f"w_hi{b}", [P, KB * PW], F32R)) for b in range(2)]
        self.wlo = [ctx.enter_context(nc.sbuf_tensor(f"w_lo{b}", [P, KB * PW], F32R)) for b in range(2)]
        self.passed = ctx.enter_context(nc.semaphore("passed"))

    def semaphores(self, ctx, tag):
        held = []

        def clear():
            self.nc.clear_and_free_semaphores(held)
            self.nc.all_engine_barrier()
        ctx.callback(clear)

        def new(name):
            held.append(self.nc.alloc_semaphore(f"{tag}_{name}"))
            return held[-1]
        return new

    def hold(self, eng, sem, value):
        eng.wait_ge(sem, value)
        eng.sem_inc(self.passed, 1)


def loop(eng, count, body):
    if count > 1:
        with eng.Fori(0, count - 1) as i:
            body(i, False)
    body(count - 1, True)


def constants(core):
    nc = core.nc
    with ExitStack() as ctx:
        made = core.semaphores(ctx, "const")("made")
        block = ctx.enter_context(nc.Block())

        @block.gpsimd
        def _(pool):
            nc.gpsimd.memset(core.ident[:], 0.0).then_inc(made, 1)
            nc.gpsimd.memset(core.maskT[:], 0.0).then_inc(made, 1)
            nc.gpsimd.memset(core.maskb[:], 0.0).then_inc(made, 1)
            pool.wait_ge(made, 3)
            nc.gpsimd.affine_select(out=core.ident[:], in_=core.ident[:], compare_op=ALU.not_equal, fill=1.0,
                                    base=0, pattern=[[-1, P]], channel_multiplier=1).then_inc(made, 1)
            nc.gpsimd.affine_select(out=core.maskT[:], in_=core.maskT[:], compare_op=ALU.is_ge, fill=NEG,
                                    base=0, pattern=[[1, P]], channel_multiplier=-1).then_inc(made, 1)
            nc.gpsimd.affine_select(out=core.maskb[:], in_=core.maskb[:], compare_op=ALU.is_ge, fill=NEG,
                                    base=0, pattern=[[-1, P]], channel_multiplier=1).then_inc(made, 1)
            pool.wait_ge(made, 6)
            nc.gpsimd.tensor_copy(core.identb[:], core.ident[:]).then_inc(made, 1)


def norm_split(core, tag, srcs, hi, lo, norm_w, following):
    nc = core.nc
    AHEAD = 2
    with ExitStack() as ctx:
        sb = lambda n, s, dt=F32: ctx.enter_context(nc.sbuf_tensor(f"{tag}_{n}", s, dt))
        sem = core.semaphores(ctx, f"{tag}")
        rows = sb("rows", [P, NT + 1, D])
        junk = sb("junk", [P, D])
        ss = sb("ss", [P, NT + 1])
        wb = sb("wb", [P, D])
        loaded = [sem(f"loaded{t}") for t in range(NT + 1)]
        w_loaded, summed, rooted, scaled = sem("w_loaded"), sem("summed"), sem("rooted"), sem("scaled")
        turned, hi_made, lo_made, padded = sem("turned"), sem("hi_made"), sem("lo_made"), sem("padded")
        mean_made, inverted, p_loaded, p_split = sem("mean_made"), sem("inverted"), sem("panel_loaded"), sem("panel_split")
        block = ctx.enter_context(nc.Block())

        def half_tiles(t):
            n = rows_of(t)
            return [(2 * t + half, slice(4 * half, 4 * half + 4),
                     core.banks[:, (2 * t + half) % 4, 0:4 * n].rearrange("p (k n) -> p k n", k=4)) for half in range(2)]

        @block.sync
        def _(sp):
            sp.dma_start(rows[:, 0, :], srcs[0][0:P, :]).then_inc(loaded[0], 16)
            sp.dma_start(wb[:], norm_w.to_broadcast([P, D])).then_inc(w_loaded, 16)
            for t in range(1, NT):
                sp.dma_start(rows[:, t, :], srcs[0][t * P:(t + 1) * P, :]).then_inc(loaded[t], 16)
            sp.dma_start(rows[0:TS, NT, :], srcs[1]).then_inc(loaded[NT], 16)
            sp.dma_start(core.raw[:].rearrange("p (k m) -> p k m", k=KB), following.rearrange("(k p) m -> p k m", p=P)).then_inc(p_loaded, 16)

        @block.scalar
        def _(act):
            for t in range(NT + 1 + 2 * AHEAD):
                if t == NT + 1:
                    act.wait_ge(p_loaded, 16)
                    nc.scalar.activation(core.whi[0][:], core.raw[:], ACT.Copy).then_inc(p_split, 1)
                if t <= NT:
                    n = rows_of(t)
                    act.wait_ge(loaded[t], 16)
                    if t:
                        act.wait_ge(summed, t)
                    nc.scalar.activation(junk[0:n, :], rows[0:n, t, :], ACT.Square, accum_out=ss[0:n, t:t + 1]).then_inc(summed, 1)
                if 0 <= t - AHEAD <= NT:
                    r = t - AHEAD
                    n = rows_of(r)
                    act.wait_ge(mean_made, r + 1)
                    nc.scalar.activation(ss[0:n, r:r + 1], ss[0:n, r:r + 1], ACT.Sqrt).then_inc(rooted, 1)
                s = t - 2 * AHEAD
                if s >= 0:
                    for i, blocks, bank in half_tiles(s):
                        act.wait_ge(turned, i + 1)
                        nc.scalar.activation(hi[:, blocks, s * P:s * P + rows_of(s)], bank, ACT.Copy).then_inc(hi_made, 1)

        @block.vector
        def _(dve):
            nc.vector.memset(hi[:, :, T:TW].bitcast(F32), 0.0).then_inc(padded, 1)
            nc.vector.memset(lo[:, :, T:TW].bitcast(F32), 0.0).then_inc(padded, 1)

            def mean(t):
                n = rows_of(t)
                dve.wait_ge(summed, t + 1)
                nc.vector.tensor_scalar(ss[0:n, t:t + 1], ss[0:n, t:t + 1], 1.0 / D, EPS, ALU.mult, ALU.add).then_inc(mean_made, 1)

            def scale(t):
                n = rows_of(t)
                dve.wait_ge(rooted, t + 1)
                nc.vector.reciprocal(ss[0:n, t:t + 1], ss[0:n, t:t + 1]).then_inc(inverted, 1)
                dve.wait_ge(inverted, t + 1)
                nc.vector.scalar_tensor_tensor(out=rows[0:n, t, :], in0=rows[0:n, t, :], scalar=ss[0:n, t:t + 1], in1=wb[0:n, :],
                                               op0=ALU.mult, op1=ALU.mult).then_inc(scaled, 1)
            dve.wait_ge(w_loaded, 16)
            for t in range(NT + 1 + 2 * AHEAD):
                if t <= NT:
                    mean(t)
                if 0 <= t - AHEAD <= NT:
                    scale(t - AHEAD)
                s = t - 2 * AHEAD
                if s >= 0:
                    for i, blocks, bank in half_tiles(s):
                        dve.wait_ge(hi_made, i + 1)
                        cols = slice(s * P, s * P + rows_of(s))
                        nc.vector.tensor_tensor(lo[:, blocks, cols], bank, hi[:, blocks, cols].bitcast(F32), ALU.subtract).then_inc(lo_made, 1)
            dve.wait_ge(p_split, 1)
            nc.vector.tensor_tensor(core.wlo[0][:], core.raw[:], core.whi[0][:].bitcast(F32), ALU.subtract).then_inc(p_split, 1)

        @block.tensor
        def _(pe):
            for t in range(NT + 1):
                n = rows_of(t)
                pe.wait_ge(scaled, t + 1)
                for half in range(2):
                    i = 2 * t + half
                    if i >= 4:
                        pe.wait_ge(lo_made, i - 3)
                    for k in range(4):
                        kb = 4 * half + k
                        last = nc.tensor.transpose(core.banks[:, i % 4, k * n:(k + 1) * n],
                                                   rows[0:n, t, kb * P:(kb + 1) * P], core.ident[0:n, 0:n])
                    last.then_inc(turned, 1)


class Stream:

    def __init__(self, core, tag, sb, sem, hi, lo, panels, rounds, banks, following):
        self.core, self.nc, self.rounds, self.banks = core, core.nc, rounds, banks
        self.panels, self.following = panels, following
        view = lambda x: x[:].rearrange("p (k m) -> p k m", k=KB)
        self.raw, self.whi, self.wlo = view(core.raw), [view(x) for x in core.whi], [view(x) for x in core.wlo]
        self.raw_loaded = sem(f"{tag}_raw_loaded")
        self.hi_made, self.lo_made = sem(f"{tag}_whi_made"), sem(f"{tag}_wlo_made")
        self.full, self.free = sem(f"{tag}_bank_full"), sem(f"{tag}_bank_free")
        self.tiles = [(j, t) for j, p in enumerate(panels) for t in range(NT + 1 if p[0] else 6)]
        self.slots = len(self.tiles)
        self.ends = [sum(1 for jj, _ in self.tiles if jj < j) for j in range(len(panels) + 1)]
        assert self.slots % len(banks) == 0 and len(panels) % 2 == 0
        self.hi, self.lo = hi, lo
        self.by_range = False

    def mine(self, ep, n):
        if not 0 <= n < self.slots:
            return []
        j, t = self.tiles[n]
        return [(self.panels[j][3], t)] if self.panels[j][2] is ep else []

    def bank(self, n, rows, cols):
        return self.core.banks[0:rows, self.banks[n % len(self.banks)], 0:cols]

    def wait_full(self, eng, i, n):
        eng.wait_ge(self.full, i * self.slots + n + 1)

    def wait_free(self, eng, i, n):
        eng.wait_ge(self.free, len(self.banks) + i * self.slots + n + 1)

    def epilogues(self):
        return list(dict.fromkeys(p[2] for p in self.panels))

    def load(self, sp, i, j, last=False):
        np_ = len(self.panels)
        if last and j > np_:
            return
        self.core.hold(sp, self.lo_made, 4 * (i * np_ + j))
        src = self.following if last and j == np_ else self.panels[j % np_][1](i + j // np_)
        sp.dma_start(self.raw, src.rearrange("(k p) m -> p k m", p=P)).then_inc(self.raw_loaded, 16)

    def split_hi(self, act, i, j, c):
        q = slice(c * KB // 4, (c + 1) * KB // 4)
        if c == 0:
            np_ = len(self.panels)
            act.wait_ge(self.raw_loaded, 16 * (i * np_ + j))
            if not (isinstance(i, int) and i * np_ + j < 2):
                act.wait_ge(self.full, i * self.slots + self.ends[j - 1])
        self.nc.scalar.activation(self.whi[j % 2][:, q, :], self.raw[:, q, :], ACT.Copy).then_inc(self.hi_made, 1)

    def split_lo(self, dve, i, j, c):
        q = slice(c * KB // 4, (c + 1) * KB // 4)
        dve.wait_ge(self.hi_made, 4 * (i * len(self.panels) + j) + c + 1)
        self.nc.vector.tensor_tensor(self.wlo[j % 2][:, q, :], self.raw[:, q, :],
                                     self.whi[j % 2][:, q, :].bitcast(F32), ALU.subtract).then_inc(self.lo_made, 1)

    def start_sp(self, sp):
        for ep in self.epilogues():
            ep.start_sp(sp)
        self.load(sp, 0, 1)

    def start_act(self, act):
        act.sem_inc(self.hi_made, 4)
        act.sem_inc(self.free, len(self.banks))
        for ep in self.epilogues():
            ep.start_act(act)

    def start_dve(self, dve):
        dve.sem_inc(self.lo_made, 4)
        for ep in self.epilogues():
            ep.start_dve(dve)

    def sp(self, sp, i, n, last):
        j, t = self.tiles[n]
        if t == 5:
            self.load(sp, i, j + 2, last)
        for ep in self.epilogues():
            ep.sp(sp, i, n)

    def act(self, act, i, n, last):
        j, t = self.tiles[n]
        for ep in self.epilogues():
            ep.act(act, i, n)
        if t < 4:
            self.split_hi(act, i, j + 1, t)

    def dve(self, dve, i, n, last):
        j, t = self.tiles[n]
        if 1 <= t < 5:
            self.split_lo(dve, i, j + 1, t - 1)
        for ep in self.epilogues():
            ep.dve(dve, i, n)

    def pe(self, pe, i, n):
        j, t = self.tiles[n]
        if t == 0:
            pe.wait_ge(self.lo_made, 4 * (i * len(self.panels) + j + 1))
        pe.wait_ge(self.free, i * self.slots + n + 1)
        wh, wl = self.whi[j % 2], self.wlo[j % 2]
        passes = [(x, w, k) for k in range(KB) for x, w in ((self.hi, wh), (self.hi, wl), (self.lo, wh))]
        for c, (x, w, k) in enumerate(passes):
            first, end = c == 0, c == len(passes) - 1
            if self.panels[j][0]:
                ins = self.nc.tensor.matmul(self.bank(n, P, PW), x[:, k, t * P:(t + 1) * P], w[:, k, :], start=first, stop=end)
            else:
                m, r = (t % 2, t // 2) if self.by_range else (t // 3, t % 3)
                ins = self.nc.tensor.matmul(self.bank(n, P, TT), w[:, k, m * P:(m + 1) * P], x[:, k, r * TT:(r + 1) * TT],
                                            start=first, stop=end)
        ins.then_inc(self.full, 1)


class CopyTm:

    def __init__(self, sb, sem, name, per, to_prompt, to_running):
        self.per, self.to = per, (to_prompt, to_running)
        self.stage = sb(f"{name}_stage", [P, NT + 1, PW])
        self.stored = sem(f"{name}_stored")

    def start_sp(self, sp):
        sp.sem_inc(self.stored, 32)

    def start_act(self, act):
        pass

    def start_dve(self, dve):
        pass

    def act(self, act, i, n):
        s = self.stream
        for k, t in s.mine(self, n):
            if t == 0:
                act.wait_ge(self.stored, 32 * (i * self.per + k + 1))
            s.wait_full(act, i, n)
            s.nc.scalar.activation(self.stage[0:rows_of(t), t, :], s.bank(n, rows_of(t), PW), ACT.Copy).then_inc(s.free, 1)

    def dve(self, dve, i, n):
        pass

    def sp(self, sp, i, n):
        s = self.stream
        for k, t in s.mine(self, n):
            if t == NT:
                s.core.hold(sp, s.free, len(s.banks) + i * s.slots + n + 1)
                cols = bass.ds((i * self.per + k) * PW, PW)
                sp.dma_start(self.to[0][:, cols].rearrange("(t p) d -> p t d", p=P), self.stage[:, 0:NT, :]).then_inc(self.stored, 16)
                sp.dma_start(self.to[1][:, cols], self.stage[0:TS, NT, :]).then_inc(self.stored, 16)

    def finish(self, sp):
        sp.wait_ge(self.stored, 32 * (self.stream.rounds * self.per + 1))


class HeadNormTm:
    HEADS = PW // HD

    def __init__(self, sb, sem, per, weights, to):
        self.per, self.weights, self.to = per, weights, to
        self.stage = [sb(f"norm_stage{x}", [P, NT + 1, PW]) for x in range(2)]
        self.sq, self.ss = sb("sq", [P, NT + 1, PW]), sb("ss", [P, (NT + 1) * self.HEADS])
        self.w = [sb(f"norm_w{x}", [P, HD]) for x in range(2)]
        self.w_loaded, self.cleared, self.copied = sem("w_loaded"), sem("cleared"), sem("copied")
        self.meaned, self.rooted, self.scaled = sem("meaned"), sem("rooted"), sem("scaled")
        self.stored = [sem(f"norm_stored{x}") for x in range(2)]

    def ended(self, n):
        return [k for k, t in self.stream.mine(self, n) if t == NT]

    def start_sp(self, sp):
        for x in range(2):
            sp.dma_start(self.w[x][:], self.weights[x].to_broadcast([P, HD])).then_inc(self.w_loaded, 16)
            sp.sem_inc(self.stored[x], 32)

    def start_act(self, act):
        act.wait_ge(self.cleared, 3)

    def start_dve(self, dve):
        for a in (*self.stage, self.sq):
            self.stream.nc.vector.memset(a[:, NT, :], 0.0).then_inc(self.cleared, 1)
        dve.sem_inc(self.meaned, 2)
        dve.wait_ge(self.w_loaded, 32)

    def act(self, act, i, n):
        s = self.stream
        for k in self.ended(n - 2):
            q = i * self.per + k
            act.wait_ge(self.meaned, 2 * q + 4)
            s.nc.scalar.activation(self.ss[:], self.ss[:], ACT.Sqrt).then_inc(self.rooted, 1)
        for k, t in s.mine(self, n):
            q, m, x = i * self.per + k, rows_of(t), k % 2
            if t == 0:
                act.wait_ge(self.stored[x], 32 * (i * (self.per // 2) + k // 2 + 1))
                act.wait_ge(self.meaned, 2 * q + 2)
            s.wait_full(act, i, n)
            s.nc.scalar.activation(self.stage[x][0:m, t, :], s.bank(n, m, PW), ACT.Copy).then_inc(self.copied, 1)
            s.nc.scalar.activation(self.sq[0:m, t, :], s.bank(n, m, PW), ACT.Square).then_inc(s.free, 1)

    def dve(self, dve, i, n):
        s = self.stream
        v = s.nc.vector
        every = [P, (NT + 1) * self.HEADS, HD]
        for k in self.ended(n - 1):
            q = i * self.per + k
            s.wait_free(dve, i, n - 1)
            v.tensor_reduce(self.ss[:], self.sq[:].rearrange("p t (h d) -> p (t h) d", d=HD), AX.X, ALU.add).then_inc(self.meaned, 1)
            dve.wait_ge(self.meaned, 2 * q + 3)
            v.tensor_scalar(self.ss[:], self.ss[:], 1.0 / HD, EPS, ALU.mult, ALU.add).then_inc(self.meaned, 1)
        for k in self.ended(n - 2):
            q, stage = i * self.per + k, self.stage[k % 2][:].rearrange("p t (h d) -> p (t h) d", d=HD)
            dve.wait_ge(self.rooted, q + 1)
            dve.wait_ge(self.copied, (q + 1) * (NT + 1))
            v.reciprocal(self.ss[:], self.ss[:]).then_inc(self.scaled, 1)
            dve.wait_ge(self.scaled, 3 * q + 1)
            v.tensor_tensor(stage, stage, self.ss[:, :, None].to_broadcast(every), ALU.mult).then_inc(self.scaled, 1)
        for k in self.ended(n - 3):
            q, stage = i * self.per + k, self.stage[k % 2][:].rearrange("p t (h d) -> p (t h) d", d=HD)
            dve.wait_ge(self.scaled, 3 * q + 2)
            v.tensor_tensor(stage, stage, self.w[k % 2][:, None, :].to_broadcast(every), ALU.mult).then_inc(self.scaled, 1)

    def sp(self, sp, i, n):
        s = self.stream
        for k in self.ended(n - 4):
            q, x = i * self.per + k, k % 2
            s.core.hold(sp, self.scaled, 3 * q + 3)
            cols = bass.ds((i * (self.per // 2) + k // 2) * PW, PW)
            sp.dma_start(self.to[x][0][:, cols].rearrange("(t p) d -> p t d", p=P), self.stage[x][:, 0:NT, :]).then_inc(self.stored[x], 16)
            sp.dma_start(self.to[x][1][:, cols], self.stage[x][0:TS, NT, :]).then_inc(self.stored[x], 16)

    def finish(self, sp):
        for x in range(2):
            sp.wait_ge(self.stored[x], 32 * (self.stream.rounds * (self.per // 2) + 1))


class Decays:
    FR, DR = slice(0, H), slice(32, 32 + HS)
    R = 64
    TURNS = 17

    def __init__(self, core, sb, sem, hi, lo, w_in, b_f, dt_bias, a_log, cache_logf, logf_to, aug_q, aug_k, acum_d, keep):
        self.core, self.nc, self.hi, self.lo = core, core.nc, hi, lo
        self.srcs, self.logf_to, self.aug, self.acum_d, self.keep = (w_in, b_f, dt_bias, a_log, cache_logf), logf_to, (aug_q, aug_k), acum_d, keep
        R = self.R
        self.w, self.whi, self.wlo = sb("dec_w", [P, KB, P]), sb("dec_whi", [P, KB, P], F32R), sb("dec_wlo", [P, KB, P], F32R)
        self.bias, self.A = sb("bias", [R, 1]), sb("A", [R, 1])
        self.v, self.e, self.u, self.c, self.both = (sb(f"dec_{n}", [R, T]) for n in ("v", "e", "u", "c", "both"))
        log_u = sb("dec_l", [R, KEYS])
        self.l, self.keys_logf = log_u[:, 0:T], log_u[0:H, :]
        self.acum = self.u
        self.past = sb("past", [P, 2, H])
        self.keys_sum, self.keys_one = (sb(f"keys_{n}", [H, KEYS]) for n in ("sum", "one"))
        self.ones = sb("ones", [R, P])
        self.logf_tm = sb("logf_tm", [P, NT + 1, H])
        self.last, self.diag = sb("last", [R, NT + 1]), sb("diag", [R, HS, NT + 1])
        self.loaded, self.zeroed, self.chain, self.act_chain = sem("dec_loaded"), sem("dec_zeroed"), sem("dec_vec_chain"), sem("dec_act_chain")
        self.full, self.turned, self.out = sem("dec_full"), sem("dec_turned"), sem("dec_out")
        self.at = {}

    def start_sp(self, sp):
        nc, FR, DR = self.nc, self.FR, self.DR
        w_in, b_f, dt_bias, a_log, cache_logf = self.srcs
        w = self.w
        sp.wait_ge(self.zeroed, 3)
        sp.dma_start(w[:, :, FR], w_in[:, C_F:C_F + H].rearrange("(k p) m -> p k m", p=P)).then_inc(self.loaded, 16)
        sp.dma_start(w[:, :, DR], w_in[:, C_DT:C_DT + HS].rearrange("(k p) m -> p k m", p=P)).then_inc(self.loaded, 16)
        with nc.allow_non_contiguous_dma(reason="one value per head"):
            sp.dma_start(self.bias[FR, :], b_f.rearrange("(h o) -> h o", o=1)).then_inc(self.loaded, 16)
            sp.dma_start(self.bias[DR, :], dt_bias.rearrange("(h o) -> h o", o=1)).then_inc(self.loaded, 16)
            sp.dma_start(self.A[DR, :], a_log.rearrange("(h o) -> h o", o=1)).then_inc(self.loaded, 16)
        sp.dma_start(self.past[:], cache_logf.rearrange("(t p) h -> p t h", p=P)).then_inc(self.loaded, 16)

    def start_dve(self, dve):
        memset = self.nc.vector.memset
        dt_tm, acum_tm = self.keep[0], self.keep[1]
        for m, x in ((self.w[:], 0.0), (self.bias[:], 0.0), (self.A[:], 0.0), (self.ones[:], 1.0), (self.keys_one[:], 1.0),
                     (dt_tm[:], 0.0), (acum_tm[:], 0.0), (self.logf_tm[:], 0.0)):
            memset(m, x).then_inc(self.zeroed, 1)

    def dve(self, dve, n):
        nc, FR, DR, core = self.nc, self.FR, self.DR, self.core
        v, e, u, l, c, both, acum, at = self.v, self.e, self.u, self.l, self.c, self.both, self.acum, self.at
        dt_tm, acum_tm, w_tm, ea_tm, cdec = self.keep
        if n == 0:
            self.step = Chain(dve, self.chain)
        step = self.step
        if n == 2:
            dve.wait_ge(self.zeroed, 8)
            dve.wait_ge(self.act_chain, 1)
            step(nc.vector.tensor_tensor(self.wlo[:], self.w[:], self.whi[:].bitcast(F32), ALU.subtract))
            at["split"] = step.n
        elif n == 8:
            dve.wait_ge(self.act_chain, 6)
            step(nc.vector.tensor_scalar(u[:], e[:], 1.0, None, ALU.add))
            at["u"] = step.n
            step(nc.vector.tensor_scalar(c[:], u[:], -1.0, None, ALU.add))
        elif n == 9:
            step(nc.vector.tensor_tensor(c[:], e[:], c[:], ALU.subtract))
            at["c"] = step.n
        elif n == 10:
            dve.wait_ge(self.act_chain, 9)
            step(nc.vector.tensor_tensor(c[:], c[:], e[:], ALU.mult))
            step(nc.vector.tensor_tensor(l[:], l[:], c[:], ALU.add))
        elif n == 11:
            step(nc.vector.scalar_tensor_tensor(out=both[0:32, :], in0=v[0:32, :], scalar=0.0, in1=l[0:32, :], op0=ALU.min, op1=ALU.subtract))
            step(nc.vector.scalar_tensor_tensor(out=both[DR, :], in0=v[DR, :], scalar=0.0, in1=l[DR, :], op0=ALU.max, op1=ALU.add))
        elif n == 12:
            step(nc.vector.tensor_scalar(e[DR, :], both[DR, :], self.A[DR, :], -1.0, ALU.mult, ALU.mult))
            for t in range(NT + 1):
                cols = slice(t * P, t * P + rows_of(t))
                step(nc.vector.tensor_tensor_scan(acum[DR, cols], self.ones[DR, 0:rows_of(t)], e[DR, cols], 0.0, ALU.mult, ALU.add))
            at["acum"] = step.n
        elif n == 13:
            lk = self.keys_logf
            step(nc.vector.tensor_copy(lk[:, 0:TP], both[FR, 0:TP]))
            dve.wait_ge(self.turned, 1)
            step(nc.vector.tensor_copy(lk[:, TP:TP + PAST], core.banks[0:H, 4, 0:PAST]))
            step(nc.vector.tensor_copy(lk[:, TP + PAST:KEYS], both[FR, TP:T]))
        elif n == 14:
            for a, b in ((0, TP), (TP, KEYS)):
                step(nc.vector.tensor_tensor_scan(self.keys_sum[:, a:b], self.keys_one[:, a:b], self.keys_logf[:, a:b], 0.0, ALU.mult, ALU.add))
        elif n == 15:
            step(nc.vector.tensor_scalar(self.keys_logf[:], self.keys_sum[:], -1.0, None, ALU.mult))
            at["aug"] = step.n
            last, diag = self.last, self.diag
            step(nc.vector.tensor_copy(last[DR, 0:NT], acum[DR, P - 1:TP:P]))
            step(nc.vector.tensor_copy(last[DR, NT:NT + 1], acum[DR, T - 1:T]))
            step(nc.vector.tensor_tensor(diag[DR, :, :], core.ident[DR, DR].rearrange("p (h o) -> p h o", o=1).to_broadcast([HS, HS, NT + 1]),
                                         last[DR, None, :].to_broadcast([HS, HS, NT + 1]), ALU.mult))
            at["last"] = step.n
        elif self.TURNS < n <= self.TURNS + NT + 1:
            t = n - self.TURNS - 1
            m = rows_of(t)
            dve.wait_ge(self.turned, 2 + t)
            b = core.banks[0:m, t % 2, :]
            step(nc.vector.tensor_copy(self.logf_tm[0:m, t, :], b[:, 0:H]))
            step(nc.vector.tensor_copy(dt_tm[0:m, t, :], b[:, 32:64]))
            step(nc.vector.tensor_copy(acum_tm[0:m, t, :], b[:, P + 32:P + 64]))
            at["tm"] = step.n
        elif n == self.TURNS + NT + 3:
            dve.wait_ge(self.turned, 3 + NT)
            lastb = core.banks[:, 3, 0:HS * (NT + 1)].rearrange("p (h t) -> p t h", h=HS)
            step(nc.vector.tensor_tensor(w_tm[:], lastb, acum_tm[:], ALU.subtract))
            at["w"] = step.n
        elif n == self.TURNS + NT + 5:
            dve.wait_ge(self.act_chain, 12)
            step(nc.vector.tensor_tensor(w_tm[:], w_tm[:], dt_tm[:], ALU.mult))

    def sp(self, sp, n):
        nc, at = self.nc, self.at
        if n == 16:
            sp.wait_ge(self.chain, at["aug"])
            sp.dma_start(self.acum_d, self.acum[self.DR, :]).then_inc(self.out, 16)
            for a, r, x in ((0, 0, self.keys_one), (0, 1, self.keys_sum), (1, 0, self.keys_logf), (1, 1, self.keys_one)):
                sp.dma_start(self.aug[a][:, r, :], x[:]).then_inc(self.out, 16)
        elif n == self.TURNS + NT + 2:
            sp.wait_ge(self.chain, at["tm"])
            sp.dma_start(self.logf_to[0].rearrange("(t p) h -> p t h", p=P), self.logf_tm[:, 0:NT, :]).then_inc(self.out, 16)
            sp.dma_start(self.logf_to[1], self.logf_tm[0:TS, NT, :]).then_inc(self.out, 16)

    def finish(self, sp):
        sp.wait_ge(self.out, 7 * 16)

    def act(self, act, n):
        nc, DR, v, e, at = self.nc, self.DR, self.v, self.e, self.at
        dt_tm, acum_tm, w_tm, ea_tm, cdec = self.keep
        if n == 0:
            self.act_step = Chain(act, self.act_chain)
        step = self.act_step
        if n == 1:
            act.wait_ge(self.loaded, 16 * 6)
            step(nc.scalar.activation(self.whi[:], self.w[:], ACT.Copy))
        elif 4 <= n < 7:
            j = n - 4
            act.wait_ge(self.full, j + 1)
            step(nc.scalar.activation(v[:, j * TT:(j + 1) * TT], self.core.banks[0:self.R, j, 0:TT], ACT.Identity, bias=self.bias[:]))
        elif n == 7:
            step(nc.scalar.activation(e[:], v[:], ACT.Abs))
            step(nc.scalar.activation(e[:], e[:], ACT.Exp, scale=-1.0))
        elif n == 9:
            act.wait_ge(self.chain, at["u"])
            step(nc.scalar.activation(self.l[:], self.u[:], ACT.Ln))
            step(nc.scalar.activation(self.A[DR, :], self.A[DR, :], ACT.Exp))
            act.wait_ge(self.chain, at["c"])
            step(nc.scalar.activation(e[:], self.l[:], ACT.Exp, scale=-1.0))
        elif n == self.TURNS + NT + 4:
            act.wait_ge(self.chain, at["w"])
            step(nc.scalar.activation(ea_tm[:], acum_tm[:], ACT.Exp))
            step(nc.scalar.activation(cdec[:], self.core.banks[:, 3, 0:HS * (NT + 1)].rearrange("p (h t) -> p h t", h=HS), ACT.Exp))
            step(nc.scalar.activation(w_tm[:], w_tm[:], ACT.Exp))

    def pe(self, pe, n):
        nc, core, DR, R, at = self.nc, self.core, self.DR, self.R, self.at
        if 3 <= n < 6:
            j = n - 3
            pe.wait_ge(self.chain, at["split"])
            passes = [(x, y, k) for k in range(KB) for x, y in ((self.hi, self.whi), (self.hi, self.wlo), (self.lo, self.whi))]
            for c, (x, y, k) in enumerate(passes):
                ins = nc.tensor.matmul(core.banks[:, j, 0:TT], y[:, k, :], x[:, k, j * TT:(j + 1) * TT], start=c == 0, stop=c == len(passes) - 1)
            ins.then_inc(self.full, 1)
        elif n == 6:
            for t in range(2):
                ins = nc.tensor.transpose(core.banks[0:H, 4, t * P:(t + 1) * P], self.past[:, t, :], core.ident[:])
            ins.then_inc(self.turned, 1)
        elif self.TURNS <= n < self.TURNS + NT + 1:
            t = n - self.TURNS
            m = rows_of(t)
            pe.wait_ge(self.chain, at["last"] + (3 * (t - 1) if t >= 2 else 0))
            for s, x in enumerate((self.both, self.acum)):
                ins = nc.tensor.transpose(core.banks[0:m, t % 2, s * P:s * P + R], x[:, t * P:t * P + m], core.ident[0:R, 0:R])
            ins.then_inc(self.turned, 1)
        elif n == self.TURNS + NT + 2:
            nc.tensor.matmul(core.banks[:, 3, 0:HS * (NT + 1)], self.ones[DR, :], self.diag[DR, :, :].rearrange("p h t -> p (h t)"),
                             start=True, stop=True).then_inc(self.turned, 1)


def project_qkv(core, hi, lo, w_in, norm_weights, q_to, k_to, v_to, *decay_args):
    nc = core.nc
    with ExitStack() as ctx:
        sb = lambda n, s, dt=F32: ctx.enter_context(nc.sbuf_tensor(f"qkv_{n}", s, dt))
        sem = core.semaphores(ctx, "qkv")
        norm = HeadNormTm(sb, sem, 4, norm_weights, (q_to, k_to))
        v = CopyTm(sb, sem, "v", 2, *v_to)

        def panel(part, r):
            ep, occurrence = (norm, 2 * r + part) if part < 2 else (v, r)
            return True, lambda i: w_in[:, bass.ds((2 * i + r) * PW + part * D, PW)], ep, occurrence
        stream = Stream(core, "tiles", sb, sem, hi, lo, [panel(part, r) for r in range(2) for part in range(3)], 2, (5, 6, 7),
                        w_in[:, C_X:C_X + PW])
        norm.stream = v.stream = stream
        decays = Decays(core, sb, sem, hi, lo, w_in, *decay_args)
        block = ctx.enter_context(nc.Block())

        @block.vector
        def _(dve):
            decays.start_dve(dve)
            stream.start_dve(dve)

            def body(i, last):
                for n in range(stream.slots):
                    stream.dve(dve, i, n, last)
                    if last:
                        decays.dve(dve, n)
            loop(dve, stream.rounds, body)

        @block.sync
        def _(sp):
            stream.start_sp(sp)
            decays.start_sp(sp)

            def body(i, last):
                for n in range(stream.slots):
                    stream.sp(sp, i, n, last)
                    if last:
                        decays.sp(sp, n)
            loop(sp, stream.rounds, body)
            norm.finish(sp)
            v.finish(sp)
            decays.finish(sp)

        @block.scalar
        def _(act):
            stream.start_act(act)

            def body(i, last):
                for n in range(stream.slots):
                    stream.act(act, i, n, last)
                    if last:
                        decays.act(act, n)
            loop(act, stream.rounds, body)

        @block.tensor
        def _(pe):
            def body(i, last):
                for n in range(stream.slots):
                    stream.pe(pe, i, n)
                    if last:
                        decays.pe(pe, n)
            loop(pe, stream.rounds, body)


class SiluTm:

    def __init__(self, sb, sem, per, to_prompt, to_running):
        self.per, self.to = per, (to_prompt, to_running)
        self.stage = sb("z_stage", [P, NT + 1, PW])
        self.tanh = [sb(f"z_tanh{j}", [P, PW]) for j in range(2)]
        self.tanhed, self.made, self.stored = sem("z_tanhed"), sem("z_made"), sem("z_stored")
        assert per * (NT + 1) % 2 == 0

    def start_sp(self, sp):
        sp.sem_inc(self.stored, 32)

    def start_act(self, act):
        pass

    def start_dve(self, dve):
        dve.sem_inc(self.made, 2)

    def act(self, act, i, n):
        s = self.stream
        for k, t in s.mine(self, n):
            q, m = i * self.per + k, rows_of(t)
            if t == 0:
                act.wait_ge(self.stored, 32 * (q + 1))
            s.wait_full(act, i, n)
            act.wait_ge(self.made, q * (NT + 1) + t + 1)
            s.nc.scalar.activation(self.tanh[(k * (NT + 1) + t) % 2][0:m, :], s.bank(n, m, PW), ACT.Tanh, scale=0.5).then_inc(self.tanhed, 1)
            s.nc.scalar.activation(self.stage[0:m, t, :], s.bank(n, m, PW), ACT.Copy).then_inc(s.free, 1)

    def dve(self, dve, i, n):
        s = self.stream
        for k, t in s.mine(self, n):
            q, m = i * self.per + k, rows_of(t)
            dve.wait_ge(self.tanhed, q * (NT + 1) + t + 1)
            s.wait_free(dve, i, n)
            s.nc.vector.scalar_tensor_tensor(out=self.stage[0:m, t, :], in0=self.tanh[(k * (NT + 1) + t) % 2][0:m, :], scalar=1.0,
                                             in1=self.stage[0:m, t, :], op0=ALU.add, op1=ALU.mult).then_inc(self.made, 1)

    def sp(self, sp, i, n):
        for k, t in self.stream.mine(self, n):
            if t == NT:
                q = i * self.per + k
                self.stream.core.hold(sp, self.made, (q + 1) * (NT + 1) + 2)
                cols = bass.ds(q * PW, PW)
                sp.dma_start(self.to[0][:, cols].rearrange("(t p) d -> p t d", p=P), self.stage[:, 0:NT, :]).then_inc(self.stored, 16)
                sp.dma_start(self.to[1][:, cols], self.stage[0:TS, NT, :]).then_inc(self.stored, 16)

    def finish(self, sp):
        sp.wait_ge(self.stored, 32 * (self.stream.rounds * self.per + 1))


class TanhFm:

    def __init__(self, sb, sem, per, to):
        self.per, self.to = per, to
        self.stage = [sb(f"tanh{j}", [P, TT]) for j in range(3)]
        self.stored = [sem(f"tanh_stored{j}") for j in range(3)]

    def start_sp(self, sp):
        for j in range(3):
            sp.sem_inc(self.stored[j], 16)

    def start_act(self, act):
        pass

    def start_dve(self, dve):
        pass

    def act(self, act, i, n):
        s = self.stream
        for k, t in s.mine(self, n):
            act.wait_ge(self.stored[t % 3], 16 * ((i * self.per + k) * 2 + t // 3 + 1))
            s.wait_full(act, i, n)
            s.nc.scalar.activation(self.stage[t % 3][:], s.bank(n, P, TT), ACT.Tanh, scale=0.5).then_inc(s.free, 1)

    def dve(self, dve, i, n):
        pass

    def sp(self, sp, i, n):
        s = self.stream
        for k, t in s.mine(self, n):
            s.core.hold(sp, s.free, len(s.banks) + i * s.slots + n + 1)
            r = t % 3
            sp.dma_start(self.to[bass.ds(((i * self.per + k) * 2 + t // 3) * P, P), r * TT:(r + 1) * TT], self.stage[r][:]).then_inc(self.stored[r], 16)

    def finish(self, sp):
        for j in range(3):
            sp.wait_ge(self.stored[j], 16 * (self.stream.rounds * self.per * 2 + 1))


class ConvFm:
    W = CW - 1 + TP + CW - 1 + TS
    RUN = CW - 1 + TP + CW - 1
    L = W - CW + 1
    NB = CD // P

    def __init__(self, sb, sem, per, conv_w, conv_b, state, to, tail_prompt, tail_running):
        self.per, self.params, self.to, self.tails_to = per, (conv_w, conv_b, state), to, (tail_prompt, tail_running)
        self.xs = [sb(f"xs{m}", [P, self.W]) for m in range(2)]
        self.co = [sb(f"co{m}", [P, self.L]) for m in range(2)]
        self.tanh = sb("co_tanh", [P, self.L])
        self.rows = [sb(f"conv_rows{j}", [P, P]) for j in range(2)]
        self.taps, self.past = sb("taps", [P, CW * self.NB]), sb("past_bias", [P, CW * self.NB])
        self.tails = sb("tails", [P, 2, CW - 1, self.NB])
        self.p_loaded, self.p_turned, self.p_made, self.cleared = sem("p_loaded"), sem("p_turned"), sem("p_made"), sem("cleared")
        self.copied, self.chain = sem("xs_copied"), sem("conv_chain")
        self.tanhed, self.made = sem("co_tanhed"), sem("co_made")
        self.stored = [sem(f"co_stored{m}") for m in range(2)]
        self.tails_turned, self.tails_copied, self.tails_out = sem("tails_turned"), sem("tails_copied"), sem("tails_out")

    def ended(self, n):
        return [(k, t // 3) for k, t in self.stream.mine(self, n) if t % 3 == 2]

    def start_sp(self, sp):
        w, b, state = self.params
        NB = self.NB
        sp.dma_start(self.rows[0][:], w.rearrange("j (m p) -> (j m) p", p=P)).then_inc(self.p_loaded, 16)
        sp.dma_start(self.rows[1][0:(CW - 1) * NB, :], state.rearrange("j (m p) -> (j m) p", p=P)).then_inc(self.p_loaded, 16)
        sp.dma_start(self.rows[1][(CW - 1) * NB:CW * NB, :], b.rearrange("(m p) -> m p", p=P)).then_inc(self.p_loaded, 16)
        for m in range(2):
            sp.sem_inc(self.stored[m], 32)

    def start_pe(self, pe, bank):
        pe.wait_ge(self.p_loaded, 48)
        for j in range(2):
            ins = self.stream.nc.tensor.transpose(bank[:, 256 + j * P:256 + (j + 1) * P], self.rows[j][:], self.stream.core.ident[:])
        ins.then_inc(self.p_turned, 1)

    def start_act(self, act, bank=None):
        NB, copy = self.NB, self.stream.nc.scalar.activation
        act.wait_ge(self.p_turned, 1)
        past = (CW - 1) * NB
        bank = self.bank
        copy(self.taps[:], bank[:, 256:384], ACT.Copy, scale=0.5).then_inc(self.p_made, 1)
        copy(self.past[:, 0:past], bank[:, 384:384 + past], ACT.Copy).then_inc(self.p_made, 1)
        copy(self.past[:, past:CW * NB], bank[:, 384 + past:384 + CW * NB], ACT.Copy, scale=0.5).then_inc(self.p_made, 1)
        act.wait_ge(self.p_made, 3)

    def start_dve(self, dve):
        for m in range(2):
            self.stream.nc.vector.memset(self.xs[m][:, 0:CW - 1], 0.0).then_inc(self.cleared, 1)
        dve.sem_inc(self.chain, 8)
        dve.sem_inc(self.made, 1)
        dve.wait_ge(self.cleared, 2)
        dve.wait_ge(self.p_made, 3)

    def act(self, act, i, n):
        s, NB = self.stream, self.NB
        copy = s.nc.scalar.activation
        for k, m in self.ended(n - 4):
            B = (i * self.per + k) * 2 + m
            act.wait_ge(self.chain, 4 * B + 12)
            act.wait_ge(self.made, B + 1)
            copy(self.tanh[:], self.co[m][:], ACT.Tanh).then_inc(self.tanhed, 1)
        for k, t in s.mine(self, n):
            m, r = t // 3, t % 3
            B = (i * self.per + k) * 2 + m
            xs, bank = self.xs[m], s.bank(n, P, TT)
            if r == 0:
                act.wait_ge(self.chain, 4 * B + 4)
                copy(xs[:, self.RUN - CW + 1:self.RUN], self.past[:, 0:(CW - 1) * NB].rearrange("p (j m) -> p j m", m=NB)[:, :, bass.ds(B, 1)]
                     .rearrange("p j o -> p (j o)"), ACT.Copy).then_inc(self.copied, 1)
            s.wait_full(act, i, n)
            if r < 2:
                copy(xs[:, CW - 1 + r * TT:CW - 1 + (r + 1) * TT], bank, ACT.Copy).then_inc(s.free, 1)
                continue
            own = TP - 2 * TT
            for st, end in ((0, own), (1, TT)):
                copy(self.tails[:, st, :, bass.ds(B, 1)].rearrange("p j o -> p (j o)"), bank[:, end - CW + 1:end], ACT.Copy).then_inc(self.copied, 1)
            copy(xs[:, CW - 1 + 2 * TT:CW - 1 + TP], bank[:, 0:own], ACT.Copy).then_inc(self.copied, 1)
            copy(xs[:, self.RUN:self.W], bank[:, own:TT], ACT.Copy).then_inc(s.free, 1)

    def dve(self, dve, i, n):
        s, NB, L = self.stream, self.NB, self.L
        for lag, taps in ((1, (0, 1)), (2, (2,)), (3, (3,))):
            for k, m in self.ended(n - lag):
                B = (i * self.per + k) * 2 + m
                co, xs = self.co[m][:], self.xs[m]
                if lag == 1:
                    dve.wait_ge(self.copied, 4 * B + 4)
                    s.wait_free(dve, i, n - 1)
                    dve.wait_ge(self.stored[m], 32 * (i * self.per + k + 1))
                step = Chain(dve, self.chain)
                step.enter(B + 2, 4)
                step.n = taps[0]
                for j in taps:
                    if j == 0:
                        step(s.nc.vector.tensor_scalar(co, xs[:, 0:L], self.taps[:, bass.ds(B, 1)], self.past[:, bass.ds(B + (CW - 1) * NB, 1)],
                                                       ALU.mult, ALU.add))
                    else:
                        step(s.nc.vector.scalar_tensor_tensor(out=co, in0=xs[:, j:j + L], scalar=self.taps[:, bass.ds(B + j * NB, 1)], in1=co,
                                                              op0=ALU.mult, op1=ALU.add))
        for k, m in self.ended(n - 5):
            B = (i * self.per + k) * 2 + m
            dve.wait_ge(self.tanhed, B + 1)
            s.nc.vector.scalar_tensor_tensor(out=self.co[m][:], in0=self.tanh[:], scalar=1.0, in1=self.co[m][:],
                                             op0=ALU.add, op1=ALU.mult).then_inc(self.made, 1)

    def sp(self, sp, i, n):
        for k, m in self.ended(n - 5):
            B = (i * self.per + k) * 2 + m
            self.stream.core.hold(sp, self.made, B + 2)
            rows = bass.ds(B * P, P)
            sp.dma_start(self.to[rows, 0:TP], self.co[m][:, 0:TP]).then_inc(self.stored[m], 16)
            sp.dma_start(self.to[rows, TP:T], self.co[m][:, self.RUN - CW + 1:self.L]).then_inc(self.stored[m], 16)

    def finish_pe(self, pe, bank):
        s = self.stream
        s.wait_free(pe, s.rounds - 1, s.slots - 1)
        pe.wait_ge(self.copied, 4 * self.NB)
        rows = (CW - 1) * self.NB
        for st in range(2):
            ins = s.nc.tensor.transpose(bank[0:rows, 256 + st * P:256 + (st + 1) * P], self.tails[:, st, :, :].rearrange("p j m -> p (j m)"), s.core.ident[:])
        ins.then_inc(self.tails_turned, 1)

    def finish_act(self, act, bank):
        rows = (CW - 1) * self.NB
        act.wait_ge(self.tails_turned, 1)
        for st in range(2):
            self.stream.nc.scalar.activation(self.rows[st][0:rows, :], bank[0:rows, 256 + st * P:256 + (st + 1) * P], ACT.Copy).then_inc(self.tails_copied, 1)

    def finish(self, sp):
        rows = (CW - 1) * self.NB
        sp.wait_ge(self.tails_copied, 2)
        for st in range(2):
            sp.dma_start(self.tails_to[st].rearrange("j (m p) -> (j m) p", p=P), self.rows[st][0:rows, :]).then_inc(self.tails_out, 16)
        sp.wait_ge(self.tails_out, 32)
        for m in range(2):
            sp.wait_ge(self.stored[m], 32 * (self.stream.rounds * self.per + 1))


def rows_of(t):
    return P if t < NT else TS


class MergeFm:

    def __init__(self, sb, sem, gates, merged):
        self.gates, self.merged = gates, merged
        self.g = [sb(f"g{j}", [P, TT]) for j in range(4)]
        self.tmp = [sb(f"tmp{j}", [P, TT]) for j in range(2)]
        self.g_loaded = [sem(f"g_loaded{j}") for j in range(4)]
        self.gated = sem("gated")

    def part(self, k, t):
        return 2 * (k % 4) + t % 2, slice(t // 2 * TT, (t // 2 + 1) * TT)

    def load_gate(self, sp, n):
        for k, t in self.stream.mine(self, n):
            v = (k - 4) * 6 + t
            if v < 0:
                continue
            if v >= 4:
                sp.wait_ge(self.gated, v - 3)
            blk, cols = self.part(k, t)
            sp.dma_start(self.g[v % 4][:], self.gates[1 if k < 8 else 0][blk * P:(blk + 1) * P, cols]).then_inc(self.g_loaded[v % 4], 16)

    def start_sp(self, sp):
        pass

    def start_act(self, act):
        pass

    def start_dve(self, dve):
        pass

    def sp(self, sp, i, n):
        self.load_gate(sp, n + 2)

    def act(self, act, i, n):
        pass

    def dve(self, dve, i, n):
        s = self.stream
        v = s.nc.vector
        for k, t in s.mine(self, n):
            blk, cols = self.part(k, t)
            out, bank = self.merged[:, blk, cols], s.bank(n, P, TT)
            s.wait_full(dve, 0, n)
            if k < 4:
                v.tensor_copy(out, bank).then_inc(s.free, 1)
                continue
            u = (k - 4) * 6 + t
            tmp, g = self.tmp[n % 2][:], self.g[u % 4][:]
            s.wait_free(dve, 0, n - 1)
            if u:
                dve.wait_ge(self.gated, u)
            dve.wait_ge(self.g_loaded[u % 4], 16 * (u // 4 + 1))
            if k < 8:
                v.tensor_tensor(tmp, bank, out, ALU.add).then_inc(s.free, 1)
                s.wait_free(dve, 0, n)
                v.scalar_tensor_tensor(out=out, in0=g, scalar=1.0, in1=tmp, op0=ALU.add, op1=ALU.mult).then_inc(self.gated, 1)
            else:
                v.scalar_tensor_tensor(out=tmp, in0=g, scalar=1.0, in1=bank, op0=ALU.add, op1=ALU.mult).then_inc(s.free, 1)
                s.wait_free(dve, 0, n)
                v.tensor_tensor(out, out, tmp, ALU.add).then_inc(self.gated, 1)


class ResidualTm:

    def __init__(self, sb, sem, x2, x_srcs, to):
        self.x2, self.srcs, self.to = x2, x_srcs, to
        self.ss = sb("ss", [P, NT + 1, D // PW])
        self.junk = sb("junk", [P, PW])
        self.x_loaded = [sem(f"x_loaded{t}") for t in range(NT + 1)]
        self.squared, self.stored = sem("squared"), sem("x2_stored")

    def load_x(self, sp):
        for r in range(NT + 1):
            sp.dma_start(self.x2[0:rows_of(r), r, :], self.srcs[1] if r == NT else self.srcs[0][r * P:(r + 1) * P, :]).then_inc(self.x_loaded[r], 16)

    def start_sp(self, sp):
        pass

    def start_act(self, act):
        pass

    def start_dve(self, dve):
        pass

    def sp(self, sp, i, n):
        s = self.stream
        for k, t in s.mine(self, n):
            if k == D // PW - 1:
                s.wait_free(sp, 0, n)
                sp.dma_start(self.to[1] if t == NT else self.to[0][t * P:(t + 1) * P, :], self.x2[0:rows_of(t), t, :]).then_inc(self.stored, 16)

    def act(self, act, i, n):
        s = self.stream
        for k, t in s.mine(self, n):
            m = rows_of(t)
            s.wait_free(act, 0, n)
            if k + t:
                act.wait_ge(self.squared, k * (NT + 1) + t)
            s.nc.scalar.activation(self.junk[0:m, :], self.x2[0:m, t, k * PW:(k + 1) * PW], ACT.Square,
                                   accum_out=self.ss[0:m, t, k:k + 1]).then_inc(self.squared, 1)

    def dve(self, dve, i, n):
        s = self.stream
        for k, t in s.mine(self, n):
            x = self.x2[0:rows_of(t), t, k * PW:(k + 1) * PW]
            if k == 0:
                dve.wait_ge(self.x_loaded[t], 16)
            s.wait_full(dve, 0, n)
            s.nc.vector.scalar_tensor_tensor(out=x, in0=s.bank(n, rows_of(t), PW), scalar=0.5, in1=x, op0=ALU.mult, op1=ALU.add).then_inc(s.free, 1)


def branches(core, y_d, rms, ssm_norm_w, att_d, gates, w_pa, w_pb, merged, following):
    nc = core.nc
    ST = NT + 1
    with ExitStack() as ctx:
        sb = lambda n, s, dt=F32: ctx.enter_context(nc.sbuf_tensor(f"br_{n}", s, dt))
        sem = core.semaphores(ctx, "br")
        op_hi, op_lo = sb("operand_hi", [P, KB, T], F32R), sb("operand_lo", [P, KB, T], F32R)
        rows = [sb(f"rows{j}", [P, D]) for j in range(3)]
        wb = sb("wb", [P, 2 * D])
        merge = MergeFm(sb, sem, gates, merged)
        matrices = [w_pb[0:D, :], w_pb[D:2 * D, :], w_pa]
        panels = [(False, lambda i, s=s, k=k: matrices[s][:, k * PW:(k + 1) * PW], merge, 4 * s + k) for s in range(3) for k in range(4)]
        stream = merge.stream = Stream(core, "tiles", sb, sem, op_hi, op_lo, panels, 1, (0, 1, 2, 3), following)
        stream.by_range = True
        loaded = [sem(f"rows_loaded{j}") for j in range(3)]
        w_loaded, scaled, turned, t_hi, t_lo = sem("w_loaded"), sem("scaled"), sem("turned"), sem("turned_hi"), sem("turned_lo")
        block = ctx.enter_context(nc.Block())
        SPAN = 24
        HEAD = 5

        def turn_at(n):
            s, t = n // SPAN, n % SPAN
            if s < 3 and t < ST - HEAD:
                return s * ST + HEAD + t
            if s < 2 and t >= SPAN - HEAD:
                return (s + 1) * ST + t - (SPAN - HEAD)
            return None

        def rows_source(u):
            s, t = u // ST, u % ST
            a, cols = (y_d, slice(s * D, (s + 1) * D)) if s < 2 else (att_d, slice(0, D))
            return a[t * P:t * P + rows_of(t), cols]

        def halves(u):
            t = u % ST
            n = rows_of(t)
            return [(2 * u + half, slice(4 * half, 4 * half + 4), slice(t * P, t * P + n),
                     core.banks[:, 4 + (2 * u + half) % 4, 0:4 * n].rearrange("p (k n) -> p k n", k=4)) for half in range(2)]

        @block.sync
        def _(sp):
            def load_rows(u):
                if u is None:
                    return
                if u >= 3:
                    sp.wait_ge(turned, 2 * (u - 2))
                sp.dma_start(rows[u % 3][0:rows_of(u % ST), :], rows_source(u)).then_inc(loaded[u % 3], 16)
            load_rows(0)
            sp.dma_start(wb[:], ssm_norm_w.to_broadcast([P, 2 * D])).then_inc(w_loaded, 16)
            load_rows(1)
            for u in range(2, HEAD + 2):
                load_rows(u)
            stream.load(sp, 0, 1)
            for n in range(stream.slots):
                load_rows(turn_at(n + 2))
                stream.sp(sp, 0, n, True)

        @block.tensor
        def _(pe):
            def turn(u):
                n = rows_of(u % ST)
                if u >= 2 * ST:
                    pe.wait_ge(loaded[u % 3], 16 * (u // 3 + 1))
                else:
                    pe.wait_ge(scaled, u + 1)
                for i, blocks, _, _ in halves(u):
                    if i >= 4:
                        core.hold(pe, t_lo, i - 3)
                    for k in range(4):
                        kb = blocks.start + k
                        ins = nc.tensor.transpose(core.banks[:, 4 + i % 4, k * n:(k + 1) * n], rows[u % 3][0:n, kb * P:(kb + 1) * P], core.ident[0:n, 0:n])
                    ins.then_inc(turned, 1)
            for u in range(HEAD):
                turn(u)
            for n in range(stream.slots):
                s, t = n // SPAN, n % SPAN
                if t < 6:
                    end = min((t // 2 + 1) * TT, T)
                    pe.wait_ge(t_lo, 2 * (s * ST + (end + P - 1) // P))
                stream.pe(pe, 0, n)
                if turn_at(n) is not None:
                    turn(turn_at(n))

        @block.scalar
        def _(act):
            def make_hi(u):
                for i, blocks, cols, bank in halves(u):
                    act.wait_ge(turned, i + 1)
                    nc.scalar.activation(op_hi[:, blocks, cols], bank, ACT.Copy).then_inc(t_hi, 1)
            act.sem_inc(stream.hi_made, 4)
            for u in range(HEAD):
                make_hi(u)
            for n in range(stream.slots):
                stream.act(act, 0, n, True)
                if turn_at(n) is not None:
                    make_hi(turn_at(n))

        @block.vector
        def _(dve):
            def scale(u):
                s, t = u // ST, u % ST
                n, r = rows_of(t), rows[u % 3]
                if s == 2:
                    return
                dve.wait_ge(loaded[u % 3], 16 * (u // 3 + 1))
                for g in range(D // GW):
                    cols, c = slice(g * GW, (g + 1) * GW), s * (D // GW) + g
                    ins = nc.vector.scalar_tensor_tensor(out=r[0:n, cols], in0=r[0:n, cols], scalar=rms[0:n, t, c:c + 1],
                                                         in1=wb[0:n, c * GW:(c + 1) * GW], op0=ALU.mult, op1=ALU.mult)
                ins.then_inc(scaled, 1)

            def make_lo(u):
                for i, blocks, cols, bank in halves(u):
                    dve.wait_ge(t_hi, i + 1)
                    nc.vector.tensor_tensor(op_lo[:, blocks, cols], bank, op_hi[:, blocks, cols].bitcast(F32), ALU.subtract).then_inc(t_lo, 1)
            dve.sem_inc(stream.free, len(stream.banks))
            dve.sem_inc(stream.lo_made, 4)
            dve.wait_ge(w_loaded, 16)
            for u in range(HEAD):
                scale(u)
                if u:
                    make_lo(u - 1)
            make_lo(HEAD - 1)
            scale(HEAD)
            for n in range(stream.slots):
                if turn_at(n + 1) is not None:
                    scale(turn_at(n + 1))
                stream.dve(dve, 0, n, True)
                if turn_at(n) is not None:
                    make_lo(turn_at(n))


def out_norm(core, merged, w_out, x_srcs, x2_to, norm2_w, hi, lo, following):
    nc = core.nc
    ST = NT + 1
    with ExitStack() as ctx:
        sb = lambda n, s, dt=F32: ctx.enter_context(nc.sbuf_tensor(f"out_{n}", s, dt))
        sem = core.semaphores(ctx, "out")
        x2 = sb("x2", [P, ST, D])
        rows = [sb(f"rows{j}", [P, D]) for j in range(3)]
        wb, ms = sb("wb", [P, D]), sb("ms", [P, ST])
        residual = ResidualTm(sb, sem, x2, x_srcs, x2_to)
        panels = [(True, lambda i, k=k: w_out[:, k * PW:(k + 1) * PW], residual, k) for k in range(4)]
        stream = residual.stream = Stream(core, "tiles", sb, sem, hi, lo, panels, 1, (0, 1, 2, 3), following)
        w_loaded, scaled, turned, t_hi, t_lo = sem("w_loaded"), sem("scaled"), sem("turned"), sem("turned_hi"), sem("turned_lo")
        padded, meaned, rooted, inverted = sem("padded"), sem("meaned"), sem("rooted"), sem("inverted")
        m_hi, m_lo = sem("merged_hi"), sem("merged_lo")
        block = ctx.enter_context(nc.Block())
        LAST = stream.slots - ST
        LAG = 3
        END = stream.slots + LAG

        def turn_at(n):
            return n - LAST - LAG if LAST + LAG <= n < END else None

        def halves(t):
            n = rows_of(t)
            return [(2 * t + half, slice(4 * half, 4 * half + 4), slice(t * P, t * P + n),
                     core.banks[:, 4 + (2 * t + half) % 4, 0:4 * n].rearrange("p (k n) -> p k n", k=4)) for half in range(2)]
        thirds = [slice(r * TT, (r + 1) * TT) for r in range(3)]

        @block.sync
        def _(sp):
            residual.load_x(sp)
            sp.dma_start(wb[:], norm2_w.to_broadcast([P, D])).then_inc(w_loaded, 16)
            stream.load(sp, 0, 1)
            for n in range(stream.slots):
                stream.sp(sp, 0, n, True)
            sp.wait_ge(residual.stored, 16 * ST)

        @block.tensor
        def _(pe):
            for n in range(END):
                if n < ST:
                    pe.wait_ge(m_lo, min(((n + 1) * P - 1) // TT, 2) + 1)
                if n == ST - 1:
                    pe.wait_ge(padded, 2)
                if n < stream.slots:
                    stream.pe(pe, 0, n)
                t = turn_at(n)
                if t is None:
                    continue
                m = rows_of(t)
                pe.wait_ge(scaled, t + 1)
                for i, blocks, _, _ in halves(t):
                    if i >= 4:
                        core.hold(pe, t_lo, i - 3)
                    for k in range(4):
                        kb = blocks.start + k
                        ins = nc.tensor.transpose(core.banks[:, 4 + i % 4, k * m:(k + 1) * m], rows[t % 3][0:m, kb * P:(kb + 1) * P], core.ident[0:m, 0:m])
                    ins.then_inc(turned, 1)

        @block.scalar
        def _(act):
            act.sem_inc(stream.hi_made, 4)
            for r in thirds:
                nc.scalar.activation(hi[:, :, r], merged[:, :, r], ACT.Copy).then_inc(m_hi, 1)
            for n in range(END):
                if n < stream.slots:
                    stream.act(act, 0, n, True)
                t = turn_at(n)
                if t is not None:
                    for i, blocks, cols, bank in halves(t):
                        act.wait_ge(turned, i + 1)
                        nc.scalar.activation(hi[:, blocks, cols], bank, ACT.Copy).then_inc(t_hi, 1)
                t = n - LAST - 1
                if 0 <= t < ST:
                    act.wait_ge(meaned, 2 * t + 2)
                    nc.scalar.activation(ms[0:rows_of(t), t:t + 1], ms[0:rows_of(t), t:t + 1], ACT.Sqrt).then_inc(rooted, 1)

        @block.vector
        def _(dve):
            dve.sem_inc(stream.free, len(stream.banks))
            dve.sem_inc(stream.lo_made, 4)
            for j, r in enumerate(thirds):
                dve.wait_ge(m_hi, j + 1)
                nc.vector.tensor_tensor(lo[:, :, r], merged[:, :, r], hi[:, :, r].bitcast(F32), ALU.subtract).then_inc(m_lo, 1)
            for x in (hi, lo):
                nc.vector.memset(x[:, :, T:TW].bitcast(F32), 0.0).then_inc(padded, 1)

            def scale(t):
                m = rows_of(t)
                if t >= 3:
                    dve.wait_ge(turned, 2 * (t - 2))
                dve.wait_ge(rooted, t + 1)
                nc.vector.reciprocal(ms[0:m, t:t + 1], ms[0:m, t:t + 1]).then_inc(inverted, 1)
                dve.wait_ge(inverted, t + 1)
                nc.vector.scalar_tensor_tensor(out=rows[t % 3][0:m, :], in0=x2[0:m, t, :], scalar=ms[0:m, t:t + 1], in1=wb[0:m, :],
                                               op0=ALU.mult, op1=ALU.mult).then_inc(scaled, 1)
            for n in range(END):
                if turn_at(n + 1) is not None:
                    if turn_at(n + 1) == 0:
                        dve.wait_ge(w_loaded, 16)
                    scale(turn_at(n + 1))
                if n < stream.slots:
                    stream.dve(dve, 0, n, True)
                t = n - LAST - 1
                if 0 <= t < ST:
                    m = rows_of(t)
                    dve.wait_ge(residual.squared, 3 * ST + t + 1)
                    nc.vector.tensor_reduce(ms[0:m, t:t + 1], residual.ss[0:m, t, :], AX.X, ALU.add).then_inc(meaned, 1)
                    dve.wait_ge(meaned, 2 * t + 1)
                    nc.vector.tensor_scalar(ms[0:m, t:t + 1], ms[0:m, t:t + 1], 1.0 / D, EPS, ALU.mult, ALU.add).then_inc(meaned, 1)
                t = turn_at(n)
                if t is not None:
                    for i, blocks, cols, bank in halves(t):
                        dve.wait_ge(t_hi, i + 1)
                        nc.vector.tensor_tensor(lo[:, blocks, cols], bank, hi[:, blocks, cols].bitcast(F32), ALU.subtract).then_inc(t_lo, 1)


def mlp(core, hi, lo, acc, w_up, w_down, x2_prompt, x2_running, y_prompt, y_running):
    nc = core.nc
    FB = FS // P
    NB = 6
    UP, DOWN = 6, 12
    PER = 2 * UP + 2 * DOWN
    start_of = [0, UP, 2 * UP, 2 * UP + DOWN]
    SLICES = FF // FS
    with ExitStack() as ctx:
        sb = lambda n, s, dt=F32: ctx.enter_context(nc.sbuf_tensor(f"mlp_{n}", s, dt))
        sem = core.semaphores(ctx, f"mlp")
        raw, whi, wlo = [core.raw, sb("raw1", [P, KB * PW])], core.whi, core.wlo
        uhi, ulo = sb("uhi", [P, FB, T], F32R), sb("ulo", [P, FB, T], F32R)
        spare = sb("relu_sq", [P, 4 * TT])
        relu = [spare[:, j * TT:(j + 1) * TT] for j in range(2)]
        sq = [spare[:, (2 + j) * TT:(3 + j) * TT] for j in range(2)]
        raw_loaded = [sem(f"raw_loaded{b}") for b in range(2)]
        hi_made = [sem(f"whi_made{b}") for b in range(2)]
        lo_made = [sem(f"wlo_made{b}") for b in range(2)]
        full, free, relued, u_made = sem("bank_full"), sem("bank_free"), sem("relued"), sem("u_made")
        cleared, chain = sem("cleared"), sem("vec_chain")
        ST = NT + 1
        SUMS, OWN, SPARE = 2 * ST, 7, 2
        own_x2 = sb("x2", [P, OWN, 512])
        piece = [own_x2[:, i, :] for i in range(OWN)] + [spare[:, i * 512:(i + 1) * 512] for i in range(SPARE)] + \
            [raw[b][:, i * 512:(i + 1) * 512] for b in range(2) for i in range(4)] + [own_x2[:, 0, :]]
        assert len(piece) == SUMS
        x2_loaded = [sem(f"x2_loaded{i}") for i in range(SUMS)]
        turned, added, y_stored, first_stored = sem("turned"), sem("added"), sem("y_stored"), sem("y_first_stored")

        def rows_dram(prompt, running, i):
            t, cols = i % ST, slice(i // ST * 512, (i // ST + 1) * 512)
            return running[:, cols] if t == NT else prompt[t * P:(t + 1) * P, cols]
        block = ctx.enter_context(nc.Block())

        def weights(s, j):
            if j < 2:
                return w_up[:, bass.ds(s * FS + j * PW, PW)].rearrange("(k p) m -> p k m", p=P)
            return w_down[bass.ds(s * FS, FS), (j - 2) * 512:(j - 1) * 512].rearrange("(k p) m -> p k m", p=P)

        def items(j):
            return (0, j + 2) if j < 2 else (1, j - 2)

        @block.sync
        def _(sp):
            def load(s, j, fresh=False):
                b = j % 2
                if not fresh:
                    sp.wait_ge(lo_made[b], 2 * s + j // 2)
                view = raw[b][:].rearrange("p (k m) -> p k m", k=KB if j < 2 else FB)
                sp.dma_start(view, weights(s, j)).then_inc(raw_loaded[b], 16)
            load(0, 1, True)

            def body(s, last):
                for j in range(4):
                    on, slot = items(j)
                    if not (last and on):
                        load(s + on, slot)
            loop(sp, SLICES, body)
            def load_x2(i):
                sp.dma_start(piece[i][0:rows_of(i % ST), :], rows_dram(x2_prompt, x2_running, i)).then_inc(x2_loaded[i], 16)

            def store_y(i):
                sp.wait_ge(added, i + 1)
                sp.dma_start(rows_dram(y_prompt, y_running, i), piece[i][0:rows_of(i % ST), :]).then_inc(y_stored if i else first_stored, 16)
            for i in range(SUMS - 1):
                if i == OWN:
                    sp.wait_ge(u_made, SLICES * 2 * UP + 2)
                elif i == OWN + SPARE or i == OWN + SPARE + 4:
                    sp.wait_ge(lo_made[(i - OWN - SPARE) // 4], 2 * SLICES)
                load_x2(i)
            store_y(0)
            sp.wait_ge(first_stored, 16)
            load_x2(SUMS - 1)
            for i in range(1, SUMS):
                store_y(i)
            sp.wait_ge(y_stored, 16 * (SUMS - 1))

        @block.scalar
        def _(act):
            def split(s, j, fresh=False):
                b = j % 2
                act.wait_ge(raw_loaded[b], 16 * (2 * s + j // 2 + b))
                if not fresh:
                    before = s * PER + start_of[1 + b] if j >= 2 else (s - 1) * PER + start_of[2] + DOWN * (1 + b)
                    act.wait_ge(full, before + 1)
                nc.scalar.activation(whi[b][:], raw[b][:], ACT.Copy).then_inc(hi_made[b], 1)
            act.sem_inc(hi_made[0], 1)
            split(0, 1, True)

            def body(s, last):
                for j in range(4):
                    if j < 2:
                        for t in range(UP):
                            n = start_of[j] + t
                            act.wait_ge(full, s * PER + n + 2)
                            act.wait_ge(u_made, s * 2 * UP + j * UP + t + 1)
                            nc.scalar.activation(relu[t % 2], core.banks[:, n % NB, 0:TT], ACT.Relu).then_inc(relued, 1)
                    on, slot = items(j)
                    if not (last and on):
                        split(s + on, slot)
            loop(act, SLICES, body)

        @block.vector
        def _(dve):
            def split(s, j):
                b = j % 2
                dve.wait_ge(hi_made[b], 2 * s + j // 2 + 1)
                nc.vector.tensor_tensor(wlo[b][:], raw[b][:], whi[b][:].bitcast(F32), ALU.subtract).then_inc(lo_made[b], 1)
            nc.vector.memset(acc[:], 0.0).then_inc(cleared, 1)
            dve.sem_inc(free, NB)
            dve.sem_inc(u_made, 2)
            dve.sem_inc(lo_made[0], 1)
            split(0, 1)
            dve.wait_ge(cleared, 1)
            STEPS = 2 * UP

            def add(i):
                t = i % ST
                part = piece[i][0:rows_of(t), :]
                dve.wait_ge(x2_loaded[i], 16)
                dve.wait_ge(turned, i + 1)
                nc.vector.tensor_tensor(part, core.banks[0:rows_of(t), NB + i % 2, :], part, ALU.add).then_inc(added, 1)

            def body(s, last):
                step = Chain(dve, chain)
                step.enter(s, STEPS)
                for j in range(4):
                    if j < 2:
                        if j == 0:
                            dve.wait_ge(full, s * PER + 1)
                        for t in range(UP):
                            dve.wait_ge(relued, s * 2 * UP + j * UP + t + 1)
                            n = start_of[j] + t
                            m, cols = 2 * j + t // 3, slice((t % 3) * TT, (t % 3 + 1) * TT)
                            step(nc.vector.tensor_tensor(sq[t % 2], relu[t % 2], relu[t % 2], ALU.mult))
                            nc.vector.tensor_copy(uhi[:, m, cols], sq[t % 2]).then_inc(free, 1)
                            dve.wait_ge(free, NB + s * PER + n + 1)
                            nc.vector.tensor_tensor(ulo[:, m, cols], sq[t % 2], uhi[:, m, cols].bitcast(F32), ALU.subtract).then_inc(u_made, 1)
                    else:
                        for t in range(DOWN):
                            n = start_of[j] + t
                            m, cols = 4 * (j - 2) + t // 3, slice((t % 3) * TT, (t % 3 + 1) * TT)
                            dve.wait_ge(full, s * PER + n + 2)
                            nc.vector.tensor_tensor(acc[:, m, cols], core.banks[:, n % NB, 0:TT], acc[:, m, cols], ALU.add).then_inc(free, 1)
                            if last and j == 3 and t < ST:
                                add(t)
                    on, slot = items(j)
                    if not (last and on):
                        split(s + on, slot)
                step.leave()
            loop(dve, SLICES, body)
            for i in range(ST, 2 * ST):
                add(i)

        @block.tensor
        def _(pe):
            pe.sem_inc(full, 1)

            def turn(i):
                t, half = i % ST, i // ST
                if t == 0:
                    pe.wait_ge(free, NB + (SLICES - 1) * PER + start_of[3] + half * DOWN)
                if i >= 2:
                    pe.wait_ge(added, i - 1)
                for k in range(4):
                    ins = nc.tensor.transpose(core.banks[0:rows_of(t), NB + i % 2, k * P:(k + 1) * P],
                                              acc[:, 4 * half + k, t * P:t * P + rows_of(t)], core.ident[:])
                ins.then_inc(turned, 1)

            def body(s, last):
                for j in range(4):
                    b = j % 2
                    pe.wait_ge(lo_made[b], 2 * s + j // 2 + 1)
                    if j == 2:
                        pe.wait_ge(u_made, (s + 1) * 2 * UP + 2)
                    kb, width = (KB, PW) if j < 2 else (FB, 512)
                    xh, xl = (hi, lo) if j < 2 else (uhi, ulo)
                    wh, wl = (w[b][:].rearrange("p (k m) -> p k m", k=kb) for w in (whi, wlo))
                    for t in range(UP if j < 2 else DOWN):
                        n = start_of[j] + t
                        m, r = t // 3, t % 3
                        pe.wait_ge(free, s * PER + n + 1)
                        passes = [(x, w, k) for k in range(kb) for x, w in ((xh, wh), (xh, wl), (xl, wh))]
                        for c, (x, w, k) in enumerate(passes):
                            ins = nc.tensor.matmul(core.banks[:, n % NB, 0:TT], w[:, k, m * P:(m + 1) * P], x[:, k, r * TT:(r + 1) * TT],
                                                   start=c == 0, stop=c == len(passes) - 1)
                        ins.then_inc(full, 1)
                        if last and j == 3 and t < ST:
                            turn(t)
            loop(pe, SLICES, body)
            for i in range(ST, 2 * ST):
                turn(i)


def attention_z_xbc(core, hi, lo, w_in, z_d, xbc_d, conv, q_d, k_prompt, k_running, v_prompt, v_running, cache_k, cache_v,
                    aug_q, aug_k, att_d):
    nc = core.nc
    KX = HD + 2
    ST = NT + 1
    HR = 4
    ROUNDS = H // HR
    nkeys = [P * (s + 1) for s in range(NT)] + [PAST + TS]
    koff = [0] * NT + [TP]
    blocks = [[(j * P, min(P, n - j * P)) for j in range((n + P - 1) // P)] for n in nkeys]
    groups = [[b[g:g + 4] for g in range(0, len(b), 4)] for b in blocks]
    first_group = [sum(len(g) for g in groups[:s]) for s in range(ST + 1)]
    NG = first_group[ST]
    PREP = 5
    PREP_AT = 3
    B_SCORES, B_TURNED, B_PREP, B_OUT, B_TILES = 0, 2, 4, 5, (6, 7)
    with ExitStack() as ctx:
        sb = lambda n, s, dt=F32: ctx.enter_context(nc.sbuf_tensor(f"att_{n}", s, dt))
        sem = core.semaphores(ctx, f"att")
        two = lambda n, s: [sb(f"{n}{b}", s) for b in range(2)]
        XP, ZP = CD // PW // ROUNDS, DI // PW // ROUNDS
        xbc = ConvFm(sb, sem, XP, *conv["params"], xbc_d, *conv["tails"])
        z = SiluTm(sb, sem, ZP, z_d[0:TP, :], z_d[TP:T, :])
        x_panel = lambda k: (False, lambda i: w_in[:, bass.ds((i * XP + k) * PW + C_X, PW)], xbc, k)
        z_panel = lambda k: (True, lambda i: w_in[:, bass.ds((i * ZP + k) * PW + C_Z, PW)], z, k)
        stream = Stream(core, "tiles", sb, sem, hi, lo, [x_panel(0), x_panel(1), z_panel(0), x_panel(2), x_panel(3), z_panel(1)],
                        ROUNDS, B_TILES, w_in[:, C_GA:C_GA + PW])
        xbc.stream = z.stream = stream
        out_bank = core.banks[:, B_OUT, :]
        xbc.bank = out_bank
        q = two("q", [P, NT + 1, HD])
        k = two("k", [P, NT + 3, HD])
        v = two("v", [P, NT + 3, HD])
        qT = two("qT", [KX, TP + TS])
        kT = two("kT", [KX, KEYS])
        pr = two("pr", [P, TP])
        prT = two("prT", [P, 512])
        o = two("o", [P, ST, HD])
        nmax = two("nmax", [P, 1])
        rsum = two("rsum", [P, 1])
        rinv = two("rinv", [P, 1])
        loaded = [sem(f"loaded{b}") for b in range(2)]
        aug_loaded = [sem(f"aug_loaded{b}") for b in range(2)]
        stored = [sem(f"stored{b}") for b in range(2)]
        prep_full, prep_free = sem("prep_full"), sem("prep_free")
        s_full, s_max, s_exp = sem("scores_full"), sem("max_made"), sem("exp_made")
        t_full, t_dve = sem("probs_turned"), sem("probs_copied")
        pv, o_made = sem("pv_done"), sem("o_made")
        chain = sem("vec_chain")
        block = ctx.enter_context(nc.Block())

        order = [(hb, s) for hb in range(HR) for s in range(ST)]
        spare = stream.slots // (stream.slots - len(order))
        steps = [None if n % spare == spare - 1 else order[n - n // spare] for n in range(stream.slots)]
        assert [x for x in steps if x] == order

        def after(hb, s):
            return (hb, s + 1) if s + 1 < ST else (hb + 1, 0)

        def exists(hb, last):
            return not (last and hb == HR)

        def prep_parts(b):
            def tiles(x, lo_, hi_):
                return [(x[b][0:P, t, :], P, (t - lo_) * P) for t in range(lo_, hi_)]
            return [(tiles(q, 0, 4), qT, 0, 512, True), (tiles(k, 0, 4), kT, 0, 512, False),
                    (tiles(q, 4, 8), qT, 512, 512, True), (tiles(k, 4, 8), kT, 512, 512, False),
                    (tiles(k, NT, NT + 2) + [(k[b][0:TS, NT + 2, :], TS, PAST), (q[b][0:TS, NT, :], TS, PAST + TS)], None, 0, 0, None)]

        @block.sync
        def _(sp):
            def load(i, hb, first=False):
                h, b = HR * i + hb, hb % 2
                cols = bass.ds(h * HD, HD)
                if not first:
                    core.hold(sp, pv, (h - 1) * ST + 2)
                sp.dma_start(q[b][:, 0:NT, :], q_d[0:TP, cols].rearrange("(t p) d -> p t d", p=P)).then_inc(loaded[b], 16)
                sp.dma_start(q[b][0:TS, NT, :], q_d[TP:T, cols]).then_inc(loaded[b], 16)
                for x, prompt, cache, running in ((k, k_prompt, cache_k, k_running), (v, v_prompt, cache_v, v_running)):
                    sp.dma_start(x[b][:, 0:NT, :], prompt[:, cols].rearrange("(t p) d -> p t d", p=P)).then_inc(loaded[b], 16)
                    sp.dma_start(x[b][:, NT:NT + 2, :], cache[:, cols].rearrange("(t p) d -> p t d", p=P)).then_inc(loaded[b], 16)
                    sp.dma_start(x[b][0:TS, NT + 2, :], running[:, cols]).then_inc(loaded[b], 16)
                hh = bass.ds(h, 1)
                sp.dma_start(qT[b][HD:KX, 0:TP], aug_q[hh, :, 0:TP].rearrange("o a t -> (o a) t")).then_inc(aug_loaded[b], 16)
                sp.dma_start(qT[b][HD:KX, TP:T], aug_q[hh, :, TP + PAST:KEYS].rearrange("o a t -> (o a) t")).then_inc(aug_loaded[b], 16)
                sp.dma_start(kT[b][HD:KX, :], aug_k[hh, :, :].rearrange("o a t -> (o a) t")).then_inc(aug_loaded[b], 16)

            def store(i, hb):
                h, b = HR * i + hb, hb % 2
                cols = bass.ds(h * HD, HD)
                core.hold(sp, o_made, (h + 1) * ST + 2)
                sp.dma_start(att_d[0:TP, cols].rearrange("(t p) d -> p t d", p=P), o[b][:, 0:NT, :]).then_inc(stored[b], 16)
                sp.dma_start(att_d[TP:T, cols], o[b][0:TS, NT, :]).then_inc(stored[b], 16)
            for b in range(2):
                sp.sem_inc(stored[b], 32)
            load(0, 0, True)
            stream.start_sp(sp)

            def body(i, last):
                for n in range(stream.slots):
                    if steps[n]:
                        hb, s = steps[n]
                        if s == 1 and exists(hb + 1, last):
                            load(i, hb + 1)
                    stream.sp(sp, i, n, last)
                    if steps[n] and s == ST - 1:
                        store(i, hb)
            loop(sp, ROUNDS, body)
            for b in range(2):
                sp.wait_ge(stored[b], 32 * (H // 2 + 1))
            z.finish(sp)
            xbc.finish(sp)

        @block.tensor
        def _(pe):
            def prep(i, hb, g):
                h, b = HR * i + hb, hb % 2
                pe.wait_ge(loaded[b], 16 * 8 * (HR // 2 * i + hb // 2 + 1))
                core.hold(pe, prep_free, h * (PREP + 1) + g + 1)
                for src, n, col in prep_parts(b)[g][0]:
                    ins = nc.tensor.transpose(core.banks[0:HD, B_PREP, col:col + n], src, core.ident[0:n, 0:n])
                ins.then_inc(prep_full, 1)

            def scores(i, hb, s):
                h, b = HR * i + hb, hb % 2
                m, n, off = rows_of(s), nkeys[s], koff[s]
                if s == 0:
                    pe.wait_ge(prep_free, (h + 1) * (PREP + 1) + 1)
                    pe.wait_ge(aug_loaded[b], 48 * (HR // 2 * i + hb // 2 + 1))
                pe.wait_ge(s_exp, h * ST + s + 2)
                for c in range(0, n, 512):
                    w = min(512, n - c)
                    bank = core.banks[0:m, B_SCORES + c // 512, 0:w]
                    end = c + w == n
                    ins = nc.tensor.matmul(bank, qT[b][:, s * P:s * P + m], kT[b][:, off + c:off + c + w], start=True, stop=not end)
                    if end:
                        ins = nc.tensor.matmul(bank[:, w - m:w], core.identb[0:m, 0:m], core.maskb[0:m, 0:m], start=False, stop=True)
                ins.then_inc(s_full, 1)

            def turn(i, hb, s, g):
                h, m, par = HR * i + hb, rows_of(s), (hb * ST + s) % 2
                n = h * NG + first_group[s] + g
                slot = B_TURNED + (hb * NG + first_group[s] + g) % 2
                if g == 0:
                    core.hold(pe, s_exp, h * ST + s + 3)
                for j, (off, w) in enumerate(groups[s][g]):
                    ins = nc.tensor.transpose(core.banks[0:w, slot, j * m:(j + 1) * m], pr[par][0:m, off:off + w], core.ident[0:m, 0:m])
                ins.then_inc(t_full, 1)

            def product(i, hb, s, g):
                h, b, m, par = HR * i + hb, hb % 2, rows_of(s), (hb * ST + s) % 2
                n = h * NG + first_group[s] + g
                slot = (hb * NG + first_group[s] + g) % 2
                pe.wait_ge(o_made, h * ST + s + 1)
                core.hold(pe, t_dve, n + 3)
                for j, (off, w) in enumerate(groups[s][g]):
                    tile = (off // P) + (NT if s == NT else 0)
                    first, end = off == 0, off + w == nkeys[s]
                    ins = nc.tensor.matmul(out_bank[0:m, par * HD:(par + 1) * HD],
                                           prT[slot][0:w, j * m:(j + 1) * m], v[b][0:w, tile, :], start=first, stop=end)
                if end:
                    ins.then_inc(pv, 1)

            pe.sem_inc(pv, 2)
            xbc.start_pe(pe, out_bank)
            for g in range(PREP):
                prep(0, 0, g)
            scores(0, 0, 0)

            def body(i, last):
                for n in range(stream.slots):
                    if steps[n] is None:
                        stream.pe(pe, i, n)
                        continue
                    hb, s = steps[n]
                    for g in range(len(groups[s])):
                        turn(i, hb, s, g)
                    hn, sn = after(hb, s)
                    if exists(hn, last):
                        scores(i, hn, sn)
                    stream.pe(pe, i, n)
                    if PREP_AT <= s < PREP_AT + PREP and exists(hb + 1, last):
                        prep(i, hb + 1, s - PREP_AT)
                    for g in range(len(groups[s])):
                        product(i, hb, s, g)
            loop(pe, ROUNDS, body)
            pe.wait_ge(o_made, H * ST + 2)
            xbc.finish_pe(pe, out_bank)

        @block.scalar
        def _(act):
            act.sem_inc(prep_free, 1)
            act.sem_inc(s_exp, 2)

            def prep_copy(i, hb, g):
                h, b = HR * i + hb, hb % 2
                act.wait_ge(prep_full, h * PREP + g + 1)
                _, dst, col, n, is_q = prep_parts(b)[g]
                if dst is not None:
                    nc.scalar.activation(dst[b][0:HD, col:col + n], core.banks[0:HD, B_PREP, 0:n], ACT.Copy, scale=HD ** -0.5 if is_q else 1.0).then_inc(prep_free, 1)
                else:
                    nc.scalar.activation(kT[b][0:HD, TP:KEYS], core.banks[0:HD, B_PREP, 0:PAST + TS], ACT.Copy).then_inc(prep_free, 1)
                    nc.scalar.activation(qT[b][0:HD, TP:T], core.banks[0:HD, B_PREP, PAST + TS:PAST + 2 * TS], ACT.Copy, scale=HD ** -0.5).then_inc(prep_free, 1)

            def exp(i, hb, s):
                e, m, n, par = (HR * i + hb) * ST + s, rows_of(s), nkeys[s], (hb * ST + s) % 2
                act.wait_ge(s_max, e + 1)
                act.wait_ge(pv, e + 1)
                act.wait_ge(chain, e + 1)
                nc.scalar.activation(pr[par][0:m, 0:n], core.banks[0:m, B_SCORES:B_SCORES + 2, :].rearrange("p a n -> p (a n)")[:, 0:n],
                                     ACT.Exp, bias=nmax[par][0:m, :], accum_out=rsum[par][0:m, :]).then_inc(s_exp, 1)
            stream.start_act(act)
            for g in range(PREP):
                prep_copy(0, 0, g)
            exp(0, 0, 0)

            def body(i, last):
                for n in range(stream.slots):
                    if steps[n]:
                        hb, s = steps[n]
                        hn, sn = after(hb, s)
                        if exists(hn, last):
                            exp(i, hn, sn)
                    stream.act(act, i, n, last)
                    if steps[n] and PREP_AT <= s < PREP_AT + PREP and exists(hb + 1, last):
                        prep_copy(i, hb + 1, s - PREP_AT)
            loop(act, ROUNDS, body)
            xbc.finish_act(act, out_bank)

        @block.vector
        def _(dve):
            dve.sem_inc(t_dve, 2)
            dve.sem_inc(o_made, 2)
            dve.sem_inc(chain, 2)

            def top(i, hb, s):
                e, m, n, par = (HR * i + hb) * ST + s, rows_of(s), nkeys[s], (hb * ST + s) % 2
                dve.wait_ge(s_full, e + 1)
                nc.vector.tensor_reduce(nmax[par][0:m, :], core.banks[0:m, B_SCORES:B_SCORES + 2, :].rearrange("p a n -> p (a n)")[:, 0:n],
                                        AX.X, ALU.max, negate=True).then_inc(s_max, 1)

            def copies(i, hb, s):
                h, m = HR * i + hb, rows_of(s)
                for g in range(len(groups[s])):
                    n = h * NG + first_group[s] + g
                    slot = (hb * NG + first_group[s] + g) % 2
                    dve.wait_ge(t_full, n + 1)
                    wide = len(groups[s][g]) * m
                    nc.vector.tensor_copy(prT[slot][:, 0:wide], core.banks[:, B_TURNED + slot, 0:wide]).then_inc(t_dve, 1)

            def scale(i, hb, s):
                e, b, m, par = (HR * i + hb) * ST + s, hb % 2, rows_of(s), (hb * ST + s) % 2
                if s == 0:
                    dve.wait_ge(stored[b], 32 * (HR // 2 * i + hb // 2 + 1))
                dve.wait_ge(s_exp, e + 3)
                nc.vector.reciprocal(rinv[par][0:m, :], rsum[par][0:m, :]).then_inc(chain, 1)
                dve.wait_ge(chain, e + 3)
                dve.wait_ge(pv, e + 3)
                nc.vector.tensor_scalar(o[b][0:m, s, :], out_bank[0:m, par * HD:(par + 1) * HD], rinv[par][0:m, :], None, ALU.mult).then_inc(o_made, 1)
            stream.start_dve(dve)
            top(0, 0, 0)

            def body(i, last):
                for n in range(stream.slots):
                    if steps[n]:
                        hb, s = steps[n]
                        copies(i, hb, s)
                        hn, sn = after(hb, s)
                        if exists(hn, last):
                            top(i, hn, sn)
                    stream.dve(dve, i, n, last)
                    if steps[n]:
                        scale(i, hb, s)
            loop(dve, ROUNDS, body)


def ssd_gates(core, hi, lo, w_in, following, gate_d, xbc_d, z_d, y_d, acum_d, state_in, d_skip, rms, ssm_prompt, ssm_running, keep):
    nc = core.nc
    NC = NT + 1
    dt_tm, acum_tm, w_tm, ea_tm, cdec = keep
    with ExitStack() as ctx:
        sb = lambda n, s, dt=F32: ctx.enter_context(nc.sbuf_tensor(f"ssd_{n}", s, dt))
        sem = core.semaphores(ctx, f"ssd")
        two = lambda n, s: [sb(f"{n}{b}", s) for b in range(2)]
        xbc = [sb(f"xbc{j}", [P, 4, P]) for j in range(3)]
        ab = [sb(f"ab{j}", [P, GH, P]) for j in range(3)]
        z = two("z", [P, NC, GW])
        st_in = two("st_in", [P, 2, N])
        Y = two("Y", [P, NC, GW])
        dsk = sb("dsk", [P, HS])
        h = [sb("h_prompt", [P, GW]), sb("h_running", [P, GW])]
        st_out = two("st_out", [P, 2, N])
        xb = two("xb", [P, GW + N])
        xdt, xw, xd = two("xdt", [P, GW]), two("xw", [P, GW]), two("xd", [P, GW])
        L = two("L", [P, GH, P])
        M = two("M", [P, GH, P])
        t1 = two("t1", [P, GW])
        junk = sb("junk", [P, GW])
        sems = lambda n: [sem(f"{n}{b}") for b in range(2)]
        loaded, y_stored = sems("loaded"), sems("y_stored")
        chunk_loaded = [sem(f"chunk_loaded{j}") for j in range(3)]
        gates = TanhFm(sb, sem, 2, gate_d)
        panel = lambda k: (False, lambda i: w_in[:, bass.ds((i * 2 + k) * PW + C_GA, PW)], gates, k)
        stream = gates.stream = Stream(core, "tiles", sb, sem, hi, lo, [panel(0), panel(1)], G // 2, (1,), following)
        CHUNKS = [(b, c) for b in range(2) for c in range(NC)]
        slot_of = {x: (n // 3) * 2 + n % 3 for n, x in enumerate(CHUNKS) if n % 3 < 2}
        assert len(slot_of) == stream.slots

        def after(b, c):
            return (b, c + 1) if c + 1 < NC else (b + 1, 0)
        par_loaded, st_stored, cleared = sem("par_loaded"), sem("st_stored"), sem("cleared")
        turned, xb_made, cb_made = sem("turned"), sem("xb_made"), sem("cb_made")
        L_in, L_made, M_made = sem("L_in"), sem("L_made"), sem("M_made")
        off_made, st_made, diag_made = sem("off_made"), sem("st_made"), sem("diag_made")
        x_scaled, gated, summed = sem("x_scaled"), sem("gated"), sem("summed")
        mean_made, rooted = sem("mean_made"), sem("rooted")
        in_turned, out_turned, st_copied, chain = sem("in_turned"), sem("out_turned"), sem("st_copied"), sem("vec_chain")
        block = ctx.enter_context(nc.Block())
        LOADS = 3
        STEPS = 2 + 5 * NC
        H_AT = lambda c: 4 + 5 * c
        Y_READ = lambda c: H_AT(c) + 2
        Y_SUM = lambda c: H_AT(c) + 3
        spread = lambda x, n: x.rearrange("p (h o) -> p h o", o=1).to_broadcast([n, GH, HD])
        heads = lambda x: x.rearrange("p (h d) -> p h d", h=GH)

        @block.sync
        def _(sp):
            sp.dma_start(dsk[:], d_skip.to_broadcast([P, HS])).then_inc(par_loaded, 16)

            def load(i, b):
                g = 2 * i + b
                cols = bass.ds(g * GW, GW)
                sp.dma_start(z[b][:, 0:NT, :], z_d[0:TP, cols].rearrange("(t p) d -> p t d", p=P)).then_inc(loaded[b], 16)
                sp.dma_start(z[b][0:TS, NT, :], z_d[TP:T, cols]).then_inc(loaded[b], 16)
                sp.dma_start(st_in[b][:], state_in[cols, :].rearrange("(m p) n -> p m n", p=P)).then_inc(loaded[b], 16)

            def load_chunk(i, b, c, first=False):
                g, n, j = 2 * i + b, rows_of(c), (b * NC + c) % 3
                cols = slice(c * P, c * P + n)
                if not first:
                    core.hold(sp, off_made, g * NC + c - 2)
                    core.hold(sp, L_in, g * NC + c - 2)
                sp.dma_start(xbc[j][:, 0:2, 0:n], xbc_d[bass.ds(g * GW, GW), cols].rearrange("(m p) t -> p m t", p=P)).then_inc(chunk_loaded[j], 16)
                sp.dma_start(xbc[j][:, 2, 0:n], xbc_d[bass.ds(g * N + DI, N), cols]).then_inc(chunk_loaded[j], 16)
                sp.dma_start(xbc[j][:, 3, 0:n], xbc_d[bass.ds(g * N + DI + G * N, N), cols]).then_inc(chunk_loaded[j], 16)
                sp.dma_start(ab[j][:, :, 0:n], acum_d[:, bass.ds(g * GH, GH), cols].to_broadcast([P, GH, n])).then_inc(chunk_loaded[j], 16)

            def store(i, b):
                g = 2 * i + b
                cols = bass.ds(g * GW, GW)
                core.hold(sp, st_copied, 2 * g + 2)
                sp.dma_start(ssm_prompt[cols, :].rearrange("(m p) n -> p m n", p=P), st_out[0][:]).then_inc(st_stored, 16)
                sp.dma_start(ssm_running[cols, :].rearrange("(m p) n -> p m n", p=P), st_out[1][:]).then_inc(st_stored, 16)
                core.hold(sp, gated, (g + 1) * NC + 2)
                core.hold(sp, summed, (g + 1) * NC + 1)
                sp.dma_start(y_d[0:TP, cols].rearrange("(t p) d -> p t d", p=P), Y[b][:, 0:NT, :]).then_inc(y_stored[b], 16)
                sp.dma_start(y_d[TP:T, cols], Y[b][0:TS, NT, :]).then_inc(y_stored[b], 16)
            for b in range(2):
                sp.sem_inc(y_stored[b], 32)
            sp.sem_inc(st_stored, 32)
            load_chunk(0, 0, 0, True)
            load_chunk(0, 0, 1, True)
            load(0, 0)
            load_chunk(0, 0, 2, True)
            stream.start_sp(sp)
            load(0, 1)

            def body(i, last):
                for b, c in CHUNKS:
                    ahead = after(*after(*after(b, c)))
                    if not (last and ahead[0] == 2):
                        load_chunk(i, *ahead)
                    if (b, c) in slot_of:
                        stream.sp(sp, i, slot_of[b, c], last)
                    if c == NC - 1:
                        store(i, b)
                        if not last:
                            load(i + 1, b)
            loop(sp, G // 2, body)
            gates.finish(sp)
            for b in range(2):
                sp.wait_ge(y_stored[b], 32 * (G // 2 + 1))
            sp.wait_ge(st_stored, 32 * (G + 1))

        @block.tensor
        def _(pe):
            pe.sem_inc(st_made, 2)
            pe.sem_inc(diag_made, 2)

            def turn(i, b, c):
                e, n, par, x = (2 * i + b) * NC + c, rows_of(c), (b * NC + c) % 2, xbc[(b * NC + c) % 3]
                pe.wait_ge(chunk_loaded[(b * NC + c) % 3], 64 * (2 * NC // 3 * i + (b * NC + c) // 3 + 1))
                pe.wait_ge(xb_made, e + 2)
                for m in range(3):
                    ins = nc.tensor.transpose(core.banks[0:n, 0, m * P:(m + 1) * P], x[:, m, 0:n], core.ident[:])
                ins.then_inc(turned, 1)
                pe.wait_ge(M_made, e + 1)
                nc.tensor.matmul(core.banks[0:n, 2 + par, 0:n], x[:, 2, 0:n], x[:, 3, 0:n], start=True, stop=True).then_inc(cb_made, 1)

            turn(0, 0, 0)

            def body(i, last):
                for b in range(2):
                    g = 2 * i + b
                    pe.wait_ge(loaded[b], 16 * LOADS * (i + 1))
                    pe.wait_ge(chain, g * STEPS + 1)
                    for m in range(2):
                        ins = nc.tensor.transpose(core.banks[:, 4, m * P:(m + 1) * P], st_in[b][:, m, :], core.ident[:])
                    ins.then_inc(in_turned, 1)
                    for c in range(NC):
                        e, n, par = g * NC + c, rows_of(c), (b * NC + c) % 2
                        if not (last and (b, c) == CHUNKS[-1]):
                            turn(i, *after(b, c))
                        before = 2 if c in (0, NT) else H_AT(c - 1)
                        pe.wait_ge(chain, g * STEPS + max(before, Y_READ(c - 2) if c >= 2 else 0))
                        nc.tensor.matmul(core.banks[0:n, 4 + par, 0:GW], xbc[(b * NC + c) % 3][:, 3, 0:n], h[c == NT][:], start=True, stop=True).then_inc(off_made, 1)
                        pe.wait_ge(x_scaled, 3 * e + 9)
                        nc.tensor.matmul(core.banks[:, 4 + par, GW:2 * GW], xb[par][0:n, GW:GW + N], xw[par][0:n, :], start=True, stop=True).then_inc(st_made, 1)
                        if (b, c) in slot_of:
                            stream.pe(pe, i, slot_of[b, c])
                        core.hold(pe, M_made, e + 3)
                        for k in range(GH):
                            ins = nc.tensor.matmul(core.banks[0:n, 6 + par, k * HD:(k + 1) * HD], M[par][0:n, k, 0:n],
                                                   xdt[par][0:n, k * HD:(k + 1) * HD], start=True, stop=True)
                        ins.then_inc(diag_made, 1)
                    pe.wait_ge(chain, g * STEPS + Y_READ(NC - 1))
                    for s in range(2):
                        for m in range(2):
                            ins = nc.tensor.transpose(core.banks[:, 6 + s, m * P:(m + 1) * P], h[s][:, m * P:(m + 1) * P], core.ident[:])
                        ins.then_inc(out_turned, 1)
                    pe.wait_ge(st_copied, 2 * g + 2)
            loop(pe, G // 2, body)

        @block.scalar
        def _(act):
            act.sem_inc(xb_made, 2)
            act.sem_inc(summed, 1)
            act.wait_ge(cleared, 1)

            def copy_x(i, b, c):
                e, n, par = (2 * i + b) * NC + c, rows_of(c), (b * NC + c) % 2
                act.wait_ge(turned, e + 1)
                act.wait_ge(st_made, e + 1)
                act.wait_ge(x_scaled, 3 * e + 3)
                nc.scalar.activation(xb[par][0:n, :], core.banks[0:n, 0, 0:GW + N], ACT.Copy).then_inc(xb_made, 1)

            def square(i, b, c):
                e, n = (2 * i + b) * NC + c, rows_of(c)
                act.wait_ge(gated, e + 3)
                act.wait_ge(summed, e + 1)
                nc.scalar.activation(junk[0:n, :], Y[b][0:n, c, :], ACT.Square, accum_out=rms[0:n, c, bass.ds(2 * i + b, 1)]).then_inc(summed, 1)

            copy_x(0, 0, 0)
            stream.start_act(act)

            def body(i, last):
                for b in range(2):
                    g = 2 * i + b
                    for c in range(NC):
                        e, n, par = g * NC + c, rows_of(c), (b * NC + c) % 2
                        if not (last and (b, c) == CHUNKS[-1]):
                            copy_x(i, *after(b, c))
                        act.wait_ge(L_in, e + 1)
                        nc.scalar.activation(L[par][0:n, :, 0:n], L[par][0:n, :, 0:n], ACT.Exp).then_inc(L_made, 1)
                        if c:
                            square(i, b, c - 1)
                        if (b, c) in slot_of:
                            stream.act(act, i, slot_of[b, c], last)
                    square(i, b, NC - 1)
                    act.wait_ge(st_stored, 32 * (g + 1))
                    for s in range(2):
                        act.wait_ge(out_turned, 2 * g + s + 2)
                        nc.scalar.activation(st_out[s][:], core.banks[:, 6 + s, 0:2 * P].rearrange("p (m n) -> p m n", m=2), ACT.Copy).then_inc(st_copied, 1)
            loop(act, G // 2, body)
            act.wait_ge(mean_made, 1)
            nc.scalar.activation(rms[:], rms[:], ACT.Sqrt).then_inc(rooted, 1)

        @block.gpsimd
        def _(pool):
            pool.sem_inc(x_scaled, 6)
            pool.sem_inc(gated, 2)
            core.hold(pool, par_loaded, 16)
            core.hold(pool, cleared, 1)

            def gate(i, b, c):
                e, n, par = (2 * i + b) * NC + c, rows_of(c), (b * NC + c) % 2
                core.hold(pool, chain, (2 * i + b) * STEPS + Y_SUM(c))
                nc.gpsimd.tensor_tensor(Y[b][0:n, c, :], t1[par][0:n, :], z[b][0:n, c, :], ALU.mult).then_inc(gated, 1)

            def scale_x(i, b, c):
                g = 2 * i + b
                gh = bass.ds(g * GH, GH)
                e, n, par = g * NC + c, rows_of(c), (b * NC + c) % 2
                core.hold(pool, xb_made, e + 3)
                x = heads(xb[par][0:n, 0:GW])
                core.hold(pool, st_made, e + 1)
                nc.gpsimd.tensor_tensor(heads(xw[par][0:n, :]), x, spread(w_tm[0:n, c, gh], n), ALU.mult).then_inc(x_scaled, 1)
                core.hold(pool, diag_made, e + 1)
                nc.gpsimd.tensor_tensor(heads(xdt[par][0:n, :]), x, spread(dt_tm[0:n, c, gh], n), ALU.mult).then_inc(x_scaled, 1)
                if c >= 2:
                    core.hold(pool, chain, g * STEPS + Y_SUM(c - 2))
                elif c == 1:
                    core.hold(pool, chain, g * STEPS + 1)
                elif b:
                    core.hold(pool, chain, (g - 1) * STEPS + Y_SUM(NC - 2))
                nc.gpsimd.tensor_tensor(heads(xd[par][0:n, :]), x, spread(dsk[0:n, gh], n), ALU.mult).then_inc(x_scaled, 1)
            scale_x(0, 0, 0)

            def body(i, last):
                for b in range(2):
                    core.hold(pool, loaded[b], 16 * LOADS * (i + 1))
                    core.hold(pool, y_stored[b], 32 * (i + 1))
                    for c in range(NC):
                        if not (last and (b, c) == CHUNKS[-1]):
                            scale_x(i, *after(b, c))
                        if c:
                            gate(i, b, c - 1)
                    gate(i, b, NC - 1)
            loop(pool, G // 2, body)

        @block.vector
        def _(dve):
            nc.vector.memset(rms[:], 1.0).then_inc(cleared, 1)
            dve.sem_inc(M_made, 2)
            dve.sem_inc(out_turned, 1)
            stream.start_dve(dve)

            def body(i, last):
                for b in range(2):
                    g = 2 * i + b
                    gh = bass.ds(g * GH, GH)
                    step = Chain(dve, chain)
                    step.enter(g, STEPS)

                    def y_sum(c):
                        e, n, par = g * NC + c, rows_of(c), (b * NC + c) % 2
                        dve.wait_ge(off_made, e + 1)
                        dve.wait_ge(gated, e + 1)
                        y = t1[par][0:n, :]
                        step(nc.vector.tensor_tensor(heads(y), heads(core.banks[0:n, 4 + par, 0:GW]), spread(ea_tm[0:n, c, gh], n), ALU.mult))
                        dve.wait_ge(diag_made, e + 3)
                        step(nc.vector.tensor_tensor(y, core.banks[0:n, 6 + par, 0:GW], y, ALU.add))
                        assert step.n == Y_READ(c)
                        dve.wait_ge(x_scaled, 3 * e + 9)
                        step(nc.vector.tensor_tensor(y, y, xd[par][0:n, :], ALU.add))

                    dve.wait_ge(loaded[b], 16 * LOADS * (i + 1))
                    dve.wait_ge(out_turned, 2 * g + 1)
                    step(nc.vector.memset(h[0][:], 0.0))
                    dve.wait_ge(in_turned, g + 1)
                    step(nc.vector.tensor_copy(h[1][:], core.banks[:, 4, 0:GW]))
                    for c in range(NC):
                        e, n, par = g * NC + c, rows_of(c), (b * NC + c) % 2
                        dve.wait_ge(chunk_loaded[(b * NC + c) % 3], 64 * (2 * NC // 3 * i + (b * NC + c) // 3 + 1))
                        dve.wait_ge(M_made, e + 1)
                        for k in range(GH):
                            ins = nc.vector.scalar_tensor_tensor(out=L[par][0:n, k, 0:n], in0=ab[(b * NC + c) % 3][0:n, k, 0:n],
                                                                 scalar=acum_tm[0:n, c, bass.ds(g * GH + k, 1)],
                                                                 in1=core.maskT[0:n, 0:n], op0=ALU.subtract, op1=ALU.add)
                        ins.then_inc(L_in, 1)
                        if c:
                            y_sum(c - 1)
                        hc = heads(h[c == NT][:])
                        dve.wait_ge(off_made, e + 1)
                        step(nc.vector.tensor_tensor(hc, hc, spread(cdec[:, gh, c], P), ALU.mult))
                        dve.wait_ge(st_made, e + 3)
                        step(nc.vector.tensor_tensor(hc, heads(core.banks[:, 4 + par, GW:2 * GW]), hc, ALU.add))
                        assert step.n == H_AT(c)
                        dve.wait_ge(L_made, e + 1)
                        dve.wait_ge(cb_made, e + 1)
                        dve.wait_ge(diag_made, e + 1)
                        nc.vector.tensor_tensor(M[par][0:n, :, 0:n], L[par][0:n, :, 0:n],
                                                core.banks[0:n, 2 + par, 0:n].rearrange("p (o l) -> p o l", o=1).to_broadcast([n, GH, n]),
                                                ALU.mult).then_inc(M_made, 1)
                        if (b, c) in slot_of:
                            stream.dve(dve, i, slot_of[b, c], last)
                    y_sum(NC - 1)
                    step.leave()
            loop(dve, G // 2, body)
            dve.wait_ge(summed, G * NC + 1)
            nc.vector.tensor_scalar(rms[:], rms[:], 1.0 / GW, 4 * EPS, ALU.mult, ALU.add).then_inc(mean_made, 1)
            dve.wait_ge(rooted, 1)
            nc.vector.reciprocal(rms[:], rms[:])


def hybrid_layer(nc, I, O):
    scratch = lambda n, s: nc.dram_tensor(f"scratch_{n}", s, F32, kind="Internal").ap()
    q_d, att_d = scratch("q", [T, D]), scratch("att", [T, D])
    z_d, y_d = scratch("z", [T, DI]), scratch("y", [T, DI])
    xbc_d = scratch("xbc", [CD, T])
    gate_d = scratch("gates", [2 * D, T])
    ga_d, gs_d = gate_d[0:D, :], gate_d[D:2 * D, :]
    x2_d = scratch("x2", [T, D])
    aug_q, aug_k = scratch("aug_q", [H, 2, KEYS]), scratch("aug_k", [H, 2, KEYS])
    acum_d = scratch("acum", [1, HS, T])

    x_p, x_s = I["x_prompt"][0], I["x_sample"][0]
    w_in = I["w_in"][0]
    flat = lambda a: a[0, 0].rearrange("t h d -> t (h d)")
    row = lambda a: a
    columns = lambda w, c0, rows, width: (lambda p: w[rows, bass.ds(p * width + c0, width)])
    every = slice(0, D)
    with ExitStack() as ctx:
        core = Core(nc, ctx)
        constants(core)
        rms = ctx.enter_context(nc.sbuf_tensor("rms", [P, NT + 1, G], F32))
        with ExitStack() as keep_ctx:
            keep = [keep_ctx.enter_context(nc.sbuf_tensor(f"keep_{n}", s, F32)) for n, s in
                    (("dt", [P, NT + 1, HS]), ("acum", [P, NT + 1, HS]), ("w", [P, NT + 1, HS]), ("ea", [P, NT + 1, HS]), ("cdec", [P, HS, NT + 1]))]
            with ExitStack() as x_ctx:
                hi = x_ctx.enter_context(nc.sbuf_tensor("xn_hi", [P, KB, TW], F32R))
                lo = x_ctx.enter_context(nc.sbuf_tensor("xn_lo", [P, KB, TW], F32R))
                norm_split(core, "norm1", (x_p, x_s), hi, lo, I["norm1_w"], w_in[:, C_Q:C_Q + PW])
                project_qkv(core, hi, lo, w_in, (I["q_norm_w"], I["k_norm_w"]), (q_d[0:TP, :], q_d[TP:T, :]),
                            (flat(O["k_prompt"]), flat(O["k_sample"])), (flat(O["v_prompt"]), flat(O["v_sample"])),
                            I["b_f"][0], I["dt_bias"][0], I["A_log"][0], I["cache_logf"][0, 0],
                            (O["logf_prompt"][0, 0], O["logf_sample"][0, 0]), aug_q, aug_k, acum_d[0], keep)
                attention_z_xbc(core, hi, lo, w_in, z_d, xbc_d,
                                dict(params=(I["conv_w"][0], I["conv_b"][0], I["state_conv"][0, 0]),
                                     tails=(O["conv_prompt"][0, 0], O["conv_sample"][0, 0])),
                                q_d, flat(O["k_prompt"]), flat(O["k_sample"]), flat(O["v_prompt"]), flat(O["v_sample"]),
                                flat(I["cache_k"]), flat(I["cache_v"]), aug_q, aug_k, att_d)
                state = lambda a: a[0, 0].rearrange("h p n -> (h p) n")
                ssd_gates(core, hi, lo, w_in, I["w_pb"][0][0:D, 0:PW], gate_d, xbc_d, z_d, y_d, acum_d, state(I["state_ssm"]), I["D_skip"], rms,
                    state(O["ssm_prompt"]), state(O["ssm_sample"]), keep)
        merged = ctx.enter_context(nc.sbuf_tensor("merged", [P, KB, T], F32))
        branches(core, y_d, rms, I["ssm_norm_w"], att_d, (ga_d, gs_d), I["w_pa"][0], I["w_pb"][0], merged, I["w_out"][0][:, 0:PW])
        hi = ctx.enter_context(nc.sbuf_tensor("h_hi", [P, KB, TW], F32R))
        lo = ctx.enter_context(nc.sbuf_tensor("h_lo", [P, KB, TW], F32R))
        out_norm(core, merged, I["w_out"][0], (x_p, x_s), (x2_d[0:TP, :], x2_d[TP:T, :]), I["norm2_w"], hi, lo,
                 I["w_up"][0][:, 0:PW])
        mlp(core, hi, lo, merged, I["w_up"][0], I["w_down"][0], x2_d[0:TP, :], x2_d[TP:T, :], O["y_prompt"][0], O["y_sample"][0])


_INS = ["x_prompt", "x_sample", "cache_k", "cache_v", "cache_logf", "state_conv", "state_ssm", "norm1_w", "w_in", "b_f",
        "q_norm_w", "k_norm_w", "conv_w", "conv_b", "dt_bias", "A_log", "D_skip", "ssm_norm_w", "w_pa", "w_pb", "w_out",
        "norm2_w", "w_up", "w_down"]
_OUTS = [("y_prompt", (1, TP, D)), ("y_sample", (1, TS, D)),
         ("k_prompt", (1, 1, TP, H, HD)), ("v_prompt", (1, 1, TP, H, HD)), ("logf_prompt", (1, 1, TP, H)),
         ("conv_prompt", (1, 1, CW - 1, CD)), ("ssm_prompt", (1, 1, HS, HD, N)),
         ("k_sample", (1, 1, TS, H, HD)), ("v_sample", (1, 1, TS, H, HD)), ("logf_sample", (1, 1, TS, H)),
         ("conv_sample", (1, 1, CW - 1, CD)), ("ssm_sample", (1, 1, HS, HD, N))]


def kernel(**inputs):
    import concourse.bacc as bacc
    from concourse.bass_utils import run_bass_kernel_spmd

    nc = bacc.Bacc("TRN2", target_bir_lowering=False, num_devices=1)
    arrays = {f"in_{n}": np.ascontiguousarray(inputs[n]) for n in _INS}
    I = {n: nc.dram_tensor(f"in_{n}", arrays[f"in_{n}"].shape, F32, kind="ExternalInput").ap() for n in _INS}
    O = {n: nc.dram_tensor(f"out_{n}", s, F32, kind="ExternalOutput").ap() for n, s in _OUTS}
    hybrid_layer(nc, I, O)
    r = run_bass_kernel_spmd(nc, [arrays], core_ids=[0])
    return tuple(r.results[0][f"out_{n}"] for n, _ in _OUTS)
```
